# Optimizing a Trainium2 kernel written in Bass

```python
import math
import jax, jax.numpy as jnp
from jax import lax
import numpy as np

D_MODEL = 2048
BATCH = 1
SEQ = 128
DEPTH = 2
DEC_BATCH = 1
DEC_SEQ = 512
PAST_LEN = 128

GRID_W = 64
HEAD_DIM = 128
ATT_HEADS = 8
ATT_KV_HEADS = 2
ATT_WIDTH = ATT_HEADS * HEAD_DIM
KV_WIDTH = ATT_KV_HEADS * HEAD_DIM
CONV_WIDTH = D_MODEL // 4
GLA_HEADS = 4
GLA_DK = 64
GLA_DV = 128
GLA_KW = GLA_HEADS * GLA_DK
GLA_VW = GLA_HEADS * GLA_DV
GLA_RANK = 16
GLA_TAU = 16.0
GLA_CHUNK = 64
Q_BLOCK = 128
ROPE_THETA = 10000.0
EPS = 1e-6
MIX_WIDTH = ATT_WIDTH + CONV_WIDTH + GLA_VW
PROJ_SIZES = (ATT_WIDTH, KV_WIDTH, KV_WIDTH, ATT_WIDTH,
              CONV_WIDTH, CONV_WIDTH, CONV_WIDTH, CONV_WIDTH,
              GLA_KW, GLA_KW, GLA_VW, GLA_VW, 2 * GLA_RANK)
SPLIT_POINTS = tuple(int(s) for s in np.cumsum(PROJ_SIZES)[:-1])
IN_WIDTH = sum(PROJ_SIZES)

kernel_name = "hybrid_diffusion_prefix_trunk_step"

def rmsnorm(x, w):
    xf = x.astype(jnp.float32)
    y = xf * lax.rsqrt(jnp.mean(xf * xf, axis=-1, keepdims=True) + EPS)
    return (y * w.astype(jnp.float32)).astype(x.dtype)

def rope_2d(x):
    t = x.shape[1]
    pos = jnp.arange(t)
    row = (pos // GRID_W).astype(jnp.float32)
    col = (pos % GRID_W).astype(jnp.float32)
    n_freq = HEAD_DIM // 4
    inv = ROPE_THETA ** (-jnp.arange(n_freq, dtype=jnp.float32) / n_freq)

    def rot(xh, p):
        ang = p[:, None] * inv[None, :]
        cos = jnp.cos(ang)[None, :, None, :]
        sin = jnp.sin(ang)[None, :, None, :]
        x1, x2 = jnp.split(xh, 2, axis=-1)
        return jnp.concatenate([x1 * cos - x2 * sin, x1 * sin + x2 * cos], axis=-1)

    xf = x.astype(jnp.float32)
    half = HEAD_DIM // 2
    return jnp.concatenate([rot(xf[..., :half], row), rot(xf[..., half:], col)], axis=-1).astype(x.dtype)

def block_attention(q, k, v):
    b, tq, h, hd = q.shape
    kvh = k.shape[2]
    g = h // kvh
    nb = tq // Q_BLOCK
    qb = q.reshape(b, nb, Q_BLOCK, kvh, g, hd).transpose(1, 0, 2, 3, 4, 5)
    kf = k.astype(jnp.float32)
    vf = v.astype(jnp.float32)
    scale = hd ** -0.5

    def one(qblk):
        s = jnp.einsum('bqkgd,bskd->bkgqs', qblk.astype(jnp.float32), kf) * scale
        p = jax.nn.softmax(s, axis=-1)
        return jnp.einsum('bkgqs,bskd->bqkgd', p, vf).astype(q.dtype)

    o = lax.map(one, qb)
    return o.transpose(1, 0, 2, 3, 4, 5).reshape(b, tq, h * hd)

def conv3_centred(u, w):
    up = jnp.pad(u, ((0, 0), (1, 1), (0, 0)))
    return up[:, :-2] * w[0] + up[:, 1:-1] * w[1] + up[:, 2:] * w[2]

def gla_scan(q, k, v, logf, s0):
    b, t, h, dk = q.shape
    dv = v.shape[-1]
    n = t // GLA_CHUNK

    def chunks(a):
        return a.reshape(b, n, GLA_CHUNK, h, a.shape[-1]).transpose(1, 0, 3, 2, 4).astype(jnp.float32)

    qc, kc, vc, gc = chunks(q), chunks(k), chunks(v), chunks(logf)
    causal = jnp.tril(jnp.ones((GLA_CHUNK, GLA_CHUNK), dtype=bool))[None, None, :, :, None]

    def step(S, inp):
        qi, ki, vi, gi = inp
        bc = jnp.cumsum(gi, axis=2)
        inter = jnp.einsum('bhld,bhde->bhle', qi * jnp.exp(bc), S)
        diff = bc[:, :, :, None, :] - bc[:, :, None, :, :]
        dec = jnp.exp(jnp.where(causal, diff, -jnp.inf))
        att = jnp.einsum('bhtd,bhtsd,bhsd->bhts', qi, dec, ki)
        intra = jnp.einsum('bhts,bhse->bhte', att, vi)
        blast = bc[:, :, -1:, :]
        S = jnp.exp(blast[:, :, 0, :])[..., None] * S + jnp.einsum('bhsd,bhse->bhde', ki * jnp.exp(blast - bc), vi)
        return S, inter + intra

    S, o = lax.scan(step, s0.astype(jnp.float32), (qc, kc, vc, gc))
    o = o.transpose(1, 0, 3, 2, 4).reshape(b, t, h, dv)
    return o, S

def gla_bidir(q, k, v, logf_f, logf_b, s0_f, s0_b):
    flip = lambda a: jnp.flip(a, axis=1)
    of, sf = gla_scan(q, k, v, logf_f, s0_f)
    ob, sb = gla_scan(flip(q), flip(k), flip(v), flip(logf_b), s0_b)
    return of + flip(ob), sf, sb

def mixer_layer(x, mod, norm_w, w_in, q_norm_w, k_norm_w, conv_w, a_up, a_bias, gla_norm_w, w_out, ctx):
    b, t, _ = x.shape
    shift, scale, gate = jnp.split(mod, 3, axis=-1)
    xn = rmsnorm(x, norm_w) * (1.0 + scale[:, None, :]) + shift[:, None, :]
    proj = xn @ w_in
    aq, ak, av, ag, ch, cb, cc, cg, gq, gk, gv, gg, glr = jnp.split(proj, SPLIT_POINTS, axis=-1)

    q = rmsnorm(aq.reshape(b, t, ATT_HEADS, HEAD_DIM), q_norm_w)
    k = rmsnorm(ak.reshape(b, t, ATT_KV_HEADS, HEAD_DIM), k_norm_w)
    v = av.reshape(b, t, ATT_KV_HEADS, HEAD_DIM)
    if ctx is None:
        k_all, v_all = k, v
    else:
        k_ctx, v_ctx, s0_f, s0_b = ctx
        q = rope_2d(q)
        k = rope_2d(k)
        k_all = jnp.concatenate([k, k_ctx.astype(k.dtype)], axis=1)
        v_all = jnp.concatenate([v, v_ctx.astype(v.dtype)], axis=1)
    out_a = block_attention(q, k_all, v_all) * jax.nn.silu(ag)

    out_b = cb * conv3_centred(cc * ch, conv_w) * jax.nn.silu(cg)

    lr = glr.reshape(b, t, 2, GLA_RANK)
    logits = jnp.einsum('btzr,zrk->btzk', lr, a_up) + a_bias
    logf = jax.nn.log_sigmoid(logits.astype(jnp.float32)) / GLA_TAU
    logf_f = logf[:, :, 0].reshape(b, t, GLA_HEADS, GLA_DK)
    logf_b = logf[:, :, 1].reshape(b, t, GLA_HEADS, GLA_DK)
    gq_h = gq.reshape(b, t, GLA_HEADS, GLA_DK) * (GLA_DK ** -0.5)
    gk_h = gk.reshape(b, t, GLA_HEADS, GLA_DK)
    gv_h = gv.reshape(b, t, GLA_HEADS, GLA_DV)
    if ctx is None:
        s0_f = jnp.zeros((b, GLA_HEADS, GLA_DK, GLA_DV), jnp.float32)
        s0_b = s0_f
    o_c, s_f, s_b = gla_bidir(gq_h, gk_h, gv_h, logf_f, logf_b, s0_f, s0_b)
    out_c = rmsnorm(o_c, gla_norm_w).astype(x.dtype).reshape(b, t, GLA_VW) * jax.nn.silu(gg)

    mix = jnp.concatenate([out_a, out_b, out_c], axis=-1) @ w_out
    x = x + gate[:, None, :] * mix
    return x, k, v, s_f, s_b

def setup_inputs(seed: int = 0) -> dict:
    key = jax.random.key(seed)
    ks = jax.random.split(key, 20)
    f32 = jnp.float32
    nrm = lambda k, s: jax.random.normal(k, s, f32)
    return {
        "x_prompt": nrm(ks[0], (BATCH, SEQ, D_MODEL)),
        "x_sample": nrm(ks[1], (DEC_BATCH, DEC_SEQ, D_MODEL)),
        "cache_k": nrm(ks[2], (DEC_BATCH, DEPTH, PAST_LEN, ATT_KV_HEADS, HEAD_DIM)),
        "cache_v": nrm(ks[3], (DEC_BATCH, DEPTH, PAST_LEN, ATT_KV_HEADS, HEAD_DIM)),
        "state_gla": 0.5 * nrm(ks[4], (DEC_BATCH, DEPTH, 2, GLA_HEADS, GLA_DK, GLA_DV)),
        "c": nrm(ks[5], (DEC_BATCH, D_MODEL)),
        "c_ctx": nrm(ks[6], (D_MODEL,)),
        "w_mod": 0.5 * nrm(ks[7], (DEPTH, D_MODEL, 3 * D_MODEL)) * D_MODEL ** -0.5,
        "b_mod": 0.01 * nrm(ks[8], (DEPTH, 3 * D_MODEL)),
        "norm_w": 1.0 + 0.02 * nrm(ks[9], (DEPTH, D_MODEL)),
        "w_in": nrm(ks[10], (DEPTH, D_MODEL, IN_WIDTH)) * D_MODEL ** -0.5,
        "q_norm_w": 1.0 + 0.02 * nrm(ks[11], (DEPTH, HEAD_DIM)),
        "k_norm_w": 1.0 + 0.02 * nrm(ks[12], (DEPTH, HEAD_DIM)),
        "conv_w": nrm(ks[13], (DEPTH, 3, CONV_WIDTH)) * 3 ** -0.5,
        "gla_a_up": nrm(ks[14], (DEPTH, 2, GLA_RANK, GLA_KW)) * GLA_RANK ** -0.5,
        "gla_a_bias": 0.1 * nrm(ks[15], (DEPTH, 2, GLA_KW)),
        "gla_norm_w": 1.0 + 0.02 * nrm(ks[16], (DEPTH, GLA_DV)),
        "w_out": nrm(ks[17], (DEPTH, MIX_WIDTH, D_MODEL)) * MIX_WIDTH ** -0.5,
        "final_norm_w": 1.0 + 0.02 * nrm(ks[18], (D_MODEL,)),
    }

def reference(x_prompt, x_sample, cache_k, cache_v, state_gla, c, c_ctx, w_mod, b_mod, norm_w, w_in,
              q_norm_w, k_norm_w, conv_w, gla_a_up, gla_a_bias, gla_norm_w, w_out, final_norm_w):
    h = x_prompt
    ks_out, vs_out, st_out = [], [], []
    for l in range(DEPTH):
        mod = jax.nn.silu(c_ctx)[None, :] @ w_mod[l] + b_mod[l]
        h, k_l, v_l, sf, sb = mixer_layer(h, mod, norm_w[l], w_in[l], q_norm_w[l], k_norm_w[l], conv_w[l],
                                          gla_a_up[l], gla_a_bias[l], gla_norm_w[l], w_out[l], None)
        ks_out.append(k_l)
        vs_out.append(v_l)
        st_out.append(jnp.stack([sf, sb], axis=1))
    y_prompt = rmsnorm(h, final_norm_w)
    new_k = jnp.stack(ks_out, axis=1)
    new_v = jnp.stack(vs_out, axis=1)
    new_state_gla = jnp.stack(st_out, axis=1).astype(x_prompt.dtype)

    z = x_sample
    for l in range(DEPTH):
        mod = jax.nn.silu(c) @ w_mod[l] + b_mod[l]
        ctx = (cache_k[:, l], cache_v[:, l], state_gla[:, l, 0], state_gla[:, l, 1])
        z, _, _, _, _ = mixer_layer(z, mod, norm_w[l], w_in[l], q_norm_w[l], k_norm_w[l], conv_w[l],
                                    gla_a_up[l], gla_a_bias[l], gla_norm_w[l], w_out[l], ctx)
    y_sample = rmsnorm(z, final_norm_w)
    return (y_prompt, y_sample, new_k, new_v, new_state_gla)


_drawn_inputs = setup_inputs


def setup_inputs(seed=0):
    import zlib

    import numpy as np

    out = dict(_drawn_inputs(seed))
    spreads = {}
    factors = {'cache_k': 8.0,
     'cache_v': 8.0,
     'state_gla': 8.0,
     'q_norm_w': 8.0,
     'k_norm_w': 8.516,
     'gla_norm_w': 8.0,
     'final_norm_w': 8.019}
    for name, (base, spread) in spreads.items():
        noise = np.random.default_rng([zlib.crc32(name.encode()), seed]).standard_normal(out[name].shape)
        drawn = base * np.exp(spread * noise) if base else spread * noise
        out[name] = __import__('jax').numpy.asarray(drawn.astype(out[name].dtype))
    for name, factor in factors.items():
        out[name] = (out[name] * factor).astype(out[name].dtype)
    return out
```

```python
from contextlib import ExitStack

import numpy as np

import concourse.bass as bass
from concourse import mybir

F32 = mybir.dt.float32
F32R = mybir.dt.float32r
ALU = mybir.AluOpType
ACT = mybir.ActivationFunctionType
AX = mybir.AxisListType

P = 128
SEQ, DEC, PAST = 128, 512, 128
TOK = DEC + SEQ
TT = TOK // P
DEPTH = 2
D = 2048
KT = D // P
HD = 128
HEADS, KVH = 8, 2
GROUP = HEADS // KVH
KEYS = DEC + PAST
CH = 64
NCH = TOK // CH
DEC_CH = DEC // CH
GLA_H, DK, DV, RANK = 4, 64, 128, 16
PAIRS = GLA_H // 2
TAU = 16.0
GRID_W = 64
EPS = 1e-6
ATT_W, KV_W, CONV_W, GKW, GVW = HEADS * HD, KVH * HD, D // 4, GLA_H * DK, GLA_H * DV
CONV_T = CONV_W // P

SIZES = [ATT_W, KV_W, KV_W, ATT_W, CONV_W, CONV_W, CONV_W, CONV_W, GKW, GKW, GVW, GVW]
T_AQ, T_AK, T_AV, T_AG, T_CH, T_CB, T_CC, T_CG, T_GQ, T_GK, T_GV, T_GG, T_LR = [
    int(x) // P for x in np.cumsum([0] + SIZES)]
PLAIN = [(T_AQ, (T_AG - T_AQ) // 2, False), (T_CH, (T_CG - T_CH) // 2, False), (T_GQ, (T_GG - T_GQ) // 2, False)]
GATES = [(T_AG, (T_CH - T_AG) // 2, True), (T_CG, (T_GQ - T_CG) // 2, True), (T_GG, (T_LR - T_GG) // 2, True)]
RUNS = PLAIN + GATES
IN_PAIRS = sum(n for _, n, _ in RUNS)
OUT_PAIRS = KT // 2
MOD_T = 3 * KT
MOD_N = 512
MOD_CHUNKS = 3 * D // MOD_N
LR_W = 2 * RANK

R_BMOD, R_NORM, R_Q, R_K = 0, MOD_T, MOD_T + KT, MOD_T + KT + 1
R_CONV = R_K + 1
R_ABIAS = R_CONV + 3 * CONV_T
R_GNORM = R_ABIAS + 2 * PAIRS
ROWS = R_GNORM + 1

HALF = TOK // 2
AT = 512 - HALF
CLAMP = 40.0 * TAU
STATES = DEC_CH + 1 + SEQ // CH + 1


def state_at(z, chunk):
    if chunk < DEC_CH:
        return chunk if z == 0 else DEC_CH - 1 - chunk
    n = chunk - DEC_CH
    return DEC_CH + 1 + (n if z == 0 else SEQ // CH - 1 - n)


STEPS = [(n, DEC_CH - 1 - n) for n in range(DEC_CH - 1)] + [(DEC_CH + n, NCH - 1 - n) for n in range(SEQ // CH)]

NAMES = """rows_in x_in consts_in rows_turned vecs_ready head_ready embed_turned x_taken x_squared
x_saved wmod_in0 wmod_in1 wmod_in2 wmod_in3 wmod_used0 wmod_used1 wmod_used2 wmod_used3
mod_row mod_turned mod_taken raw_in0 raw_in1 high0 high1 split0 split1 tile_done0 tile_done1
taken0 taken1 stored0 stored1 phase_over x_split mix_high mix_split stat_summed stat_var stat_ln stat_exp stat_rs
mod_added mod_ready scaled0 scaled1 shifted0 shifted1 x_high0 x_high1 mraw_in0 mraw_in1 mod_step0 mod_step1
mod_half mod_acc mod_summed lr_in lr_high lr_split lr_done lr_taken lr_stored old_in0 old_in1 x_new0 x_new1
x_sq x_acc k_in v_in ck_in cv_in q_in ag_in k_sq k_stat k_var k_ln k_exp k_n k_normed k_rot k_r k_roped
kv_turned kv_ready kv_stored q_sq q_scaled q_rot q_r q_roped q_ln q_exp q_n q_rs scored max_step nm_ready
probs_made inv_ready probs_scaled prob_turned pt_copied pv_done gated conv_in conv_clear conv_u conv_t conv_sum
conv_out gla_in aup_clear g_logit g_z g_min g_neg g_exp g_ln g_lf g_scan g_mid g_clamp g_factors g_small
g_smallx g_qk g_hat g_turned g_tok g_att g_masked g_summed g_u g_state g_o g_osq g_ostat g_ovar g_oln g_oexp
g_on g_normed g_out g_saved y_scaled y_turned y_taken y_out ones_set x_sum rope_in mask_in""".split()


SEED = 1
SEEDED = """wmod_used0 wmod_used1 wmod_used2 wmod_used3 split0 split1 mod_half mod_acc k_normed kv_turned pv_done q_sq q_scaled gated
g_saved x_new0 x_new1 mod_taken taken0 taken1 pt_copied probs_made g_out g_tok g_ovar tile_done0 tile_done1
stored0 stored1 k_stat kv_stored q_rot prob_turned x_high0 x_high1 mod_summed g_state mod_step0 mod_step1""".split()


def backbone(nc, io):
    with ExitStack() as ctx:
        def sb(name, shape, dtype=F32, stack=ctx):
            return stack.enter_context(nc.sbuf_tensor(name, shape, dtype))

        s = {name: ctx.enter_context(nc.semaphore(name)) for name in NAMES}

        proj_dram = nc.dram_tensor("proj_scratch", [T_LR + 1, P, TOK], F32)
        x_dram = nc.dram_tensor("x_scratch", [P, KT, TOK], F32)

        ident = sb("ident", [P, P])
        rotate = sb("rotate", [P, P])
        ones = sb("ones", [P, P])
        rows = sb("rows", [P, P])
        vecs = sb("vecs", [P, DEPTH, ROWS])
        head_rows = sb("head_rows", [3 * KT, P])
        head = sb("head", [P, 3 * KT])
        cond = sb("cond", [P, KT, 2])
        mod_raw = sb("mod_raw", [P, DEPTH, MOD_T, 2])
        mod = sb("mod", [P, MOD_T, 2])
        mod_a = sb("mod_a", [P, KT, 2])
        xf = sb("xf", [P, KT, TOK])
        sq_sum = sb("sq_sum", [P, TOK])
        raw = [sb(f"raw{i}", [P, KT, P]) for i in range(2)]
        high = [sb(f"high{i}", [P, KT, P], F32R) for i in range(2)]
        low = [sb(f"low{i}", [P, KT, P], F32R) for i in range(2)]
        stage = [sb(f"stage{i}", [P, TOK]) for i in range(2)]
        rstd = sb("rstd", [P, TOK])
        r_a = sb("r_a", [P, TOK])
        r_b = sb("r_b", [P, TOK])

        with ExitStack() as proj_space:
            def ps_(name, shape, dtype=F32):
                return sb(name, shape, dtype, proj_space)
            x_high = ps_("x_high", [P, KT, TOK], F32R)
            x_low = ps_("x_low", [P, KT, TOK], F32R)
            mraw = [ps_(f"mraw{i}", [P, KT // 2, 2 * P]) for i in range(2)]
            macc = ps_("macc", [P, 2, 2 * P])
        xt = [r_a, r_b]
        old = [m[:].rearrange("p k n -> p (k n)")[:, 0:TOK] for m in mraw]
        with ExitStack() as ends:
            xtok = sb("xtok", [P, TT, D], F32, ends)
            with ExitStack() as last:
                ytok = sb("ytok", [P, TT, D], F32, last)
            wmod = [sb(f"wmod{i}", [P, KT // 4, MOD_N], F32, ends) for i in range(4)]
            mod_rows = [sb(f"mod_rows{i}", [2, MOD_N], F32, ends) for i in range(2)]
        with ExitStack() as mixers:
            def mx(name, shape, dtype=F32, stack=mixers):
                return sb(name, shape, dtype, stack)
            cin = mx("cin", [P, 4, TOK])
            cu = mx("cu", [P, TOK + 3])
            ct = [mx(f"ct{i}", [P, TOK + 1]) for i in range(3)]
            with ExitStack() as att:
                def at_(name, shape):
                    return mx(name, shape, F32, att)
                cos, sin = at_("cos", [P, DEC]), at_("sin", [P, DEC])
                kraw, kn, ksq = at_("kraw", [P, TOK]), at_("kn", [P, TOK]), at_("ksq", [P, TOK])
                vraw, ck = at_("vraw", [P, TOK]), at_("ck", [P, P])
                keys = at_("keys", [P, KEYS + SEQ])
                vals = at_("vals", [P, TT + 1, P])
                newk = at_("newk", [P, P])
                qraw, qw, qsq = at_("qraw", [P, TOK]), at_("qw", [P, TOK]), at_("qsq", [P, TOK])
                ag = at_("ag", [P, TOK])
                t1, t2 = at_("t1", [P, DEC]), at_("t2", [P, DEC])
                qr = at_("qr", [P, DEC])
                qv, qa, qb, qs = (at_(n, [P, TT]) for n in ("qv", "qa", "qb", "qs"))
                mx_, nm, sums, inv = (at_(n, [P, TT]) for n in ("mx_", "nm", "sums", "inv"))
                probs = [at_(f"probs{i}", [P, KEYS]) for i in range(2)]
                probs_t = at_("probs_t", [P, TT, DEC])
                probs_p = at_("probs_p", [P, P])
            with ExitStack() as gla:
                def gl(name, shape):
                    return mx(name, shape, F32, gla)
                pair_mask, chunk_keep = gl("pair_mask", [P, 2, 2, P]), gl("chunk_keep", [P, TOK])
                gq, gk, lr = gl("gq", [P, TOK]), gl("gk", [P, TOK]), gl("lr", [LR_W, TOK])
                gv, gg = gl("gv", [P, 2, TOK]), gl("gg", [P, 2, TOK])
                aup = gl("aup", [LR_W, 2, P])
                gz, gm, cum = gl("gz", [P, 2, TOK]), gl("gm", [P, 2, TOK]), gl("cum", [P, 2, TOK])
                qt, kt_ = gl("qt", [P, 2, TOK]), gl("kt_", [P, 2, TOK])
                small = gl("small", [P, 2, 3, NCH])
                k_tok = gl("k_tok", [P, 2, TT, P])
                v_tok = gl("v_tok", [P, TT, 2, P])
                att_m, att_s = gl("att_m", [P, 2, 2, P]), gl("att_s", [P, TT, 2, P])
                states = gl("states", [P, 2, STATES, DV])
        psP = [ctx.enter_context(nc.psum_tensor(f"psP{i}", [P, 1024], F32)) for i in range(2)]
        psT = ctx.enter_context(nc.psum_tensor("psT", [P, 1024], F32))
        psO = ctx.enter_context(nc.psum_tensor("psO", [P, 1024], F32))

        per_layer = IN_PAIRS + OUT_PAIRS
        block = ctx.enter_context(nc.Block())

        def fence(eng, n):
            eng.drain().then_inc(s["phase_over"], 1)
            eng.wait_ge(s["phase_over"], 4 * n)

        @block.sync
        def _(sp):
            for name, dst in (("ident", ident[:]), ("rotate", rotate[:])):
                sp.dma_start(dst, io[name]).then_inc(s["consts_in"], 16)
            sp.dma_start(head_rows[0:KT, :], io["c"].rearrange("b (k p) -> (b k) p", p=P)).then_inc(s["rows_in"], 16)
            sp.dma_start(head_rows[KT:2 * KT, :], io["c_ctx"].rearrange("(k p) -> k p", p=P)).then_inc(s["rows_in"], 16)
            sp.dma_start(head_rows[2 * KT:, :], io["final_norm_w"].rearrange("(k p) -> k p", p=P)).then_inc(s["rows_in"], 16)
            for i in range(DEC // P):
                sp.dma_start(xtok[:, i, :], io["x_sample"][0, i * P:(i + 1) * P, :]).then_inc(s["x_in"], 16)
            sp.dma_start(xtok[:, TT - 1, :], io["x_prompt"][0]).then_inc(s["x_in"], 16)
            for l in range(DEPTH):
                sp.wait_ge(s["vecs_ready"], l)
                for at, src in (
                        (R_BMOD, io["b_mod"][l].rearrange("(k p) -> k p", p=P)),
                        (R_NORM, io["norm_w"][l].rearrange("(k p) -> k p", p=P)),
                        (R_Q, io["q_norm_w"][l:l + 1]), (R_K, io["k_norm_w"][l:l + 1]),
                        (R_CONV, io["conv_w"][l].rearrange("t (j p) -> (t j) p", p=P)),
                        (R_ABIAS, io["gla_a_bias"][l].rearrange("z (j p) -> (z j) p", p=P)),
                        (R_GNORM, io["gla_norm_w"][l:l + 1])):
                    sp.dma_start(rows[at:at + src.shape[0], :], src).then_inc(s["rows_in"], 16)
            def weight_pair(w, first, i, occ):
                for slot in range(2):
                    sp.wait_ge(s[f"split{slot}"], occ + i + SEED)
                    sp.dma_start(raw[slot][:], w[:, :, bass.ds((i * 2 + slot) * P + first * P, P)])\
                        .then_inc(s[f"raw_in{slot}"], 16)

            weight_pair(io["w_in"][0].rearrange("(k p) n -> p k n", p=P), 0, 0, 0)
            wm = io["w_mod"][0].rearrange("(k p) n -> p k n", p=P)
            with sp.Fori(0, MOD_CHUNKS) as i:
                for q in range(4):
                    sp.wait_ge(s[f"wmod_used{q}"], i + SEED)
                    sp.dma_start(wmod[q][:], wm[:, q * KT // 4:(q + 1) * KT // 4, bass.ds(i * MOD_N, MOD_N)])\
                        .then_inc(s[f"wmod_in{q}"], 16)

            def mod_weights(l, u):
                nxt = io["w_mod"][l + 1].rearrange("(k p) n -> p k n", p=P)
                for hf, used in enumerate(("mod_half", "mod_acc")):
                    sp.wait_ge(s[used], u + l * IN_PAIRS + SEED)
                    sp.dma_start(mraw[hf][:], nxt[:, hf * KT // 2:(hf + 1) * KT // 2, bass.ds(u * 2 * P, 2 * P)])\
                        .then_inc(s[f"mraw_in{hf}"], 16)

            for l in range(DEPTH):
                occ = l * per_layer
                w_in = io["w_in"][l].rearrange("(k p) n -> p k n", p=P)
                if l > 0:
                    weight_pair(w_in, 0, 0, occ)
                sp.wait_ge(s["phase_over"], 4 * (3 * l + 1))
                sp.dma_start(x_dram[:], xf[:]).then_inc(s["x_saved"], 16)
                if l + 1 < DEPTH:
                    mod_weights(l, 0)
                before = 0
                for run, (first, pairs, _) in enumerate(RUNS):
                    with sp.Fori(int(run == 0), pairs) as i:
                        weight_pair(w_in, first, i, occ + before)
                        if l + 1 < DEPTH:
                            mod_weights(l, i + before)
                    before += pairs
                sp.wait_ge(s["split0"], occ + IN_PAIRS + SEED)
                sp.dma_start(raw[0][:, :, 0:LR_W], w_in[:, :, T_LR * P:T_LR * P + LR_W]).then_inc(s["lr_in"], 16)

                sp.wait_ge(s["phase_over"], 4 * (3 * l + 2))
                sp.dma_start(cos[:], io["cos"]).then_inc(s["rope_in"], 16)
                sp.dma_start(sin[:], io["sin"]).then_inc(s["rope_in"], 16)
                with sp.Fori(0, KVH) as g:
                    kv = g + l * KVH
                    hd0 = g * GROUP + l * HEADS
                    sp.wait_ge(s["k_normed"], kv + SEED)
                    sp.dma_start(kraw[:], proj_dram[bass.ds(g + T_AK, 1)].rearrange("a p t -> p (a t)")).then_inc(s["k_in"], 16)
                    sp.wait_ge(s["kv_turned"], kv + SEED)
                    sp.dma_start(vraw[:], proj_dram[bass.ds(g + T_AV, 1)].rearrange("a p t -> p (a t)")).then_inc(s["v_in"], 16)
                    sp.dma_start(ck[:], io["cache_k"][0, l].rearrange("s g d -> s (g d)")[:, bass.ds(g * HD, HD)])\
                        .then_inc(s["ck_in"], 16)
                    sp.wait_ge(s["pv_done"], hd0 + SEED)
                    sp.dma_start(vals[:, TT, :], io["cache_v"][0, l].rearrange("s g d -> s (g d)")[:, bass.ds(g * HD, HD)])\
                        .then_inc(s["cv_in"], 16)
                    with sp.Fori(0, GROUP) as h:
                        hd = h + hd0
                        sp.wait_ge(s["q_sq"], hd + SEED)
                        sp.wait_ge(s["q_scaled"], hd + SEED)
                        sp.dma_start(qraw[:], proj_dram[bass.ds(g * GROUP + h + T_AQ, 1)].rearrange("a p t -> p (a t)"))\
                            .then_inc(s["q_in"], 16)
                        sp.wait_ge(s["gated"], hd + SEED)
                        sp.dma_start(ag[:], proj_dram[bass.ds(g * GROUP + h + T_AG, 1)].rearrange("a p t -> p (a t)"))\
                            .then_inc(s["ag_in"], 16)
                sp.wait_ge(s["gated"], (l + 1) * HEADS + SEED)
                sp.wait_ge(s["kv_stored"], 32 * (l + 1) * KVH + SEED)
                sp.wait_ge(s["aup_clear"], l + 1)
                sp.dma_start(pair_mask[:], io["pair_mask"]).then_inc(s["mask_in"], 16)
                sp.dma_start(chunk_keep[:], io["chunk_keep"]).then_inc(s["mask_in"], 16)
                w_out = io["w_out"][l].rearrange("(k p) n -> p k n", p=P)
                sp.wait_ge(s["lr_split"], l + 1)
                weight_pair(w_out, 0, 0, occ + IN_PAIRS)
                with sp.Fori(0, PAIRS) as pr:
                    sp.wait_ge(s["g_saved"], pr * 32 + l * 32 * PAIRS + SEED)
                    sp.dma_start(lr[:], proj_dram[T_LR, 0:LR_W, :]).then_inc(s["gla_in"], 16)
                    for z in range(2):
                        sp.dma_start(aup[z * RANK:(z + 1) * RANK, z, :], io["gla_a_up"][l, z][:, bass.ds(pr * P, P)])\
                            .then_inc(s["gla_in"], 16)
                    sp.dma_start(gq[:], proj_dram[bass.ds(pr + T_GQ, 1)].rearrange("a p t -> p (a t)")).then_inc(s["gla_in"], 16)
                    sp.dma_start(gk[:], proj_dram[bass.ds(pr + T_GK, 1)].rearrange("a p t -> p (a t)")).then_inc(s["gla_in"], 16)
                    sp.dma_start(gv[:], proj_dram[bass.ds(pr * 2 + T_GV, 2)].rearrange("a p t -> p a t")).then_inc(s["gla_in"], 16)
                    sp.dma_start(gg[:], proj_dram[bass.ds(pr * 2 + T_GG, 2)].rearrange("a p t -> p a t")).then_inc(s["gla_in"], 16)
                    for z in range(2):
                        sp.dma_start(states[:, z, 0, :], io["state_gla"][0, l, z].rearrange("h d v -> (h d) v")
                                     [bass.ds(pr * P, P), :]).then_inc(s["gla_in"], 16)

                def old_pair(i):
                    for slot in range(2):
                        sp.wait_ge(s[f"x_new{slot}"], i + l * OUT_PAIRS + SEED)
                        sp.dma_start(old[slot], x_dram[:, bass.ds(i * 2 + slot, 1), :].rearrange("p a t -> p (a t)"))\
                            .then_inc(s[f"old_in{slot}"], 16)

                sp.wait_ge(s["phase_over"], 4 * (3 * l + 3))
                old_pair(0)
                with sp.Fori(1, OUT_PAIRS) as i:
                    weight_pair(w_out, 0, i, occ + IN_PAIRS)
                    old_pair(i)
            for i in range(TT):
                sp.wait_ge(s["y_taken"], KT)
                dst = io["y_sample"][0, i * P:(i + 1) * P, :] if i < TT - 1 else io["y_prompt"][0]
                sp.dma_start(dst, ytok[:, i, :]).then_inc(s["y_out"], 16)
            sp.wait_ge(s["y_out"], 16 * TT)

        @block.tensor
        def _(pe):
            def spread(out, lhsT, rhs, start=True, stop=True):
                pe.matmul(out[:, 0:512], lhsT, rhs[:, 0:512], start=start, stop=stop)
                return pe.matmul(out[:, 512:TOK], lhsT, rhs[:, 512:TOK], start=start, stop=stop)

            pe.wait_ge(s["ones_set"], 1)
            pe.wait_ge(s["consts_in"], 16 * 2)
            pe.wait_ge(s["rows_in"], 16 * 10)
            pe.transpose(psO[:, 0:3 * KT], head_rows[:], ident[0:3 * KT, 0:3 * KT]).then_inc(s["rows_turned"], 1)
            pe.transpose(psT[:, 0:ROWS], rows[0:ROWS, :], ident[0:ROWS, 0:ROWS]).then_inc(s["rows_turned"], 1)
            pe.wait_ge(s["x_in"], 16 * TT)
            for k in range(KT):
                if k >= 2:
                    pe.wait_ge(s["x_taken"], k - 1)
                for i in range(TT):
                    mm = pe.transpose(psP[k % 2][:, i * P:(i + 1) * P], xtok[:, i, k * P:(k + 1) * P], ident[:])
                mm.then_inc(s["embed_turned"], 1)
            for l in range(1, DEPTH):
                pe.wait_ge(s["rows_in"], 16 * (10 + 7 * l))
                pe.wait_ge(s["vecs_ready"], l)
                pe.transpose(psT[:, 0:ROWS], rows[0:ROWS, :], ident[0:ROWS, 0:ROWS]).then_inc(s["rows_turned"], 1)
            pe.wait_ge(s["head_ready"], 1)
            pe.wait_ge(s["vecs_ready"], DEPTH)
            with pe.Fori(0, MOD_CHUNKS // 2) as i:
                for half in range(2):
                    if half == 0:
                        pe.wait_ge(s["mod_taken"], i + SEED)
                    for q in range(4):
                        pe.wait_ge(s[f"wmod_in{q}"], i * 32 + (half * 16 + 16))
                        for k in range(KT // 4):
                            n = q * KT // 4 + k
                            mm = pe.matmul(psT[0:2, half * 512:half * 512 + MOD_N], cond[:, n, :], wmod[q][:, k, :],
                                           start=(n == 0), stop=(n == KT - 1))
                        mm.then_inc(s[f"wmod_used{q}"], 1)
                for half in range(2):
                    pe.wait_ge(s["mod_row"], i * 2 + (half + 1))
                    for j in range(MOD_N // P):
                        at = (half * (MOD_N // P) + j) * 2
                        mm = pe.matmul(psO[:, at:at + 2], mod_rows[half][:, j * P:(j + 1) * P], ident[0:2, 0:2],
                                       start=True, stop=True)
                    mm.then_inc(s["mod_turned"], 1)

            def project(slot, operand=None, done=0):
                out = psP[slot]
                n = 0
                for k in range(KT):
                    if operand and k % 2 == 0:
                        pe.wait_ge(s[operand], done + k + 2)
                    for w, x in ((high, x_high), (high, x_low), (low, x_high)):
                        for half in range(2):
                            mm = pe.matmul(out[:, AT + half * HALF:AT + (half + 1) * HALF], w[slot][:, k, :],
                                           x[:, k, half * HALF:(half + 1) * HALF],
                                           start=(n == 0), stop=(n == 3 * KT - 1))
                        n += 1
                return mm

            def pair(i, occ, operand=None, done=0):
                for slot in range(2):
                    pe.wait_ge(s[f"split{slot}"], i + occ + 1 + SEED)
                    pe.wait_ge(s[f"taken{slot}"], i + occ + SEED)
                    project(slot, operand if slot == 0 else None, done).then_inc(s[f"tile_done{slot}"], 1)

            def mod_sums(l, u):
                pe.wait_ge(s["mod_acc"], u + l * IN_PAIRS + 1 + SEED)
                pe.wait_ge(s["mod_taken"], u + l * IN_PAIRS + MOD_CHUNKS // 2 + SEED)
                for n in range(2):
                    for v in range(2):
                        mm = pe.matmul(psT[:, 2 * n + v:2 * n + v + 1], macc[:, v, n * P:(n + 1) * P],
                                       ones[:, 0:1], start=True, stop=True)
                mm.then_inc(s["mod_summed"], 1)

            for l in range(DEPTH):
                occ = l * per_layer
                fence(pe, 3 * l + 1)
                spread(psO, ones[:], sq_sum).then_inc(s["stat_summed"], 1)
                pair(0, occ, "x_split", KT * l)
                if l + 1 < DEPTH:
                    mod_sums(l, 0)
                before = 0
                for run, (first, pairs, _) in enumerate(RUNS):
                    with pe.Fori(int(run == 0), pairs) as i:
                        pair(i, occ + before)
                        if l + 1 < DEPTH:
                            mod_sums(l, i + before)
                    before += pairs
                pe.wait_ge(s["lr_split"], l + 1)
                pe.wait_ge(s["taken0"], occ + IN_PAIRS + SEED)
                project(0).then_inc(s["lr_done"], 1)

                fence(pe, 3 * l + 2)
                with pe.Fori(0, KVH) as g:
                    kv = g + l * KVH
                    hd0 = g * GROUP + l * HEADS
                    pe.wait_ge(s["k_sq"], kv + 1)
                    pe.wait_ge(s["gated"], hd0 + SEED)
                    spread(psO, ones[:], ksq).then_inc(s["k_stat"], 1)
                    pe.wait_ge(s["k_normed"], kv + 1 + SEED)
                    pe.matmul(psO[:, 0:DEC], rotate[:], kn[:, 0:DEC], start=True, stop=True).then_inc(s["k_rot"], 1)
                    pe.wait_ge(s["v_in"], kv * 16 + 16)
                    pe.wait_ge(s["ck_in"], kv * 16 + 16)
                    pe.wait_ge(s["pt_copied"], hd0 * TT + SEED)
                    pe.transpose(psT[:, 0:P], kn[:, DEC:TOK], ident[:])
                    pe.transpose(psT[:, P:2 * P], ck[:], ident[:])
                    for i in range(TT):
                        mm = pe.transpose(psT[:, (i + 2) * P:(i + 3) * P], vraw[:, i * P:(i + 1) * P], ident[:])
                    mm.then_inc(s["kv_turned"], 1)
                    with pe.Fori(0, GROUP) as h:
                        hd = h + hd0
                        pe.wait_ge(s["q_scaled"], hd + 1 + SEED)
                        pe.wait_ge(s["gated"], hd + SEED)
                        pe.matmul(psO[:, 0:DEC], rotate[:], qw[:, 0:DEC], start=True, stop=True)
                        pe.wait_ge(s["q_sq"], hd + 1 + SEED)
                        for i in range(TT):
                            mm = pe.matmul(psO[:, TOK + i:TOK + i + 1], qsq[:, i * P:(i + 1) * P], ones[:, 0:1],
                                           start=True, stop=True)
                        mm.then_inc(s["q_rot"], 1)
                        pe.wait_ge(s["q_roped"], hd + 1)
                        pe.wait_ge(s["kv_ready"], kv * 3 + 3)
                        pe.wait_ge(s["k_roped"], kv + 1)
                        pe.wait_ge(s["cv_in"], kv * 16 + 16)

                        def score(i):
                            pe.wait_ge(s["probs_made"], hd * TT + max(i - 1, 0) + SEED)
                            if i < TT - 1:
                                q = qr[:, i * P:(i + 1) * P]
                                pe.matmul(psP[i % 2][:, 0:512], q, keys[:, 0:512], start=True, stop=True)
                                mm = pe.matmul(psP[i % 2][:, 512:KEYS], q, keys[:, 512:KEYS], start=True, stop=True)
                            else:
                                mm = pe.matmul(psP[i % 2][:, 0:SEQ], qw[:, DEC:TOK], keys[:, KEYS:KEYS + SEQ],
                                               start=True, stop=True)
                            mm.then_inc(s["scored"], 1)

                        def turn(i):
                            pe.wait_ge(s["probs_scaled"], hd * TT + i + 1)
                            pe.wait_ge(s["pt_copied"], hd * TT + i + SEED)
                            for j in range(KEYS // P if i < TT - 1 else 1):
                                mm = pe.transpose(psT[:, j * P:(j + 1) * P], probs[i % 2][:, j * P:(j + 1) * P], ident[:])
                            mm.then_inc(s["prob_turned"], 1)

                        score(0)
                        for i in range(1, TT):
                            score(i)
                            turn(i - 1)
                        turn(TT - 1)
                        pe.wait_ge(s["pt_copied"], hd * TT + TT + SEED)
                        for j in range(TT):
                            pe.matmul(psO[:, 0:DEC], vals[:, j if j < TT - 1 else TT, :], probs_t[:, j, :],
                                      start=(j == 0), stop=(j == TT - 1))
                        pe.matmul(psO[:, DEC:TOK], vals[:, TT - 1, :], probs_p[:], start=True, stop=True)\
                            .then_inc(s["pv_done"], 1)

                pe.wait_ge(s["gated"], (l + 1) * HEADS + SEED)
                with pe.Fori(0, PAIRS) as pr:
                    gp = pr + l * PAIRS
                    pe.wait_ge(s["gla_in"], gp * 16 * 9 + 16 * 9)
                    pe.wait_ge(s["g_out"], gp * 2 + SEED)
                    for z in range(2):
                        spread(psP[z], aup[:, z, :], lr).then_inc(s["g_logit"], 1)
                    for hh in range(2):
                        pe.wait_ge(s["g_tok"], gp * 4 + hh + SEED)
                        for i in range(TT):
                            mm = pe.transpose(psT[:, i * P:(i + 1) * P], gv[:, hh, i * P:(i + 1) * P], ident[:])
                        mm.then_inc(s["g_turned"], 1)
                    pe.wait_ge(s["g_qk"], gp * 2 + 2)
                    for i in range(TT):
                        if i >= 2:
                            pe.wait_ge(s["g_masked"], gp * TT + i - 1)
                        else:
                            pe.wait_ge(s["g_z"], gp * 2 + 2)
                        for z in range(2):
                            for hh in range(2):
                                part = slice(hh * DK, (hh + 1) * DK)
                                mm = pe.matmul(psP[i % 2][:, hh * 512 + z * P:][:, 0:P],
                                               kt_[part, z, i * P:(i + 1) * P], qt[part, z, i * P:(i + 1) * P],
                                               start=True, stop=True)
                        mm.then_inc(s["g_att"], 1)
                    pe.wait_ge(s["g_hat"], gp * 4 + 4)
                    for z in range(2):
                        pe.wait_ge(s["g_tok"], gp * 4 + 2 + z + SEED)
                        for i in range(TT):
                            mm = pe.transpose(psT[:, i * P:(i + 1) * P], gm[:, z, i * P:(i + 1) * P], ident[:])
                        mm.then_inc(s["g_turned"], 1)
                    pe.wait_ge(s["g_tok"], gp * 4 + 4 + SEED)
                    for n, (fwd, bwd) in enumerate(STEPS):
                        if n >= 2:
                            pe.wait_ge(s["g_state"], (gp * len(STEPS) + n - 1) * 4 + SEED)
                        for z, ch in enumerate((fwd, bwd)):
                            part = slice(ch % 2 * CH, (ch % 2 + 1) * CH)
                            mm = pe.matmul((psT, psO)[n % 2][:, ch % 2 * 512:][:, 0:256], k_tok[part, z, ch // 2, :],
                                           v_tok[part, ch // 2, :, :].rearrange("p a b -> p (a b)"),
                                           start=True, stop=True)
                        mm.then_inc(s["g_u"], 1)
                    pe.wait_ge(s["g_state"], (gp + 1) * len(STEPS) * 4 + SEED)
                    pe.wait_ge(s["g_summed"], gp * TT + TT)
                    for hh in range(2):
                        part = slice(hh * DK, (hh + 1) * DK)
                        for i in range(TT):
                            parts = [(z, ch) for ch in (2 * i, 2 * i + 1) for z in range(2)
                                     if state_at(z, ch) != DEC_CH + 1]
                            pe.matmul(psP[hh][:, i * P:(i + 1) * P], v_tok[:, i, hh, :], att_s[:, i, hh, :],
                                      start=True, stop=False)
                            for n, (z, ch) in enumerate(parts):
                                mm = pe.matmul(psP[hh][:, ch * CH:(ch + 1) * CH], states[part, z, state_at(z, ch), :],
                                               gz[part, z, ch * CH:(ch + 1) * CH],
                                               start=False, stop=(n == len(parts) - 1))
                        mm.then_inc(s["g_o"], 1)
                    for hh in range(2):
                        pe.wait_ge(s["g_osq"], gp * 2 + hh + 1)
                        pe.wait_ge(s["g_ovar"], gp * 2 + hh + SEED)
                        spread(psO, ones[:], stage[hh]).then_inc(s["g_ostat"], 1)

                fence(pe, 3 * l + 3)
                pair(0, occ + IN_PAIRS, "mix_split", KT * l)
                with pe.Fori(1, OUT_PAIRS) as i:
                    pair(i, occ + IN_PAIRS)

            fence(pe, 3 * DEPTH + 1)
            spread(psO, ones[:], sq_sum).then_inc(s["stat_summed"], 1)
            for k in range(KT):
                pe.wait_ge(s["y_scaled"], k + 1)
                if k >= 2:
                    pe.wait_ge(s["y_taken"], k - 1)
                for i in range(TT):
                    mm = pe.transpose(psP[k % 2][:, i * P:(i + 1) * P], xf[:, k, i * P:(i + 1) * P], ident[:])
                mm.then_inc(s["y_turned"], 1)

        @block.scalar
        def _(act):
            act.wait_ge(s["rows_turned"], 1)
            act.activation(head[:], psO[:, 0:3 * KT], ACT.Copy).then_inc(s["head_ready"], 1)
            act.wait_ge(s["head_ready"], 1)
            act.activation(cond[:].rearrange("p k v -> p v k"), head[:, 0:2 * KT].rearrange("p (v k) -> p v k", v=2),
                           ACT.Silu).then_inc(s["head_ready"], 1)
            act.wait_ge(s["rows_turned"], 2)
            act.activation(vecs[:, 0, :], psT[:, 0:ROWS], ACT.Copy).then_inc(s["vecs_ready"], 1)
            for k in range(KT):
                act.wait_ge(s["embed_turned"], k + 1)
                act.activation(xf[:, k, :], psP[k % 2][:, 0:TOK], ACT.Copy).then_inc(s["x_taken"], 1)
            for l in range(1, DEPTH):
                act.wait_ge(s["rows_turned"], l + 2)
                act.activation(vecs[:, l, :], psT[:, 0:ROWS], ACT.Copy).then_inc(s["vecs_ready"], 1)
            with act.Fori(0, MOD_CHUNKS // 2) as i:
                for half in range(2):
                    act.wait_ge(s["wmod_used3"], i * 2 + (half + 1 + SEED))
                    act.activation(mod_rows[half][:], psT[0:2, half * 512:half * 512 + MOD_N], ACT.Copy)\
                        .then_inc(s["mod_row"], 1)
                act.wait_ge(s["mod_turned"], i * 2 + 2)
                act.activation(mod_raw[:, 0, bass.ds(i * (2 * MOD_N // P), 2 * MOD_N // P), :].rearrange("p a b -> p (a b)"),
                               psO[:, 0:4 * MOD_N // P], ACT.Copy).then_inc(s["mod_taken"], 1)

            def ln_exp(src, tmp, out, ready, n, ln_sem, exp_sem):
                act.wait_ge(s[ready], n + (SEED if ready in SEEDED else 0))
                act.activation(tmp, src, ACT.Ln).then_inc(s[ln_sem], 1)
                act.wait_ge(s[ln_sem], n)
                act.activation(out, tmp, ACT.Exp, scale=-0.5).then_inc(s[exp_sem], 1)

            for l in range(DEPTH):
                occ = l * per_layer
                fence(act, 3 * l + 1)
                ln_exp(r_a[:], rstd[:], r_b[:], "stat_var", l + 1, "stat_ln", "stat_exp")
                act.wait_ge(s["mod_ready"], l + 1)
                with act.Fori(0, KT // 2) as i:
                    for slot in range(2):
                        act.wait_ge(s[f"scaled{slot}"], i + l * KT // 2 + 1)
                        for v, part in ((0, slice(0, DEC)), (1, slice(DEC, TOK))):
                            a = act.activation(stage[slot][:, part], xt[slot][:, part], ACT.Identity,
                                               bias=mod[:, bass.ds(i * 2 + slot, 1), v:v + 1].rearrange("p a b -> p (a b)"),
                                               scale=mod_a[:, bass.ds(i * 2 + slot, 1), v:v + 1].rearrange("p a b -> p (a b)"))
                            a.then_inc(s[f"shifted{slot}"], 1)
                        act.wait_ge(s[f"shifted{slot}"], i * 2 + l * KT + 2)
                        act.activation(x_high[:, bass.ds(i * 2 + slot, 1), :], stage[slot][:], ACT.Copy)\
                            .then_inc(s[f"x_high{slot}"], 1)
                before = 0
                act.wait_ge(s["x_split"], KT * (l + 1))
                for run, (first, pairs, gate) in enumerate(RUNS):
                    with act.Fori(0, pairs) as i:
                        for slot in range(2):
                            act.wait_ge(s[f"stored{slot}"], i * 16 + (before + l * IN_PAIRS) * 16 + SEED)
                            act.wait_ge(s[f"tile_done{slot}"], i + occ + before + 1 + SEED)
                            act.activation(stage[slot][:], psP[slot][:, AT:AT + TOK], ACT.Silu if gate else ACT.Copy)\
                                .then_inc(s[f"taken{slot}"], 1)
                            act.wait_ge(s[f"taken{slot}"], i + occ + before + 1 + SEED)
                            act.dma_start(proj_dram[bass.ds(i * 2 + (slot + first), 1)].rearrange("a p t -> p (a t)"),
                                          stage[slot][:]).then_inc(s[f"stored{slot}"], 16)
                        if l + 1 < DEPTH:
                            act.wait_ge(s["mod_summed"], i + before + l * IN_PAIRS + 1 + SEED)
                            act.activation(mod_raw[:, l + 1, bass.ds((i + before) * 2, 2), :].rearrange("p a b -> p (a b)"),
                                           psT[:, 0:4], ACT.Copy).then_inc(s["mod_taken"], 1)
                    before += pairs
                for slot in range(2):
                    act.wait_ge(s[f"stored{slot}"], 16 * IN_PAIRS * (l + 1) + SEED)
                act.wait_ge(s["lr_done"], l + 1)
                act.activation(stage[0][0:LR_W, :], psP[0][0:LR_W, AT:AT + TOK], ACT.Copy).then_inc(s["lr_taken"], 1)
                act.wait_ge(s["lr_taken"], l + 1)
                act.dma_start(proj_dram[T_LR, 0:LR_W, :], stage[0][0:LR_W, :]).then_inc(s["lr_stored"], 16)
                act.wait_ge(s["lr_stored"], 16 * (l + 1))

                fence(act, 3 * l + 2)
                with act.Fori(0, KVH) as g:
                    kv = g + l * KVH
                    hd0 = g * GROUP + l * HEADS
                    act.wait_ge(s["k_in"], kv * 16 + 16)
                    act.wait_ge(s["k_stat"], kv + SEED)
                    act.activation(ksq[:], kraw[:], ACT.Square).then_inc(s["k_sq"], 1)
                    ln_exp(r_a[:], rstd[:], r_b[:], "k_var", kv + 1, "k_ln", "k_exp")
                    act.wait_ge(s["kv_turned"], kv + 1 + SEED)
                    act.wait_ge(s["kv_stored"], kv * 32 + SEED)
                    act.activation(newk[:], psT[:, 0:P], ACT.Copy).then_inc(s["kv_ready"], 1)
                    act.activation(keys[:, DEC:KEYS], psT[:, P:2 * P], ACT.Copy).then_inc(s["kv_ready"], 1)
                    act.activation(vals[:, 0:TT, :], psT[:, 2 * P:2 * P + TOK].rearrange("p (a b) -> p a b", b=P), ACT.Copy)\
                        .then_inc(s["kv_ready"], 1)
                    act.wait_ge(s["kv_ready"], kv * 3 + 3)
                    act.dma_start(io["new_k"][0, l].rearrange("s g d -> s (g d)")[:, bass.ds(g * HD, HD)], newk[:])\
                        .then_inc(s["kv_stored"], 16)
                    act.dma_start(io["new_v"][0, l].rearrange("s g d -> s (g d)")[:, bass.ds(g * HD, HD)],
                                  vals[:, TT - 1, :]).then_inc(s["kv_stored"], 16)
                    with act.Fori(0, GROUP) as h:
                        hd = h + hd0
                        act.wait_ge(s["q_in"], hd * 16 + 16)
                        act.wait_ge(s["q_rot"], hd + SEED)
                        act.activation(qsq[:], qraw[:], ACT.Square).then_inc(s["q_sq"], 1)
                        ln_exp(qv[:], qb[:], qa[:], "q_roped", hd + 1, "q_ln", "q_exp")
                        act.wait_ge(s["q_rs"], hd + 1)

                        def prob(i):
                            width = KEYS if i < TT - 1 else SEQ
                            act.wait_ge(s["nm_ready"], hd * TT + i + 1)
                            act.wait_ge(s["prob_turned"], hd * TT + max(i - 1, 0) + SEED)
                            act.activation(probs[i % 2][:, 0:width], psP[i % 2][:, 0:width], ACT.Exp,
                                           bias=nm[:, i:i + 1], scale=qs[:, i:i + 1], accum_out=sums[:, i:i + 1])\
                                .then_inc(s["probs_made"], 1)

                        def take(i):
                            act.wait_ge(s["prob_turned"], hd * TT + i + 1 + SEED)
                            if i < TT - 1:
                                act.activation(probs_t[:, :, i * P:(i + 1) * P],
                                               psT[:, 0:KEYS].rearrange("p (a b) -> p a b", b=P), ACT.Copy)\
                                    .then_inc(s["pt_copied"], 1)
                            else:
                                act.activation(probs_p[:], psT[:, 0:P], ACT.Copy).then_inc(s["pt_copied"], 1)

                        prob(0)
                        for i in range(1, TT):
                            prob(i)
                            if i == 1:
                                act.wait_ge(s["pv_done"], hd + SEED)
                            take(i - 1)
                        take(TT - 1)
                act.wait_ge(s["gated"], (l + 1) * HEADS + SEED)
                with act.Fori(0, PAIRS) as pr:
                    gp = pr + l * PAIRS
                    act.wait_ge(s["g_out"], gp * 2 + SEED)
                    for z in range(2):
                        act.wait_ge(s["g_logit"], gp * 2 + z + 1)
                        act.activation(gz[:, z, :], psP[z][:, 0:TOK], ACT.Identity,
                                       bias=vecs[:, l, bass.ds(pr + (R_ABIAS + z * PAIRS), 1)]).then_inc(s["g_z"], 1)
                    for hh in range(2):
                        act.wait_ge(s["g_turned"], gp * 4 + hh + 1)
                        act.activation(v_tok[:, :, hh, :], psT[:, 0:TOK].rearrange("p (a b) -> p a b", b=P), ACT.Copy)\
                            .then_inc(s["g_tok"], 1)
                    act.wait_ge(s["g_neg"], gp + 1)
                    act.activation(cum[:], gz[:], ACT.Exp).then_inc(s["g_exp"], 1)
                    act.wait_ge(s["g_exp"], gp + 1)
                    act.activation(gz[:], cum[:], ACT.Ln, bias=1.0).then_inc(s["g_ln"], 1)
                    act.wait_ge(s["g_clamp"], gp + 1)
                    act.activation(qt[:], gm[:], ACT.Exp, scale=1 / TAU).then_inc(s["g_factors"], 1)
                    act.activation(kt_[:], gm[:], ACT.Exp, scale=-1 / TAU).then_inc(s["g_factors"], 1)
                    act.wait_ge(s["g_small"], gp * 2 + 2)
                    act.activation(small[:], small[:], ACT.Exp, scale=1 / TAU).then_inc(s["g_smallx"], 1)
                    for z in range(2):
                        act.wait_ge(s["g_turned"], gp * 4 + 3 + z)
                        act.activation(k_tok[:, z, :, :], psT[:, 0:TOK].rearrange("p (a b) -> p a b", b=P), ACT.Copy)\
                            .then_inc(s["g_tok"], 1)
                    for hh in range(2):
                        act.wait_ge(s["g_o"], gp * 2 + hh + 1)
                        act.activation(stage[hh][:], psP[hh][:, 0:TOK], ACT.Square).then_inc(s["g_osq"], 1)
                    for hh in range(2):
                        ln_exp(r_a[:], rstd[:], r_b[:], "g_ovar", gp * 2 + hh + 1, "g_oln", "g_oexp")
                    act.wait_ge(s["g_out"], gp * 2 + 2 + SEED)
                    for z in range(2):
                        act.dma_start(io["new_state"][0, l, z].rearrange("h d v -> (h d) v")[bass.ds(pr * P, P), :],
                                      states[:, z, STATES - 1, :]).then_inc(s["g_saved"], 16)
                act.wait_ge(s["g_saved"], 32 * PAIRS * (l + 1) + SEED)
                act.wait_ge(s["kv_stored"], 32 * KVH * (l + 1) + SEED)

                fence(act, 3 * l + 3)
                with act.Fori(0, KT) as k:
                    act.activation(x_high[:, bass.ds(k, 1), :], xf[:, bass.ds(k, 1), :], ACT.Copy)\
                        .then_inc(s["mix_high"], 1)
                with act.Fori(0, OUT_PAIRS) as i:
                    for slot in range(2):
                        act.wait_ge(s[f"x_new{slot}"], i + l * OUT_PAIRS + SEED)
                        act.wait_ge(s[f"tile_done{slot}"], i + occ + IN_PAIRS + 1 + SEED)
                        for v, part in ((0, slice(0, DEC)), (1, slice(DEC, TOK))):
                            a = act.activation(stage[slot][:, part], psP[slot][:, AT:AT + TOK][:, part], ACT.Identity,
                                               scale=mod[:, bass.ds(i * 2 + (slot + 2 * KT), 1), v:v + 1]
                                               .rearrange("p a b -> p (a b)"))
                        a.then_inc(s[f"taken{slot}"], 1)

            fence(act, 3 * DEPTH + 1)
            ln_exp(r_a[:], rstd[:], r_b[:], "stat_var", DEPTH + 1, "stat_ln", "stat_exp")
            for k in range(KT):
                act.wait_ge(s["y_turned"], k + 1)
                act.activation(ytok[:, :, k * P:(k + 1) * P], psP[k % 2][:, 0:TOK].rearrange("p (a b) -> p a b", b=P),
                               ACT.Copy).then_inc(s["y_taken"], 1)

        @block.vector
        def _(dve):
            dve.memset(ones[:], 1.0).then_inc(s["ones_set"], 1)
            for k in range(KT):
                dve.wait_ge(s["x_taken"], k + 1)
                if k == 0:
                    dve.tensor_tensor(sq_sum[:], xf[:, k, :], xf[:, k, :], ALU.mult).then_inc(s["x_squared"], 1)
                    continue
                dve.wait_ge(s["x_squared"], 2 * k - 1)
                dve.tensor_tensor(r_a[:], xf[:, k, :], xf[:, k, :], ALU.mult).then_inc(s["x_squared"], 1)
                dve.wait_ge(s["x_squared"], 2 * k)
                dve.tensor_tensor(sq_sum[:], sq_sum[:], r_a[:], ALU.add).then_inc(s["x_squared"], 1)

            def refine(out, v, r0, tmp, exp_sem, n, step_sem, base, scale=None):
                dve.wait_ge(s[exp_sem], n)
                dve.scalar_tensor_tensor(tmp, r0, -0.5, r0, ALU.mult, ALU.mult).then_inc(s[step_sem], 1)
                dve.wait_ge(s[step_sem], base + 1)
                dve.tensor_tensor(tmp, tmp, v, ALU.mult).then_inc(s[step_sem], 1)
                dve.wait_ge(s[step_sem], base + 2)
                return dve.scalar_tensor_tensor(out, tmp, 1.5, r0, ALU.add, ALU.mult)

            def split(slot, i, occ):
                dve.wait_ge(s[f"raw_in{slot}"], (i + occ) * 16 + 16)
                dve.wait_ge(s[f"tile_done{slot}"], i + occ + SEED)
                dve.tensor_copy(high[slot][:], raw[slot][:]).then_inc(s[f"high{slot}"], 1)
                dve.wait_ge(s[f"high{slot}"], i + occ + 1)
                dve.tensor_tensor(low[slot][:], raw[slot][:], high[slot][:].bitcast(F32), ALU.subtract)\
                    .then_inc(s[f"split{slot}"], 1)

            def mod_tiles(u):
                dve.wait_ge(s["mod_summed"], u + SEED)
                for n in range(KT):
                    hf, k = n // (KT // 2), n % (KT // 2)
                    if k == 0:
                        dve.wait_ge(s[f"mraw_in{hf}"], u * 16 + 16)
                    for v in range(2):
                        c = cond[:, n, v:v + 1]
                        if n == 0:
                            m = dve.tensor_scalar(macc[:, v, :], mraw[hf][:, k, :], c, None, ALU.mult)
                        else:
                            if v == 0:
                                dve.wait_ge(s["mod_step0"], u * (KT - 1) + n + SEED)
                            elif n == KT // 2:
                                dve.wait_ge(s["mod_half"], u + 1 + SEED)
                            else:
                                dve.wait_ge(s["mod_step1"], u * (KT - 2) + (n if n < KT // 2 else n - 1) + SEED)
                            m = dve.scalar_tensor_tensor(macc[:, v, :], mraw[hf][:, k, :], c,
                                                         macc[:, v, :], ALU.mult, ALU.add)
                        if v == 0 and n < KT - 1:
                            m.then_inc(s["mod_step0"], 1)
                        elif v == 1 and n == KT // 2 - 1:
                            m.then_inc(s["mod_half"], 1)
                        elif v == 1 and n == KT - 1:
                            m.then_inc(s["mod_acc"], 1)
                        elif v == 1:
                            m.then_inc(s["mod_step1"], 1)

            for l in range(DEPTH):
                occ = l * per_layer
                split(0, 0, occ)
                fence(dve, 3 * l + 1)
                dve.wait_ge(s["mod_taken"], MOD_CHUNKS // 2 + l * IN_PAIRS + SEED)
                dve.wait_ge(s["vecs_ready"], DEPTH)
                dve.tensor_tensor(mod[:], mod_raw[:, l], vecs[:, l, R_BMOD:R_BMOD + MOD_T].unsqueeze(2)
                                  .to_broadcast([P, MOD_T, 2]), ALU.add).then_inc(s["mod_added"], 1)
                dve.wait_ge(s["mod_added"], l + 1)
                dve.scalar_tensor_tensor(mod_a[:], mod[:, KT:2 * KT, :], 1.0, vecs[:, l, R_NORM:R_NORM + KT].unsqueeze(2)
                                         .to_broadcast([P, KT, 2]), ALU.add, ALU.mult).then_inc(s["mod_ready"], 1)
                dve.wait_ge(s["stat_summed"], l + 1)
                dve.tensor_scalar(r_a[:], psO[:, 0:TOK], 1.0 / D, EPS, ALU.mult, ALU.add).then_inc(s["stat_var"], 1)
                refine(rstd[:], r_a[:], r_b[:], sq_sum[:], "stat_exp", l + 1, "stat_rs", 3 * l)\
                    .then_inc(s["stat_rs"], 1)
                dve.wait_ge(s["stat_rs"], 3 * l + 3)
                with dve.Fori(0, KT // 2) as i:
                    n = i + l * KT // 2
                    for slot in range(2):
                        dve.wait_ge(s[f"x_high{slot}"], n + SEED)
                        dve.tensor_tensor(xt[slot][:], xf[:, bass.ds(i * 2 + slot, 1), :].rearrange("p a b -> p (a b)"),
                                          rstd[:], ALU.mult).then_inc(s[f"scaled{slot}"], 1)
                    for slot in range(2):
                        dve.wait_ge(s[f"x_high{slot}"], n + 1 + SEED)
                        dve.tensor_tensor(x_low[:, bass.ds(i * 2 + slot, 1), :].rearrange("p a b -> p (a b)"), stage[slot][:],
                                          x_high[:, bass.ds(i * 2 + slot, 1), :].rearrange("p a b -> p (a b)").bitcast(F32),
                                          ALU.subtract).then_inc(s["x_split"], 1)
                split(1, 0, occ)
                if l + 1 < DEPTH:
                    mod_tiles(l * IN_PAIRS)
                before = 0
                for run, (first, pairs, _) in enumerate(RUNS):
                    with dve.Fori(int(run == 0), pairs) as i:
                        for slot in range(2):
                            split(slot, i, occ + before)
                        if l + 1 < DEPTH:
                            mod_tiles(i + (before + l * IN_PAIRS))
                    before += pairs
                dve.wait_ge(s["lr_in"], 16 * (l + 1))
                dve.wait_ge(s["tile_done0"], occ + IN_PAIRS + SEED)
                dve.tensor_copy(high[0][:, :, 0:LR_W], raw[0][:, :, 0:LR_W]).then_inc(s["lr_high"], 1)
                dve.wait_ge(s["lr_high"], l + 1)
                dve.tensor_tensor(low[0][:, :, 0:LR_W], raw[0][:, :, 0:LR_W], high[0][:, :, 0:LR_W].bitcast(F32),
                                  ALU.subtract).then_inc(s["lr_split"], 1)

                fence(dve, 3 * l + 2)
                dve.wait_ge(s["x_saved"], 16 * (l + 1))
                dve.wait_ge(s["rope_in"], 32 * (l + 1))
                with dve.Fori(0, KVH) as g:
                    kv = g + l * KVH
                    hd0 = g * GROUP + l * HEADS
                    dve.wait_ge(s["k_stat"], kv + 1 + SEED)
                    dve.tensor_scalar(r_a[:], psO[:, 0:TOK], 1.0 / HD, EPS, ALU.mult, ALU.add).then_inc(s["k_var"], 1)
                    refine(rstd[:], r_a[:], r_b[:], ksq[:], "k_exp", kv + 1, "k_n", kv * 3).then_inc(s["k_n"], 1)
                    dve.wait_ge(s["k_n"], kv * 3 + 3)
                    dve.wait_ge(s["kv_turned"], kv + SEED)
                    dve.scalar_tensor_tensor(kn[:], kraw[:], vecs[:, l, R_K:R_K + 1], rstd[:], ALU.mult, ALU.mult)\
                        .then_inc(s["k_normed"], 1)
                    dve.wait_ge(s["k_rot"], kv + 1)
                    dve.tensor_tensor(t2[:], psO[:, 0:DEC], sin[:], ALU.mult).then_inc(s["k_r"], 1)
                    dve.wait_ge(s["k_normed"], kv + 1 + SEED)
                    dve.tensor_tensor(t1[:], kn[:, 0:DEC], cos[:], ALU.mult).then_inc(s["k_r"], 1)
                    dve.tensor_copy(keys[:, KEYS:], kn[:, DEC:TOK]).then_inc(s["k_r"], 1)
                    dve.wait_ge(s["k_r"], kv * 3 + 3)
                    dve.tensor_tensor(keys[:, 0:DEC], t1[:], t2[:], ALU.add).then_inc(s["k_roped"], 1)
                    with dve.Fori(0, GROUP) as h:
                        hd = h + hd0
                        dve.wait_ge(s["q_in"], hd * 16 + 16)
                        dve.tensor_scalar(qw[:], qraw[:], vecs[:, l, R_Q:R_Q + 1], None, ALU.mult).then_inc(s["q_scaled"], 1)
                        dve.wait_ge(s["q_rot"], hd + 1 + SEED)
                        dve.tensor_tensor(t2[:], psO[:, 0:DEC], sin[:], ALU.mult).then_inc(s["q_r"], 1)
                        dve.wait_ge(s["q_scaled"], hd + 1 + SEED)
                        dve.tensor_tensor(t1[:], qw[:, 0:DEC], cos[:], ALU.mult).then_inc(s["q_r"], 1)
                        dve.tensor_scalar(qv[:], psO[:, TOK:TOK + TT], 1.0 / HD, EPS, ALU.mult, ALU.add)\
                            .then_inc(s["q_r"], 1)
                        dve.wait_ge(s["q_r"], hd * 3 + 3)
                        dve.tensor_tensor(qr[:], t1[:], t2[:], ALU.add).then_inc(s["q_roped"], 1)
                        refine(inv[:], qv[:], qa[:], mx_[:], "q_exp", hd + 1, "q_n", hd * 3).then_inc(s["q_n"], 1)
                        dve.wait_ge(s["q_n"], hd * 3 + 3)
                        dve.tensor_scalar(qs[:], inv[:], HD ** -0.5, None, ALU.mult).then_inc(s["q_rs"], 1)
                        dve.wait_ge(s["q_rs"], hd + 1)

                        def row_max(i):
                            width = KEYS if i < TT - 1 else SEQ
                            dve.wait_ge(s["scored"], hd * TT + i + 1)
                            dve.tensor_reduce(mx_[:, i:i + 1], psP[i % 2][:, 0:width], AX.X, ALU.max)\
                                .then_inc(s["max_step"], 1)
                            dve.wait_ge(s["max_step"], hd * TT + i + 1)
                            dve.tensor_scalar(nm[:, i:i + 1], mx_[:, i:i + 1], qs[:, i:i + 1], -1.0, ALU.mult, ALU.mult)\
                                .then_inc(s["nm_ready"], 1)

                        def scale_probs(i):
                            width = KEYS if i < TT - 1 else SEQ
                            dve.wait_ge(s["probs_made"], hd * TT + i + 1 + SEED)
                            dve.reciprocal(inv[:, i:i + 1], sums[:, i:i + 1]).then_inc(s["inv_ready"], 1)
                            dve.wait_ge(s["inv_ready"], hd * TT + i + 1)
                            dve.tensor_scalar(probs[i % 2][:, 0:width], probs[i % 2][:, 0:width], inv[:, i:i + 1], None,
                                              ALU.mult).then_inc(s["probs_scaled"], 1)

                        row_max(0)
                        for i in range(1, TT):
                            row_max(i)
                            scale_probs(i - 1)
                        scale_probs(TT - 1)
                        dve.wait_ge(s["pv_done"], hd + 1 + SEED)
                        dve.wait_ge(s["ag_in"], hd * 16 + 16)
                        dve.tensor_tensor(xf[:, bass.ds(g * GROUP + h, 1), :].rearrange("p a b -> p (a b)"),
                                          psO[:, 0:TOK], ag[:], ALU.mult).then_inc(s["gated"], 1)

                dve.wait_ge(s["gated"], (l + 1) * HEADS + SEED)
                dve.wait_ge(s["kv_stored"], 32 * KVH * (l + 1) + SEED)
                dve.memset(aup[:], 0.0).then_inc(s["aup_clear"], 1)
                dve.wait_ge(s["lr_done"], l + 1)
                for slot in range(2):
                    split(slot, 0, occ + IN_PAIRS)
                dve.wait_ge(s["mask_in"], 32 * (l + 1))
                with dve.Fori(0, PAIRS) as pr:
                    gp = pr + l * PAIRS
                    dve.wait_ge(s["g_z"], gp * 2 + 2)
                    dve.tensor_scalar(gm[:], gz[:], 0.0, None, ALU.min).then_inc(s["g_min"], 1)
                    dve.wait_ge(s["g_min"], gp + 1)
                    dve.scalar_tensor_tensor(gz[:].rearrange("p a b -> p (a b)"), gm[:].rearrange("p a b -> p (a b)"), 2.0,
                                             gz[:].rearrange("p a b -> p (a b)"), ALU.mult, ALU.subtract)\
                        .then_inc(s["g_neg"], 1)
                    dve.wait_ge(s["g_ln"], gp + 1)
                    dve.tensor_tensor(gm[:], gm[:], gz[:], ALU.subtract).then_inc(s["g_lf"], 1)
                    dve.wait_ge(s["g_lf"], gp + 1)
                    dve.tensor_tensor_scan(cum[:, 0, :], chunk_keep[:], gm[:, 0, :], 0.0, ALU.mult, ALU.add)\
                        .then_inc(s["g_scan"], 1)
                    dve.tensor_tensor_scan(cum[:, 1, ::-1], chunk_keep[:], gm[:, 1, ::-1], 0.0, ALU.mult, ALU.add)\
                        .then_inc(s["g_scan"], 1)
                    dve.wait_ge(s["g_scan"], gp * 2 + 2)
                    for z in range(2):
                        mid, last = (CH // 2 - 1, CH - 1) if z == 0 else (CH // 2, 0)
                        c = cum[:, z, :].rearrange("p (c t) -> p c t", t=CH)
                        dve.tensor_tensor(gm[:, z, :].rearrange("p (c t) -> p c t", t=CH), c,
                                          c[:, :, mid:mid + 1].to_broadcast([P, NCH, CH]), ALU.subtract)\
                            .then_inc(s["g_mid"], 1)
                        dve.tensor_copy(small[:, z, 0, :], c[:, :, mid]).then_inc(s["g_mid"], 1)
                        dve.tensor_copy(small[:, z, 1, :], c[:, :, last]).then_inc(s["g_mid"], 1)
                    dve.wait_ge(s["g_mid"], gp * 6 + 6)
                    dve.tensor_scalar(gm[:], gm[:], CLAMP, -CLAMP, ALU.min, ALU.max).then_inc(s["g_clamp"], 1)
                    for z in range(2):
                        dve.tensor_tensor(small[:, z, 2, :], small[:, z, 1, :], small[:, z, 0, :], ALU.subtract)\
                            .then_inc(s["g_small"], 1)
                    dve.wait_ge(s["g_factors"], gp * 2 + 2)
                    dve.scalar_tensor_tensor(qt[:], gq[:].unsqueeze(1).to_broadcast([P, 2, TOK]), DK ** -0.5, qt[:],
                                             ALU.mult, ALU.mult).then_inc(s["g_qk"], 1)
                    dve.tensor_tensor(kt_[:], gk[:].unsqueeze(1).to_broadcast([P, 2, TOK]), kt_[:], ALU.mult)\
                        .then_inc(s["g_qk"], 1)
                    dve.wait_ge(s["g_smallx"], gp + 1)
                    dve.wait_ge(s["g_qk"], gp * 2 + 2)
                    for z in range(2):
                        dve.tensor_tensor(gm[:, z, :].rearrange("p (c t) -> p c t", t=CH),
                                          kt_[:, z, :].rearrange("p (c t) -> p c t", t=CH),
                                          small[:, z, 2, :].unsqueeze(2).to_broadcast([P, NCH, CH]), ALU.mult)\
                            .then_inc(s["g_hat"], 1)
                        dve.tensor_tensor(gz[:, z, :].rearrange("p (c t) -> p c t", t=CH),
                                          qt[:, z, :].rearrange("p (c t) -> p c t", t=CH),
                                          small[:, z, 0, :].unsqueeze(2).to_broadcast([P, NCH, CH]), ALU.mult)\
                            .then_inc(s["g_hat"], 1)
                    for i in range(TT):
                        dve.wait_ge(s["g_att"], gp * TT + i + 1)
                        dve.tensor_tensor(att_m[:].rearrange("p h z t -> p h (z t)"),
                                          psP[i % 2][:].rearrange("p (h t) -> p h t", h=2)[:, :, 0:2 * P],
                                          pair_mask[:].rearrange("p h z t -> p h (z t)"), ALU.mult).then_inc(s["g_masked"], 1)
                        dve.wait_ge(s["g_masked"], gp * TT + i + 1)
                        dve.tensor_tensor(att_s[:, i], att_m[:, :, 0], att_m[:, :, 1], ALU.add).then_inc(s["g_summed"], 1)
                        dve.wait_ge(s["g_summed"], gp * TT + i + 1)
                    for n, chunks in enumerate(STEPS):
                        dve.wait_ge(s["g_u"], gp * len(STEPS) + n + 1)
                        dve.wait_ge(s["g_state"], (gp * len(STEPS) + n) * 4 + SEED)
                        for z, ch in enumerate(chunks):
                            at = state_at(z, ch)
                            for hh in range(2):
                                part = slice(hh * DK, (hh + 1) * DK)
                                added = (psT, psO)[n % 2][part, ch % 2 * 512 + hh * DV:][:, 0:DV]
                                if at == DEC_CH + 1:
                                    m = dve.tensor_copy(states[part, z, at + 1, :], added)
                                else:
                                    m = dve.scalar_tensor_tensor(states[part, z, at + 1, :], states[part, z, at, :],
                                                                 small[part, z, 1, ch:ch + 1], added, ALU.mult, ALU.add)
                                m.then_inc(s["g_state"], 1)
                    for hh in range(2):
                        n = gp * 2 + hh
                        dve.wait_ge(s["g_ostat"], n + 1)
                        dve.tensor_scalar(r_a[:], psO[:, 0:TOK], 1.0 / DV, EPS, ALU.mult, ALU.add).then_inc(s["g_ovar"], 1)
                        refine(rstd[:], r_a[:], r_b[:], sq_sum[:], "g_oexp", n + 1, "g_on", n * 3).then_inc(s["g_on"], 1)
                        dve.wait_ge(s["g_on"], n * 3 + 3)
                        dve.scalar_tensor_tensor(stage[hh][:], psP[hh][:, 0:TOK], vecs[:, l, R_GNORM:R_GNORM + 1], rstd[:],
                                                 ALU.mult, ALU.mult).then_inc(s["g_normed"], 1)
                        dve.wait_ge(s["g_normed"], n + 1)
                        dve.tensor_tensor(xf[:, bass.ds(pr * 2 + (KT - GLA_H + hh), 1), :].rearrange("p a b -> p (a b)"),
                                          stage[hh][:], gg[:, hh, :], ALU.mult).then_inc(s["g_out"], 1)

                fence(dve, 3 * l + 3)
                with dve.Fori(0, KT) as k:
                    dve.wait_ge(s["mix_high"], k + l * KT + 1)
                    dve.tensor_tensor(x_low[:, bass.ds(k, 1), :], xf[:, bass.ds(k, 1), :],
                                      x_high[:, bass.ds(k, 1), :].bitcast(F32), ALU.subtract).then_inc(s["mix_split"], 1)
                with dve.Fori(1, OUT_PAIRS) as i:
                    for slot in range(2):
                        split(slot, i, occ + IN_PAIRS)

            fence(dve, 3 * DEPTH + 1)
            dve.wait_ge(s["stat_summed"], DEPTH + 1)
            dve.tensor_scalar(r_a[:], psO[:, 0:TOK], 1.0 / D, EPS, ALU.mult, ALU.add).then_inc(s["stat_var"], 1)
            refine(rstd[:], r_a[:], r_b[:], sq_sum[:], "stat_exp", DEPTH + 1, "stat_rs", 3 * DEPTH).then_inc(s["stat_rs"], 1)
            dve.wait_ge(s["stat_rs"], 3 * DEPTH + 3)
            for k in range(KT):
                dve.scalar_tensor_tensor(xf[:, k, :], xf[:, k, :], head[:, 2 * KT + k:2 * KT + k + 1], rstd[:],
                                         ALU.mult, ALU.mult).then_inc(s["y_scaled"], 1)

        @block.gpsimd
        def _(pool):
            for name in SEEDED:
                pool.sem_inc(s[name], SEED)
            for l in range(DEPTH):
                fence(pool, 3 * l + 1)
                fence(pool, 3 * l + 2)
                pool.memset(cu[:], 0.0).then_inc(s["conv_clear"], 1)
                pool.wait_ge(s["x_saved"], 16 * (l + 1))
                with pool.Fori(0, CONV_T) as j:
                    n = j + l * CONV_T
                    for m, first in enumerate((T_CH, T_CB, T_CC, T_CG)):
                        pool.dma_start(cin[:, m, :], proj_dram[bass.ds(j + first, 1)].rearrange("a p t -> p (a t)"))\
                            .then_inc(s["conv_in"], 16)
                    pool.wait_ge(s["conv_clear"], l + 1)
                    pool.wait_ge(s["conv_in"], n * 64 + 64)
                    for at, part in ((1, slice(0, DEC)), (2 + DEC, slice(DEC, TOK))):
                        pool.tensor_tensor(cu[:, at:at + part.stop - part.start], cin[:, 2, part], cin[:, 0, part], ALU.mult)\
                            .then_inc(s["conv_u"], 1)
                    pool.tensor_tensor(cin[:, 1, :], cin[:, 1, :], cin[:, 3, :], ALU.mult).then_inc(s["conv_u"], 1)
                    pool.wait_ge(s["conv_u"], n * 3 + 3)
                    for tap in range(3):
                        pool.tensor_tensor(ct[tap][:], cu[:, tap:tap + TOK + 1],
                                           vecs[:, l, bass.ds(j + (R_CONV + tap * CONV_T), 1)].to_broadcast([P, TOK + 1]),
                                           ALU.mult).then_inc(s["conv_t"], 1)
                    pool.wait_ge(s["conv_t"], n * 3 + 3)
                    pool.tensor_tensor(ct[0][:], ct[0][:], ct[1][:], ALU.add).then_inc(s["conv_sum"], 1)
                    pool.wait_ge(s["conv_sum"], n * 2 + 1)
                    pool.tensor_tensor(ct[0][:], ct[0][:], ct[2][:], ALU.add).then_inc(s["conv_sum"], 1)
                    pool.wait_ge(s["conv_sum"], n * 2 + 2)
                    for at, part in ((0, slice(0, DEC)), (1 + DEC, slice(DEC, TOK))):
                        pool.tensor_tensor(xf[:, bass.ds(j + HEADS, 1), part].rearrange("p a b -> p (a b)"),
                                           ct[0][:, at:at + part.stop - part.start], cin[:, 1, part], ALU.mult)\
                            .then_inc(s["conv_out"], 1)
                    pool.wait_ge(s["conv_out"], n * 2 + 2)

                fence(pool, 3 * l + 3)
                pool.memset(sq_sum[:], 0.0).then_inc(s["x_acc"], 1)
                occ = l * per_layer
                with pool.Fori(0, OUT_PAIRS) as i:
                    for slot in range(2):
                        n = i * 2 + (l * KT + slot)
                        pool.wait_ge(s[f"taken{slot}"], i + occ + IN_PAIRS + 1 + SEED)
                        pool.wait_ge(s[f"old_in{slot}"], (i + l * OUT_PAIRS) * 16 + 16)
                        pool.tensor_tensor(stage[slot][:], stage[slot][:], old[slot], ALU.add).then_inc(s["x_sum"], 1)
                        pool.wait_ge(s["x_sum"], n + 1)
                        pool.tensor_tensor(xt[slot][:], stage[slot][:], stage[slot][:], ALU.mult).then_inc(s["x_sq"], 1)
                        pool.tensor_copy(xf[:, bass.ds(i * 2 + slot, 1), :].rearrange("p a b -> p (a b)"), stage[slot][:])\
                            .then_inc(s[f"x_new{slot}"], 1)
                        pool.wait_ge(s["x_sq"], n + 1)
                        pool.wait_ge(s["x_acc"], n + l + 1)
                        pool.tensor_tensor(sq_sum[:], sq_sum[:], xt[slot][:], ALU.add).then_inc(s["x_acc"], 1)
            fence(pool, 3 * DEPTH + 1)


_INS = ["x_prompt", "x_sample", "cache_k", "cache_v", "state_gla", "c", "c_ctx", "w_mod", "b_mod", "norm_w", "w_in",
        "q_norm_w", "k_norm_w", "conv_w", "gla_a_up", "gla_a_bias", "gla_norm_w", "w_out", "final_norm_w"]
_OUTS = {"y_prompt": (1, SEQ, D), "y_sample": (1, DEC, D), "new_k": (1, DEPTH, SEQ, KVH, HD),
         "new_v": (1, DEPTH, SEQ, KVH, HD), "new_state": (1, DEPTH, 2, GLA_H, DK, DV)}


def tables():
    f = np.float32
    d = np.arange(HD)
    half = HD // 2
    n_freq = HD // 4
    inv = (f(10000.0) ** (-np.arange(n_freq, dtype=f) / f(n_freq))).astype(f)
    pos = np.arange(DEC)
    where = np.where((d < half)[:, None], (pos // GRID_W)[None, :], (pos % GRID_W)[None, :]).astype(f)
    angle = (where * inv[d % n_freq][:, None]).astype(f)
    rotate = np.zeros((P, P), f)
    for m in range(HD):
        if m % half < n_freq:
            rotate[m + n_freq, m] = -1.0
        else:
            rotate[m - n_freq, m] = 1.0
    a = np.arange(P)
    same = (a[:, None] // CH) == (a[None, :] // CH)
    fwd = same & (a[:, None] <= a[None, :])
    bwd = same & (a[:, None] >= a[None, :])
    mask = np.stack([np.stack([fwd, bwd], 1)] * 2, 1).astype(f)
    keep = np.broadcast_to((np.arange(TOK) % CH != 0).astype(f), (P, TOK))
    return {"ident": np.eye(P, dtype=f), "rotate": rotate, "cos": np.cos(angle).astype(f), "sin": np.sin(angle).astype(f),
            "pair_mask": np.ascontiguousarray(mask), "chunk_keep": np.ascontiguousarray(keep)}


def kernel(**inputs):
    import concourse.bacc as _bacc
    from concourse.bass_utils import run_bass_kernel_spmd as _run

    nc = _bacc.Bacc("TRN2", target_bir_lowering=False, num_devices=1)
    arrays, io = {}, {}
    given = {name: np.ascontiguousarray(inputs[name]) for name in _INS}
    given.update(tables())
    for name, a in given.items():
        arrays[f"in_{name}_dram"] = a
        io[name] = nc.dram_tensor(f"in_{name}_dram", a.shape, mybir.dt.from_np(a.dtype), kind="ExternalInput").ap()
    for name, shape in _OUTS.items():
        io[name] = nc.dram_tensor(f"out_{name}_dram", shape, F32, kind="ExternalOutput").ap()
    backbone(nc, io)
    r = _run(nc, [arrays], core_ids=[0])
    return tuple(r.results[0][f"out_{name}_dram"] for name in _OUTS)
```

```python
from contextlib import ExitStack

import numpy as np

import concourse.bass as bass
from concourse import mybir

F32 = mybir.dt.float32
F32R = mybir.dt.float32r
ALU = mybir.AluOpType
ACT = mybir.ActivationFunctionType
AX = mybir.AxisListType

P = 128
SEQ, DEC, PAST = 128, 512, 128
TOK = DEC + SEQ
TT = TOK // P
DEPTH = 2
D = 2048
KT = D // P
HD = 128
HEADS, KVH = 8, 2
GROUP = HEADS // KVH
KEYS = DEC + PAST
CH = 64
NCH = TOK // CH
DEC_CH = DEC // CH
GLA_H, DK, DV, RANK = 4, 64, 128, 16
PAIRS = GLA_H // 2
TAU = 16.0
GRID_W = 64
EPS = 1e-6
ATT_W, KV_W, CONV_W, GKW, GVW = HEADS * HD, KVH * HD, D // 4, GLA_H * DK, GLA_H * DV
CONV_T = CONV_W // P

SIZES = [ATT_W, KV_W, KV_W, ATT_W, CONV_W, CONV_W, CONV_W, CONV_W, GKW, GKW, GVW, GVW]
T_AQ, T_AK, T_AV, T_AG, T_CH, T_CB, T_CC, T_CG, T_GQ, T_GK, T_GV, T_GG, T_LR = [
    int(x) // P for x in np.cumsum([0] + SIZES)]
RUNS = [(T_AQ, (T_AG - T_AQ) // 2, False), (T_GQ, (T_GG - T_GQ) // 2, False), (T_AG, (T_CH - T_AG) // 2, True),
        (T_GG, (T_LR - T_GG) // 2, True)]
RUN_PAIRS = sum(n for _, n, _ in RUNS)
IN_PAIRS = RUN_PAIRS + HEADS
FENCES = 4
OUT_PAIRS = KT // 2
MOD_T = 3 * KT
MOD_N = 512
MOD_CHUNKS = 3 * D // MOD_N
MOD_STEP = MOD_T // RUN_PAIRS
LR_W = 2 * RANK

R_BMOD, R_NORM, R_Q, R_K = 0, MOD_T, MOD_T + KT, MOD_T + KT + 1
R_CONV = R_K + 1
R_ABIAS = R_CONV + 3 * CONV_T
R_GNORM = R_ABIAS + 2 * PAIRS
ROWS = R_GNORM + 1

HALF = TOK // 2
AT = 512 - HALF
CLAMP = 40.0 * TAU
STATES = DEC_CH + 1 + SEQ // CH + 1


def state_at(z, chunk):
    if chunk < DEC_CH:
        return chunk if z == 0 else DEC_CH - 1 - chunk
    n = chunk - DEC_CH
    return DEC_CH + 1 + (n if z == 0 else SEQ // CH - 1 - n)


STEPS = [(n, DEC_CH - 1 - n) for n in range(DEC_CH - 1)] + [(DEC_CH + n, NCH - 1 - n) for n in range(SEQ // CH)]

NAMES = """rows_in x_in consts_in rows_turned vecs_ready head_ready embed_turned x_taken x_squared x_saved cg_in
cg_silu high_quarter0 high_quarter1 wmod_in0 wmod_in1 wmod_in2 wmod_in3 wmod_used0 wmod_used1 wmod_used2
wmod_used3 mod_row mod_turned mod_taken raw_in0 raw_in1 high0 high1 split0 split1 tile_done0 tile_done1
taken0 taken1 stored0 stored1 phase_over x_split mix_high mix_split stat_summed stat_var stat_ln stat_exp
stat_rs mod_added mod_ready scaled0 scaled1 shifted0 shifted1 x_high0 x_high1 mraw_in0 mraw_in1 mod_step0
mod_step1 mod_half mod_acc mod_summed lr_in lr_split lr_done lr_taken lr_stored old_in0 old_in1 x_new0
x_new1 x_sq x_acc k_in v_in ck_in cv_in q_in ag_in k_sq k_stat k_var k_ln k_exp k_n k_normed k_rot k_r
k_roped kv_turned kv_ready kv_stored q_sq q_scaled q_rot q_r q_roped q_ln q_exp q_n q_rs scored max_step
nm_ready probs_made inv_ready probs_scaled prob_turned pt_copied pv_done gated conv_in conv_clear conv_u
conv_t conv_sum conv_out gla_in aup_clear g_logit g_z g_min g_neg g_ln g_lf g_scan g_mid g_clamp g_factors
g_smallx g_qk g_hat g_turned g_tok g_att g_masked g_summed g_u g_state g_o g_osq g_ostat g_ovar g_oln g_oexp
g_on g_normed g_out g_saved y_scaled y_turned y_taken y_out ones_set x_sum tables_in""".split()


SEED = 1
SEEDED = """conv_out wmod_used0 wmod_used1 wmod_used2 wmod_used3 split0 split1 mod_half mod_acc k_normed kv_turned pv_done q_sq
q_scaled gated g_saved x_new0 x_new1 mod_taken taken0 taken1 pt_copied probs_made g_out g_tok g_ovar
tile_done0 tile_done1 stored0 stored1 k_stat kv_stored q_rot prob_turned x_high0 x_high1 mod_summed g_state
mod_step0 mod_step1""".split()


def backbone(nc, io):
    with ExitStack() as ctx:
        def sb(name, shape, dtype=F32, stack=ctx):
            return stack.enter_context(nc.sbuf_tensor(name, shape, dtype))

        s = {name: ctx.enter_context(nc.semaphore(name)) for name in NAMES}

        proj_dram = nc.dram_tensor("proj_scratch", [T_LR + 1, P, TOK], F32)
        x_dram = nc.dram_tensor("x_scratch", [P, KT, TOK], F32)

        ident = sb("ident", [P, P])
        rotate = sb("rotate", [P, P])
        ones = sb("ones", [P, P])
        rows = sb("rows", [P, P])
        vecs = sb("vecs", [P, DEPTH, ROWS])
        head_rows = sb("head_rows", [3 * KT, P])
        head = sb("head", [P, 3 * KT])
        cond = sb("cond", [P, KT, 2])
        mod_raw = sb("mod_raw", [P, DEPTH, MOD_T, 2])
        mod = sb("mod", [P, MOD_T, 2])
        mod_a = sb("mod_a", [P, KT, 2])
        xf = sb("xf", [P, KT, TOK])
        sq_sum = sb("sq_sum", [P, TOK])
        raw = [sb(f"raw{i}", [P, KT, P]) for i in range(2)]
        high = [sb(f"high{i}", [P, KT, P], F32R) for i in range(2)]
        low = [sb(f"low{i}", [P, KT, P], F32R) for i in range(2)]
        stage = [sb(f"stage{i}", [P, TOK]) for i in range(2)]
        rstd = sb("rstd", [P, TOK])
        r_a = sb("r_a", [P, TOK])
        r_b = sb("r_b", [P, TOK])

        with ExitStack() as proj_space:
            def ps_(name, shape, dtype=F32, stack=proj_space):
                return sb(name, shape, dtype, stack)
            x_high = ps_("x_high", [P, KT, TOK], F32R)
            x_low = ps_("x_low", [P, KT, TOK], F32R)
            with ExitStack() as next_mod:
                mraw = [ps_(f"mraw{i}", [P, KT // 2, MOD_STEP * P], stack=next_mod) for i in range(2)]
                macc = ps_("macc", [P, 2, MOD_STEP * P], stack=next_mod)
            cos, sin = ps_("cos", [P, DEC]), ps_("sin", [P, DEC])
            probs_t = xf[:, HEADS:HEADS + 4, :].rearrange("p a b -> p (a b)").rearrange("p (a b) -> p a b", b=DEC)
            kraw, kn, ksq, vraw = (xf[:, HEADS + 4 + i, :] for i in range(4))
            ck = ps_("ck", [P, P])
            keys = ps_("keys", [P, KEYS + SEQ])
            vals = ps_("vals", [P, TT + 1, P])
            newk = ps_("newk", [P, P])
            qraw, qw, qsq = ps_("qraw", [P, TOK]), ps_("qw", [P, TOK]), ps_("qsq", [P, TOK])
            ag = ps_("ag", [P, TOK])
            t1, t2 = ps_("t1", [P, DEC]), ps_("t2", [P, DEC])
            qr = ps_("qr", [P, DEC])
            qv, qa, qb, qs = (ps_(n, [P, TT]) for n in ("qv", "qa", "qb", "qs"))
            mx_, nm, sums, inv = (ps_(n, [P, TT]) for n in ("mx_", "nm", "sums", "inv"))
            probs = [ps_(f"probs{i}", [P, KEYS]) for i in range(2)]
            probs_p = ps_("probs_p", [P, P])
        xt = [r_a, r_b]
        old = [m[:].rearrange("p k n -> p (k n)")[:, 0:TOK] for m in mraw]
        with ExitStack() as ends:
            xtok = sb("xtok", [P, TT, D], F32, ends)
            with ExitStack() as last:
                ytok = sb("ytok", [P, TT, D], F32, last)
            wmod = [sb(f"wmod{i}", [P, KT // 4, MOD_N], F32, ends) for i in range(4)]
            mod_rows = [sb(f"mod_rows{i}", [2, MOD_N], F32, ends) for i in range(2)]
        with ExitStack() as mixers:
            def mx(name, shape, dtype=F32, stack=mixers):
                return sb(name, shape, dtype, stack)
            cin, cgate = mx("cin", [P, 3, TOK]), mx("cgate", [P, CONV_T, TOK])
            cu = mx("cu", [P, TOK + 3])
            ct = [mx(f"ct{i}", [P, TOK + 1]) for i in range(3)]
            with ExitStack() as gla:
                def gl(name, shape):
                    return mx(name, shape, F32, gla)
                pair_mask, chunk_keep = gl("pair_mask", [P, 2, 2, P]), gl("chunk_keep", [P, TOK])
                gq, gk, lr = gl("gq", [P, TOK]), gl("gk", [P, TOK]), gl("lr", [LR_W, TOK])
                gv, gg = gl("gv", [P, 2, TOK]), gl("gg", [P, 2, TOK])
                aup = gl("aup", [LR_W, 2, P])
                gz, gm, cum = gl("gz", [P, 2, TOK]), gl("gm", [P, 2, TOK]), gl("cum", [P, 2, TOK])
                qt, kt_ = gl("qt", [P, 2, TOK]), gl("kt_", [P, 2, TOK])
                small = gl("small", [P, 2, 3, NCH])
                k_tok = gl("k_tok", [P, 2, TT, P])
                v_tok = gl("v_tok", [P, TT, 2, P])
                att_m, att_s = gl("att_m", [P, 2, 2, P]), gl("att_s", [P, TT, 2, P])
                states = gl("states", [P, 2, STATES, DV])
        psP = [ctx.enter_context(nc.psum_tensor(f"psP{i}", [P, 1024], F32)) for i in range(2)]
        psT = ctx.enter_context(nc.psum_tensor("psT", [P, 1024], F32))
        psO = ctx.enter_context(nc.psum_tensor("psO", [P, 1024], F32))

        per_layer = IN_PAIRS + OUT_PAIRS
        block = ctx.enter_context(nc.Block())

        def fence(eng, n):
            eng.drain().then_inc(s["phase_over"], 1)
            eng.wait_ge(s["phase_over"], 4 * n)

        @block.sync
        def _(sp):
            for name, dst in (("ident", ident[:]), ("rotate", rotate[:])):
                sp.dma_start(dst, io[name]).then_inc(s["consts_in"], 16)
            sp.dma_start(head_rows[0:KT, :], io["c"].rearrange("b (k p) -> (b k) p", p=P)).then_inc(s["rows_in"], 16)
            sp.dma_start(head_rows[KT:2 * KT, :], io["c_ctx"].rearrange("(k p) -> k p", p=P)).then_inc(s["rows_in"], 16)
            sp.dma_start(head_rows[2 * KT:, :], io["final_norm_w"].rearrange("(k p) -> k p", p=P)).then_inc(s["rows_in"], 16)
            for i in range(DEC // P):
                sp.dma_start(xtok[:, i, :], io["x_sample"][0, i * P:(i + 1) * P, :]).then_inc(s["x_in"], 16)
            sp.dma_start(xtok[:, TT - 1, :], io["x_prompt"][0]).then_inc(s["x_in"], 16)
            for l in range(DEPTH):
                sp.wait_ge(s["vecs_ready"], l)
                for at, src in (
                        (R_BMOD, io["b_mod"][l].rearrange("(k p) -> k p", p=P)),
                        (R_NORM, io["norm_w"][l].rearrange("(k p) -> k p", p=P)),
                        (R_Q, io["q_norm_w"][l:l + 1]), (R_K, io["k_norm_w"][l:l + 1]),
                        (R_CONV, io["conv_w"][l].rearrange("t (j p) -> (t j) p", p=P)),
                        (R_ABIAS, io["gla_a_bias"][l].rearrange("z (j p) -> (z j) p", p=P)),
                        (R_GNORM, io["gla_norm_w"][l:l + 1])):
                    sp.dma_start(rows[at:at + src.shape[0], :], src).then_inc(s["rows_in"], 16)
            def weight_pair(w, first, i, occ):
                for slot in range(2):
                    sp.wait_ge(s[f"split{slot}"], occ + i + SEED)
                    sp.dma_start(raw[slot][:], w[:, :, bass.ds((i * 2 + slot) * P + first * P, P)])\
                        .then_inc(s[f"raw_in{slot}"], 16)

            weight_pair(io["w_in"][0].rearrange("(k p) n -> p k n", p=P), 0, 0, 0)
            wm = io["w_mod"][0].rearrange("(k p) n -> p k n", p=P)
            with sp.Fori(0, MOD_CHUNKS) as i:
                for q in range(4):
                    sp.wait_ge(s[f"wmod_used{q}"], i + SEED)
                    sp.dma_start(wmod[q][:], wm[:, q * KT // 4:(q + 1) * KT // 4, bass.ds(i * MOD_N, MOD_N)])\
                        .then_inc(s[f"wmod_in{q}"], 16)

            def mod_weights(l, u):
                nxt = io["w_mod"][l + 1].rearrange("(k p) n -> p k n", p=P)
                for hf, used in enumerate(("mod_half", "mod_acc")):
                    sp.wait_ge(s[used], u + l * RUN_PAIRS + SEED)
                    sp.dma_start(mraw[hf][:], nxt[:, hf * KT // 2:(hf + 1) * KT // 2, bass.ds(u * MOD_STEP * P, MOD_STEP * P)])\
                        .then_inc(s[f"mraw_in{hf}"], 16)

            for l in range(DEPTH):
                occ = l * per_layer
                w_in = io["w_in"][l].rearrange("(k p) n -> p k n", p=P)
                if l > 0:
                    weight_pair(w_in, 0, 0, occ)
                sp.wait_ge(s["phase_over"], 4 * (FENCES * l + 1))
                sp.dma_start(x_dram[:], xf[:]).then_inc(s["x_saved"], 16)
                if l + 1 < DEPTH:
                    mod_weights(l, 0)
                before = 0
                for run, (first, pairs, _) in enumerate(RUNS):
                    with sp.Fori(int(run == 0), pairs) as i:
                        weight_pair(w_in, first, i, occ + before)
                        if l + 1 < DEPTH:
                            mod_weights(l, i + before)
                    before += pairs
                sp.wait_ge(s["split0"], occ + RUN_PAIRS + SEED)
                sp.dma_start(raw[0][:, :, 0:LR_W], w_in[:, :, T_LR * P:T_LR * P + LR_W]).then_inc(s["lr_in"], 16)

                sp.wait_ge(s["phase_over"], 4 * (FENCES * l + 2))
                sp.wait_ge(s["x_saved"], 16 * (l + 1))
                sp.wait_ge(s["lr_split"], 2 * l + 2)
                sp.dma_start(cos[:], io["cos"]).then_inc(s["tables_in"], 16)
                sp.dma_start(sin[:], io["sin"]).then_inc(s["tables_in"], 16)
                with sp.Fori(0, KVH) as g:
                    kv = g + l * KVH
                    hd0 = g * GROUP + l * HEADS
                    sp.wait_ge(s["k_normed"], kv + SEED)
                    sp.dma_start(kraw[:], proj_dram[bass.ds(g + T_AK, 1)].rearrange("a p t -> p (a t)")).then_inc(s["k_in"], 16)
                    sp.wait_ge(s["kv_turned"], kv + SEED)
                    sp.dma_start(vraw[:], proj_dram[bass.ds(g + T_AV, 1)].rearrange("a p t -> p (a t)")).then_inc(s["v_in"], 16)
                    sp.dma_start(ck[:], io["cache_k"][0, l].rearrange("s g d -> s (g d)")[:, bass.ds(g * HD, HD)])\
                        .then_inc(s["ck_in"], 16)
                    with sp.Fori(0, GROUP) as h:
                        hd = h + hd0
                        weight_pair(w_in, T_CH, g * GROUP + h, occ + RUN_PAIRS)
                        sp.wait_ge(s["q_sq"], hd + SEED)
                        sp.wait_ge(s["q_scaled"], hd + SEED)
                        sp.dma_start(qraw[:], proj_dram[bass.ds(g * GROUP + h + T_AQ, 1)].rearrange("a p t -> p (a t)"))\
                            .then_inc(s["q_in"], 16)
                        sp.wait_ge(s["gated"], hd + SEED)
                        sp.dma_start(ag[:], proj_dram[bass.ds(g * GROUP + h + T_AG, 1)].rearrange("a p t -> p (a t)"))\
                            .then_inc(s["ag_in"], 16)
                w_out = io["w_out"][l].rearrange("(k p) n -> p k n", p=P)
                weight_pair(w_out, 0, 0, occ + IN_PAIRS)
                sp.wait_ge(s["phase_over"], 4 * (FENCES * l + 3))
                sp.dma_start(cgate[:], proj_dram[T_CG:T_CG + CONV_T].rearrange("a p t -> p a t")).then_inc(s["cg_in"], 16)
                sp.wait_ge(s["aup_clear"], l + 1)
                sp.dma_start(pair_mask[:], io["pair_mask"]).then_inc(s["tables_in"], 16)
                sp.dma_start(chunk_keep[:], io["chunk_keep"]).then_inc(s["tables_in"], 16)
                with sp.Fori(0, PAIRS) as pr:
                    sp.wait_ge(s["g_saved"], pr * 32 + l * 32 * PAIRS + SEED)
                    sp.dma_start(lr[:], proj_dram[T_LR, 0:LR_W, :]).then_inc(s["gla_in"], 16)
                    for z in range(2):
                        sp.dma_start(aup[z * RANK:(z + 1) * RANK, z, :], io["gla_a_up"][l, z][:, bass.ds(pr * P, P)])\
                            .then_inc(s["gla_in"], 16)
                    sp.dma_start(gq[:], proj_dram[bass.ds(pr + T_GQ, 1)].rearrange("a p t -> p (a t)")).then_inc(s["gla_in"], 16)
                    sp.dma_start(gk[:], proj_dram[bass.ds(pr + T_GK, 1)].rearrange("a p t -> p (a t)")).then_inc(s["gla_in"], 16)
                    sp.dma_start(gv[:], proj_dram[bass.ds(pr * 2 + T_GV, 2)].rearrange("a p t -> p a t")).then_inc(s["gla_in"], 16)
                    sp.dma_start(gg[:], proj_dram[bass.ds(pr * 2 + T_GG, 2)].rearrange("a p t -> p a t")).then_inc(s["gla_in"], 16)
                    for z in range(2):
                        sp.dma_start(states[:, z, 0, :], io["state_gla"][0, l, z].rearrange("h d v -> (h d) v")
                                     [bass.ds(pr * P, P), :]).then_inc(s["gla_in"], 16)
                    for j in range(CONV_T // PAIRS):
                        sp.wait_ge(s["conv_out"], pr * (2 * CONV_T // PAIRS) + 2 * (j + l * CONV_T) + SEED)
                        for m, first in enumerate((T_CH, T_CB, T_CC)):
                            sp.dma_start(cin[:, m, :], proj_dram[bass.ds(pr * (CONV_T // PAIRS) + (j + first), 1)]
                                         .rearrange("a p t -> p (a t)")).then_inc(s["conv_in"], 16)

                def old_pair(i):
                    for slot in range(2):
                        sp.wait_ge(s[f"x_new{slot}"], i + l * OUT_PAIRS + SEED)
                        sp.dma_start(old[slot], x_dram[:, bass.ds(i * 2 + slot, 1), :].rearrange("p a t -> p (a t)"))\
                            .then_inc(s[f"old_in{slot}"], 16)

                sp.wait_ge(s["phase_over"], 4 * (FENCES * l + 4))
                old_pair(0)
                with sp.Fori(1, OUT_PAIRS) as i:
                    weight_pair(w_out, 0, i, occ + IN_PAIRS)
                    old_pair(i)
            for i in range(TT):
                sp.wait_ge(s["y_taken"], KT)
                dst = io["y_sample"][0, i * P:(i + 1) * P, :] if i < TT - 1 else io["y_prompt"][0]
                sp.dma_start(dst, ytok[:, i, :]).then_inc(s["y_out"], 16)
            sp.wait_ge(s["y_out"], 16 * TT)

        @block.tensor
        def _(pe):
            def spread(out, lhsT, rhs, start=True, stop=True):
                pe.matmul(out[:, 0:512], lhsT, rhs[:, 0:512], start=start, stop=stop)
                return pe.matmul(out[:, 512:TOK], lhsT, rhs[:, 512:TOK], start=start, stop=stop)

            pe.wait_ge(s["ones_set"], 1)
            pe.wait_ge(s["consts_in"], 16 * 2)
            pe.wait_ge(s["rows_in"], 16 * 10)
            pe.transpose(psO[:, 0:3 * KT], head_rows[:], ident[0:3 * KT, 0:3 * KT]).then_inc(s["rows_turned"], 1)
            pe.transpose(psT[:, 0:ROWS], rows[0:ROWS, :], ident[0:ROWS, 0:ROWS]).then_inc(s["rows_turned"], 1)
            pe.wait_ge(s["x_in"], 16 * TT)
            for k in range(KT):
                if k >= 2:
                    pe.wait_ge(s["x_taken"], k - 1)
                for i in range(TT):
                    mm = pe.transpose(psP[k % 2][:, i * P:(i + 1) * P], xtok[:, i, k * P:(k + 1) * P], ident[:])
                mm.then_inc(s["embed_turned"], 1)
            for l in range(1, DEPTH):
                pe.wait_ge(s["rows_in"], 16 * (10 + 7 * l))
                pe.wait_ge(s["vecs_ready"], l)
                pe.transpose(psT[:, 0:ROWS], rows[0:ROWS, :], ident[0:ROWS, 0:ROWS]).then_inc(s["rows_turned"], 1)
            pe.wait_ge(s["head_ready"], 1)
            pe.wait_ge(s["vecs_ready"], DEPTH)
            with pe.Fori(0, MOD_CHUNKS // 2) as i:
                for half in range(2):
                    if half == 0:
                        pe.wait_ge(s["mod_taken"], i + SEED)
                    for q in range(4):
                        pe.wait_ge(s[f"wmod_in{q}"], i * 32 + (half * 16 + 16))
                        for k in range(KT // 4):
                            n = q * KT // 4 + k
                            mm = pe.matmul(psT[0:2, half * 512:half * 512 + MOD_N], cond[:, n, :], wmod[q][:, k, :],
                                           start=(n == 0), stop=(n == KT - 1))
                        mm.then_inc(s[f"wmod_used{q}"], 1)
                for half in range(2):
                    pe.wait_ge(s["mod_row"], i * 2 + (half + 1))
                    for j in range(MOD_N // P):
                        at = (half * (MOD_N // P) + j) * 2
                        mm = pe.matmul(psO[:, at:at + 2], mod_rows[half][:, j * P:(j + 1) * P], ident[0:2, 0:2],
                                       start=True, stop=True)
                    mm.then_inc(s["mod_turned"], 1)

            def project(slot, operand=None, done=0):
                out = psP[slot]
                n = 0
                for k in range(KT):
                    if operand and k % 2 == 0:
                        pe.wait_ge(s[operand], done + k + 2)
                    for w, x in ((high, x_high), (high, x_low), (low, x_high)):
                        for half in range(2):
                            mm = pe.matmul(out[:, AT + half * HALF:AT + (half + 1) * HALF], w[slot][:, k, :],
                                           x[:, k, half * HALF:(half + 1) * HALF],
                                           start=(n == 0), stop=(n == 3 * KT - 1))
                        n += 1
                return mm

            def pair(i, occ, operand=None, done=0):
                for slot in range(2):
                    pe.wait_ge(s[f"split{slot}"], i + occ + 1 + SEED)
                    pe.wait_ge(s[f"taken{slot}"], i + occ + SEED)
                    project(slot, operand if slot == 0 else None, done).then_inc(s[f"tile_done{slot}"], 1)

            def project_quarter(slot, quarter, n):
                if quarter == 0:
                    pe.wait_ge(s[f"split{slot}"], n + 1 + SEED)
                    pe.wait_ge(s[f"taken{1 - slot}"], n + slot + SEED)
                for k in range(quarter * KT // 4, (quarter + 1) * KT // 4):
                    for w, x in ((high, x_high), (high, x_low), (low, x_high)):
                        for half in range(2):
                            mm = pe.matmul(psP[0][:, AT + half * HALF:AT + (half + 1) * HALF], w[slot][:, k, :],
                                           x[:, k, half * HALF:(half + 1) * HALF],
                                           start=(k == 0 and w is high and x is x_high),
                                           stop=(k == KT - 1 and w is low))
                if quarter == 3:
                    mm.then_inc(s[f"tile_done{slot}"], 1)

            def mod_sums(l, u):
                pe.wait_ge(s["mod_acc"], u + l * RUN_PAIRS + 1 + SEED)
                pe.wait_ge(s["mod_taken"], u + l * RUN_PAIRS + MOD_CHUNKS // 2 + SEED)
                for n in range(MOD_STEP):
                    for v in range(2):
                        mm = pe.matmul(psT[:, 2 * n + v:2 * n + v + 1], macc[:, v, n * P:(n + 1) * P],
                                       ones[:, 0:1], start=True, stop=True)
                mm.then_inc(s["mod_summed"], 1)

            for l in range(DEPTH):
                occ = l * per_layer
                fence(pe, FENCES * l + 1)
                spread(psO, ones[:], sq_sum).then_inc(s["stat_summed"], 1)
                pair(0, occ, "x_split", KT * l)
                if l + 1 < DEPTH:
                    mod_sums(l, 0)
                before = 0
                for run, (first, pairs, _) in enumerate(RUNS):
                    with pe.Fori(int(run == 0), pairs) as i:
                        pair(i, occ + before)
                        if l + 1 < DEPTH:
                            mod_sums(l, i + before)
                    before += pairs
                pe.wait_ge(s["lr_split"], 2 * l + 2)
                pe.wait_ge(s["taken0"], occ + RUN_PAIRS + SEED)
                project(0).then_inc(s["lr_done"], 1)

                fence(pe, FENCES * l + 2)
                with pe.Fori(0, KVH) as g:
                    kv = g + l * KVH
                    hd0 = g * GROUP + l * HEADS
                    pe.wait_ge(s["k_sq"], kv + 1)
                    pe.wait_ge(s["gated"], hd0 + SEED)
                    spread(psO, ones[:], ksq).then_inc(s["k_stat"], 1)
                    pe.wait_ge(s["k_normed"], kv + 1 + SEED)
                    pe.matmul(psO[:, 0:DEC], rotate[:], kn[:, 0:DEC], start=True, stop=True).then_inc(s["k_rot"], 1)
                    pe.wait_ge(s["v_in"], kv * 16 + 16)
                    pe.wait_ge(s["ck_in"], kv * 16 + 16)
                    pe.wait_ge(s["pt_copied"], hd0 * TT + SEED)
                    pe.transpose(psT[:, 0:P], kn[:, DEC:TOK], ident[:])
                    pe.transpose(psT[:, P:2 * P], ck[:], ident[:])
                    for i in range(TT):
                        mm = pe.transpose(psT[:, (i + 2) * P:(i + 3) * P], vraw[:, i * P:(i + 1) * P], ident[:])
                    mm.then_inc(s["kv_turned"], 1)
                    with pe.Fori(0, GROUP) as h:
                        hd = h + hd0
                        n = g * GROUP + h + (occ + RUN_PAIRS)

                        def score(i):
                            pe.wait_ge(s["probs_made"], hd * TT + i + SEED)
                            if i < TT - 1:
                                q = qr[:, i * P:(i + 1) * P]
                                pe.matmul(psP[1][:, 0:512], q, keys[:, 0:512], start=True, stop=True)
                                mm = pe.matmul(psP[1][:, 512:KEYS], q, keys[:, 512:KEYS], start=True, stop=True)
                            else:
                                mm = pe.matmul(psP[1][:, 0:SEQ], qw[:, DEC:TOK], keys[:, KEYS:KEYS + SEQ],
                                               start=True, stop=True)
                            mm.then_inc(s["scored"], 1)

                        def turn(i):
                            pe.wait_ge(s["probs_scaled"], hd * TT + i + 1)
                            pe.wait_ge(s["pt_copied"], hd * TT + i + SEED)
                            for j in range(KEYS // P if i < TT - 1 else 1):
                                mm = pe.transpose(psT[:, j * P:(j + 1) * P], probs[i % 2][:, j * P:(j + 1) * P], ident[:])
                            mm.then_inc(s["prob_turned"], 1)

                        project_quarter(0, 0, n)
                        pe.wait_ge(s["q_scaled"], hd + 1 + SEED)
                        pe.wait_ge(s["gated"], hd + SEED)
                        pe.matmul(psO[:, 0:DEC], rotate[:], qw[:, 0:DEC], start=True, stop=True)
                        pe.wait_ge(s["q_sq"], hd + 1 + SEED)
                        for i in range(TT):
                            mm = pe.matmul(psO[:, TOK + i:TOK + i + 1], qsq[:, i * P:(i + 1) * P], ones[:, 0:1],
                                           start=True, stop=True)
                        mm.then_inc(s["q_rot"], 1)
                        project_quarter(0, 1, n)
                        pe.wait_ge(s["q_roped"], hd + 1)
                        pe.wait_ge(s["kv_ready"], kv * 3 + 3)
                        pe.wait_ge(s["k_roped"], kv + 1)
                        pe.wait_ge(s["cv_in"], kv * 16 + 16)
                        score(0)
                        for i in range(1, TT):
                            project_quarter((i + 1) // 4, (i + 1) % 4, n)
                            score(i)
                            turn(i - 1)
                        project_quarter(1, 2, n)
                        turn(TT - 1)
                        project_quarter(1, 3, n)
                        pe.wait_ge(s["pt_copied"], hd * TT + TT + SEED)
                        for j in range(TT):
                            pe.matmul(psO[:, 0:DEC], vals[:, j if j < TT - 1 else TT, :], probs_t[:, j, :],
                                      start=(j == 0), stop=(j == TT - 1))
                        pe.matmul(psO[:, DEC:TOK], vals[:, TT - 1, :], probs_p[:], start=True, stop=True)\
                            .then_inc(s["pv_done"], 1)

                fence(pe, FENCES * l + 3)
                with pe.Fori(0, PAIRS) as pr:
                    gp = pr + l * PAIRS
                    pe.wait_ge(s["gla_in"], gp * 16 * 9 + 16 * 9)
                    pe.wait_ge(s["g_out"], gp * 2 + SEED)
                    for z in range(2):
                        spread(psP[z], aup[:, z, :], lr).then_inc(s["g_logit"], 1)
                    for hh in range(2):
                        pe.wait_ge(s["g_tok"], gp * 4 + hh + SEED)
                        for i in range(TT):
                            mm = pe.transpose(psT[:, i * P:(i + 1) * P], gv[:, hh, i * P:(i + 1) * P], ident[:])
                        mm.then_inc(s["g_turned"], 1)
                    pe.wait_ge(s["g_qk"], gp * 2 + 2)
                    for i in range(TT):
                        if i >= 2:
                            pe.wait_ge(s["g_masked"], gp * TT + i - 1)
                        else:
                            pe.wait_ge(s["g_z"], gp * 2 + 2)
                        for z in range(2):
                            for hh in range(2):
                                part = slice(hh * DK, (hh + 1) * DK)
                                mm = pe.matmul(psP[i % 2][:, hh * 512 + z * P:][:, 0:P],
                                               kt_[part, z, i * P:(i + 1) * P], qt[part, z, i * P:(i + 1) * P],
                                               start=True, stop=True)
                        mm.then_inc(s["g_att"], 1)
                    pe.wait_ge(s["g_hat"], gp * 4 + 4)
                    for z in range(2):
                        pe.wait_ge(s["g_tok"], gp * 4 + 2 + z + SEED)
                        for i in range(TT):
                            mm = pe.transpose(psT[:, i * P:(i + 1) * P], gm[:, z, i * P:(i + 1) * P], ident[:])
                        mm.then_inc(s["g_turned"], 1)
                    pe.wait_ge(s["g_tok"], gp * 4 + 4 + SEED)
                    for n, (fwd, bwd) in enumerate(STEPS):
                        if n >= 2:
                            pe.wait_ge(s["g_state"], (gp * len(STEPS) + n - 1) * 4 + SEED)
                        for z, ch in enumerate((fwd, bwd)):
                            part = slice(ch % 2 * CH, (ch % 2 + 1) * CH)
                            mm = pe.matmul((psT, psO)[n % 2][:, ch % 2 * 512:][:, 0:256], k_tok[part, z, ch // 2, :],
                                           v_tok[part, ch // 2, :, :].rearrange("p a b -> p (a b)"),
                                           start=True, stop=True)
                        mm.then_inc(s["g_u"], 1)
                    pe.wait_ge(s["g_state"], (gp + 1) * len(STEPS) * 4 + SEED)
                    pe.wait_ge(s["g_summed"], gp * TT + TT)
                    for hh in range(2):
                        part = slice(hh * DK, (hh + 1) * DK)
                        for i in range(TT):
                            parts = [(z, ch) for ch in (2 * i, 2 * i + 1) for z in range(2)
                                     if state_at(z, ch) != DEC_CH + 1]
                            pe.matmul(psP[hh][:, i * P:(i + 1) * P], v_tok[:, i, hh, :], att_s[:, i, hh, :],
                                      start=True, stop=False)
                            for n, (z, ch) in enumerate(parts):
                                mm = pe.matmul(psP[hh][:, ch * CH:(ch + 1) * CH], states[part, z, state_at(z, ch), :],
                                               gz[part, z, ch * CH:(ch + 1) * CH],
                                               start=False, stop=(n == len(parts) - 1))
                        mm.then_inc(s["g_o"], 1)
                    for hh in range(2):
                        pe.wait_ge(s["g_osq"], gp * 2 + hh + 1)
                        pe.wait_ge(s["g_ovar"], gp * 2 + hh + SEED)
                        spread(psO, ones[:], stage[hh]).then_inc(s["g_ostat"], 1)

                fence(pe, FENCES * l + 4)
                pair(0, occ + IN_PAIRS, "mix_split", KT * l)
                with pe.Fori(1, OUT_PAIRS) as i:
                    pair(i, occ + IN_PAIRS)

            fence(pe, FENCES * DEPTH + 1)
            spread(psO, ones[:], sq_sum).then_inc(s["stat_summed"], 1)
            for k in range(KT):
                pe.wait_ge(s["y_scaled"], k + 1)
                if k >= 2:
                    pe.wait_ge(s["y_taken"], k - 1)
                for i in range(TT):
                    mm = pe.transpose(psP[k % 2][:, i * P:(i + 1) * P], xf[:, k, i * P:(i + 1) * P], ident[:])
                mm.then_inc(s["y_turned"], 1)

        @block.scalar
        def _(act):
            act.wait_ge(s["rows_turned"], 1)
            act.activation(head[:], psO[:, 0:3 * KT], ACT.Copy).then_inc(s["head_ready"], 1)
            act.wait_ge(s["head_ready"], 1)
            act.activation(cond[:].rearrange("p k v -> p v k"), head[:, 0:2 * KT].rearrange("p (v k) -> p v k", v=2),
                           ACT.Silu).then_inc(s["head_ready"], 1)
            act.wait_ge(s["rows_turned"], 2)
            act.activation(vecs[:, 0, :], psT[:, 0:ROWS], ACT.Copy).then_inc(s["vecs_ready"], 1)
            for k in range(KT):
                act.wait_ge(s["embed_turned"], k + 1)
                act.activation(xf[:, k, :], psP[k % 2][:, 0:TOK], ACT.Copy).then_inc(s["x_taken"], 1)
            for l in range(1, DEPTH):
                act.wait_ge(s["rows_turned"], l + 2)
                act.activation(vecs[:, l, :], psT[:, 0:ROWS], ACT.Copy).then_inc(s["vecs_ready"], 1)
            with act.Fori(0, MOD_CHUNKS // 2) as i:
                for half in range(2):
                    act.wait_ge(s["wmod_used3"], i * 2 + (half + 1 + SEED))
                    act.activation(mod_rows[half][:], psT[0:2, half * 512:half * 512 + MOD_N], ACT.Copy)\
                        .then_inc(s["mod_row"], 1)
                act.wait_ge(s["mod_turned"], i * 2 + 2)
                act.activation(mod_raw[:, 0, bass.ds(i * (2 * MOD_N // P), 2 * MOD_N // P), :].rearrange("p a b -> p (a b)"),
                               psO[:, 0:4 * MOD_N // P], ACT.Copy).then_inc(s["mod_taken"], 1)

            def ln_exp(src, tmp, out, ready, n, ln_sem, exp_sem):
                act.wait_ge(s[ready], n + (SEED if ready in SEEDED else 0))
                act.activation(tmp, src, ACT.Ln).then_inc(s[ln_sem], 1)
                act.wait_ge(s[ln_sem], n)
                act.activation(out, tmp, ACT.Exp, scale=-0.5).then_inc(s[exp_sem], 1)

            for l in range(DEPTH):
                occ = l * per_layer
                fence(act, FENCES * l + 1)
                ln_exp(r_a[:], rstd[:], r_b[:], "stat_var", l + 1, "stat_ln", "stat_exp")
                act.wait_ge(s["mod_ready"], l + 1)
                with act.Fori(0, KT // 2) as i:
                    for slot in range(2):
                        act.wait_ge(s[f"scaled{slot}"], i + l * KT // 2 + 1)
                        for v, part in ((0, slice(0, DEC)), (1, slice(DEC, TOK))):
                            a = act.activation(stage[slot][:, part], xt[slot][:, part], ACT.Identity,
                                               bias=mod[:, bass.ds(i * 2 + slot, 1), v:v + 1].rearrange("p a b -> p (a b)"),
                                               scale=mod_a[:, bass.ds(i * 2 + slot, 1), v:v + 1].rearrange("p a b -> p (a b)"))
                            a.then_inc(s[f"shifted{slot}"], 1)
                        act.wait_ge(s[f"shifted{slot}"], i * 2 + l * KT + 2)
                        act.activation(x_high[:, bass.ds(i * 2 + slot, 1), :], stage[slot][:], ACT.Copy)\
                            .then_inc(s[f"x_high{slot}"], 1)
                before = 0
                act.wait_ge(s["x_split"], KT * (l + 1))
                for run, (first, pairs, gate) in enumerate(RUNS):
                    with act.Fori(0, pairs) as i:
                        for slot in range(2):
                            act.wait_ge(s[f"stored{slot}"], i * 16 + (before + l * IN_PAIRS) * 16 + SEED)
                            act.wait_ge(s[f"tile_done{slot}"], i + occ + before + 1 + SEED)
                            act.activation(stage[slot][:], psP[slot][:, AT:AT + TOK], ACT.Silu if gate else ACT.Copy)\
                                .then_inc(s[f"taken{slot}"], 1)
                            act.wait_ge(s[f"taken{slot}"], i + occ + before + 1 + SEED)
                            act.dma_start(proj_dram[bass.ds(i * 2 + (slot + first), 1)].rearrange("a p t -> p (a t)"),
                                          stage[slot][:]).then_inc(s[f"stored{slot}"], 16)
                        if l + 1 < DEPTH:
                            act.wait_ge(s["mod_summed"], i + before + l * RUN_PAIRS + 1 + SEED)
                            act.activation(mod_raw[:, l + 1, bass.ds((i + before) * MOD_STEP, MOD_STEP), :].rearrange("p a b -> p (a b)"),
                                           psT[:, 0:2 * MOD_STEP], ACT.Copy).then_inc(s["mod_taken"], 1)
                    before += pairs
                for slot in range(2):
                    act.wait_ge(s[f"stored{slot}"], 16 * (IN_PAIRS * l + RUN_PAIRS) + SEED)
                act.wait_ge(s["lr_done"], l + 1)
                act.activation(stage[0][0:LR_W, :], psP[0][0:LR_W, AT:AT + TOK], ACT.Copy).then_inc(s["lr_taken"], 1)
                act.wait_ge(s["lr_taken"], l + 1)
                act.dma_start(proj_dram[T_LR, 0:LR_W, :], stage[0][0:LR_W, :]).then_inc(s["lr_stored"], 16)
                act.wait_ge(s["lr_stored"], 16 * (l + 1))

                fence(act, FENCES * l + 2)
                with act.Fori(0, KVH) as g:
                    kv = g + l * KVH
                    hd0 = g * GROUP + l * HEADS
                    act.wait_ge(s["k_in"], kv * 16 + 16)
                    act.wait_ge(s["k_stat"], kv + SEED)
                    act.activation(ksq[:], kraw[:], ACT.Square).then_inc(s["k_sq"], 1)
                    ln_exp(r_a[:], rstd[:], r_b[:], "k_var", kv + 1, "k_ln", "k_exp")
                    act.wait_ge(s["kv_turned"], kv + 1 + SEED)
                    act.wait_ge(s["kv_stored"], kv * 32 + SEED)
                    act.activation(newk[:], psT[:, 0:P], ACT.Copy).then_inc(s["kv_ready"], 1)
                    act.activation(keys[:, DEC:KEYS], psT[:, P:2 * P], ACT.Copy).then_inc(s["kv_ready"], 1)
                    act.activation(vals[:, 0:TT, :], psT[:, 2 * P:2 * P + TOK].rearrange("p (a b) -> p a b", b=P), ACT.Copy)\
                        .then_inc(s["kv_ready"], 1)
                    act.wait_ge(s["kv_ready"], kv * 3 + 3)
                    act.dma_start(vals[:, TT, :], io["cache_v"][0, l].rearrange("s g d -> s (g d)")[:, bass.ds(g * HD, HD)])\
                        .then_inc(s["cv_in"], 16)
                    act.dma_start(io["new_k"][0, l].rearrange("s g d -> s (g d)")[:, bass.ds(g * HD, HD)], newk[:])\
                        .then_inc(s["kv_stored"], 16)
                    act.dma_start(io["new_v"][0, l].rearrange("s g d -> s (g d)")[:, bass.ds(g * HD, HD)],
                                  vals[:, TT - 1, :]).then_inc(s["kv_stored"], 16)
                    with act.Fori(0, GROUP) as h:
                        hd = h + hd0
                        act.wait_ge(s["q_in"], hd * 16 + 16)
                        act.wait_ge(s["q_rot"], hd + SEED)
                        act.activation(qsq[:], qraw[:], ACT.Square).then_inc(s["q_sq"], 1)
                        ln_exp(qv[:], qb[:], qa[:], "q_roped", hd + 1, "q_ln", "q_exp")
                        act.wait_ge(s["q_rs"], hd + 1)

                        def prob(i):
                            width = KEYS if i < TT - 1 else SEQ
                            act.wait_ge(s["nm_ready"], hd * TT + i + 1)
                            act.wait_ge(s["prob_turned"], hd * TT + max(i - 1, 0) + SEED)
                            act.activation(probs[i % 2][:, 0:width], psP[1][:, 0:width], ACT.Exp,
                                           bias=nm[:, i:i + 1], scale=qs[:, i:i + 1], accum_out=sums[:, i:i + 1])\
                                .then_inc(s["probs_made"], 1)

                        def take(i):
                            act.wait_ge(s["prob_turned"], hd * TT + i + 1 + SEED)
                            if i < TT - 1:
                                act.activation(probs_t[:, :, i * P:(i + 1) * P],
                                               psT[:, 0:KEYS].rearrange("p (a b) -> p a b", b=P), ACT.Copy)\
                                    .then_inc(s["pt_copied"], 1)
                            else:
                                act.activation(probs_p[:], psT[:, 0:P], ACT.Copy).then_inc(s["pt_copied"], 1)

                        def take_tile(slot):
                            n = g * GROUP + h
                            act.wait_ge(s[f"stored{slot}"], n * 16 + (RUN_PAIRS + l * IN_PAIRS) * 16 + SEED)
                            act.wait_ge(s[f"tile_done{slot}"], n + occ + RUN_PAIRS + 1 + SEED)
                            act.activation(stage[slot][:], psP[0][:, AT:AT + TOK], ACT.Copy).then_inc(s[f"taken{slot}"], 1)
                            act.wait_ge(s[f"taken{slot}"], n + occ + RUN_PAIRS + 1 + SEED)
                            act.dma_start(proj_dram[bass.ds(n * 2 + (slot + T_CH), 1)].rearrange("a p t -> p (a t)"),
                                          stage[slot][:]).then_inc(s[f"stored{slot}"], 16)

                        prob(0)
                        prob(1)
                        act.wait_ge(s["pv_done"], hd + SEED)
                        take(0)
                        take_tile(0)
                        for i in range(2, TT):
                            prob(i)
                            take(i - 1)
                        take(TT - 1)
                        take_tile(1)
                for slot in range(2):
                    act.wait_ge(s[f"stored{slot}"], 16 * IN_PAIRS * (l + 1) + SEED)
                act.wait_ge(s["kv_stored"], 32 * KVH * (l + 1) + SEED)

                fence(act, FENCES * l + 3)
                act.wait_ge(s["cg_in"], 16 * (l + 1))
                act.activation(cgate[:], cgate[:], ACT.Silu).then_inc(s["cg_silu"], 1)
                with act.Fori(0, PAIRS) as pr:
                    gp = pr + l * PAIRS
                    act.wait_ge(s["g_out"], gp * 2 + SEED)
                    for z in range(2):
                        act.wait_ge(s["g_logit"], gp * 2 + z + 1)
                        act.activation(gz[:, z, :], psP[z][:, 0:TOK], ACT.Identity,
                                       bias=vecs[:, l, bass.ds(pr + (R_ABIAS + z * PAIRS), 1)]).then_inc(s["g_z"], 1)
                    for hh in range(2):
                        act.wait_ge(s["g_turned"], gp * 4 + hh + 1)
                        act.activation(v_tok[:, :, hh, :], psT[:, 0:TOK].rearrange("p (a b) -> p a b", b=P), ACT.Copy)\
                            .then_inc(s["g_tok"], 1)
                    act.wait_ge(s["g_neg"], gp + 1)
                    act.activation(cum[:], gz[:], ACT.Exp).then_inc(s["g_ln"], 1)
                    act.wait_ge(s["g_ln"], gp * 2 + 1)
                    act.activation(gz[:], cum[:], ACT.Ln, bias=1.0).then_inc(s["g_ln"], 1)
                    act.wait_ge(s["g_clamp"], gp + 1)
                    act.activation(qt[:], gm[:], ACT.Exp, scale=1 / TAU).then_inc(s["g_factors"], 1)
                    act.activation(kt_[:], gm[:], ACT.Exp, scale=-1 / TAU).then_inc(s["g_factors"], 1)
                    act.wait_ge(s["g_mid"], gp * 8 + 8)
                    act.activation(small[:], small[:], ACT.Exp, scale=1 / TAU).then_inc(s["g_smallx"], 1)
                    for z in range(2):
                        act.wait_ge(s["g_turned"], gp * 4 + 3 + z)
                        act.activation(k_tok[:, z, :, :], psT[:, 0:TOK].rearrange("p (a b) -> p a b", b=P), ACT.Copy)\
                            .then_inc(s["g_tok"], 1)
                    for hh in range(2):
                        act.wait_ge(s["g_o"], gp * 2 + hh + 1)
                        act.activation(stage[hh][:], psP[hh][:, 0:TOK], ACT.Square).then_inc(s["g_osq"], 1)
                    for hh in range(2):
                        ln_exp(r_a[:], rstd[:], r_b[:], "g_ovar", gp * 2 + hh + 1, "g_oln", "g_oexp")
                    act.wait_ge(s["g_out"], gp * 2 + 2 + SEED)
                    for z in range(2):
                        act.dma_start(io["new_state"][0, l, z].rearrange("h d v -> (h d) v")[bass.ds(pr * P, P), :],
                                      states[:, z, STATES - 1, :]).then_inc(s["g_saved"], 16)
                act.wait_ge(s["g_saved"], 32 * PAIRS * (l + 1) + SEED)

                fence(act, FENCES * l + 4)
                with act.Fori(0, KT) as k:
                    act.activation(x_high[:, bass.ds(k, 1), :], xf[:, bass.ds(k, 1), :], ACT.Copy)\
                        .then_inc(s["mix_high"], 1)
                with act.Fori(0, OUT_PAIRS) as i:
                    for slot in range(2):
                        act.wait_ge(s[f"x_new{slot}"], i + l * OUT_PAIRS + SEED)
                        act.wait_ge(s[f"tile_done{slot}"], i + occ + IN_PAIRS + 1 + SEED)
                        for v, part in ((0, slice(0, DEC)), (1, slice(DEC, TOK))):
                            a = act.activation(stage[slot][:, part], psP[slot][:, AT:AT + TOK][:, part], ACT.Identity,
                                               scale=mod[:, bass.ds(i * 2 + (slot + 2 * KT), 1), v:v + 1]
                                               .rearrange("p a b -> p (a b)"))
                        a.then_inc(s[f"taken{slot}"], 1)

            fence(act, FENCES * DEPTH + 1)
            ln_exp(r_a[:], rstd[:], r_b[:], "stat_var", DEPTH + 1, "stat_ln", "stat_exp")
            for k in range(KT):
                act.wait_ge(s["y_turned"], k + 1)
                act.activation(ytok[:, :, k * P:(k + 1) * P], psP[k % 2][:, 0:TOK].rearrange("p (a b) -> p a b", b=P),
                               ACT.Copy).then_inc(s["y_taken"], 1)

        @block.vector
        def _(dve):
            dve.memset(ones[:], 1.0).then_inc(s["ones_set"], 1)
            for k in range(KT):
                dve.wait_ge(s["x_taken"], k + 1)
                if k == 0:
                    dve.tensor_tensor(sq_sum[:], xf[:, k, :], xf[:, k, :], ALU.mult).then_inc(s["x_squared"], 1)
                    continue
                dve.wait_ge(s["x_squared"], 2 * k - 1)
                dve.tensor_tensor(r_a[:], xf[:, k, :], xf[:, k, :], ALU.mult).then_inc(s["x_squared"], 1)
                dve.wait_ge(s["x_squared"], 2 * k)
                dve.tensor_tensor(sq_sum[:], sq_sum[:], r_a[:], ALU.add).then_inc(s["x_squared"], 1)

            def refine(out, v, r0, tmp, exp_sem, n, step_sem, base, scale=None):
                dve.wait_ge(s[exp_sem], n)
                dve.scalar_tensor_tensor(tmp, r0, -0.5, r0, ALU.mult, ALU.mult).then_inc(s[step_sem], 1)
                dve.wait_ge(s[step_sem], base + 1)
                dve.tensor_tensor(tmp, tmp, v, ALU.mult).then_inc(s[step_sem], 1)
                dve.wait_ge(s[step_sem], base + 2)
                return dve.scalar_tensor_tensor(out, tmp, 1.5, r0, ALU.add, ALU.mult)

            def split(slot, i, occ, whole):
                dve.wait_ge(s[f"raw_in{slot}"], (i + occ) * 16 + 16)
                dve.wait_ge(s[f"tile_done{slot}"], i + occ + SEED)
                dve.tensor_copy(high[slot][:], raw[slot][:]).then_inc(s[f"high{slot}"], 1)
                dve.wait_ge(s[f"high{slot}"], i + whole + 1)
                dve.tensor_tensor(low[slot][:], raw[slot][:], high[slot][:].bitcast(F32), ALU.subtract)\
                    .then_inc(s[f"split{slot}"], 1)

            def split_quarter(slot, quarter, n, quarters):
                if quarter == 0:
                    dve.wait_ge(s[f"raw_in{slot}"], n * 16 + 16)
                    dve.wait_ge(s[f"tile_done{slot}"], n + SEED)
                part = slice(quarter * KT // 4, (quarter + 1) * KT // 4)
                dve.tensor_copy(high[slot][:, part], raw[slot][:, part]).then_inc(s[f"high_quarter{slot}"], 1)
                dve.wait_ge(s[f"high_quarter{slot}"], quarters * 4 + quarter + 1)
                m = dve.tensor_tensor(low[slot][:, part], raw[slot][:, part], high[slot][:, part].bitcast(F32), ALU.subtract)
                if quarter == 3:
                    m.then_inc(s[f"split{slot}"], 1)

            def mod_tiles(u):
                dve.wait_ge(s["mod_summed"], u + SEED)
                for n in range(KT):
                    hf, k = n // (KT // 2), n % (KT // 2)
                    if k == 0:
                        dve.wait_ge(s[f"mraw_in{hf}"], u * 16 + 16)
                    for v in range(2):
                        c = cond[:, n, v:v + 1]
                        if n == 0:
                            m = dve.tensor_scalar(macc[:, v, :], mraw[hf][:, k, :], c, None, ALU.mult)
                        else:
                            if v == 0:
                                dve.wait_ge(s["mod_step0"], u * (KT - 1) + n + SEED)
                            elif n == KT // 2:
                                dve.wait_ge(s["mod_half"], u + 1 + SEED)
                            else:
                                dve.wait_ge(s["mod_step1"], u * (KT - 2) + (n if n < KT // 2 else n - 1) + SEED)
                            m = dve.scalar_tensor_tensor(macc[:, v, :], mraw[hf][:, k, :], c,
                                                         macc[:, v, :], ALU.mult, ALU.add)
                        if v == 0 and n < KT - 1:
                            m.then_inc(s["mod_step0"], 1)
                        elif v == 1 and n == KT // 2 - 1:
                            m.then_inc(s["mod_half"], 1)
                        elif v == 1 and n == KT - 1:
                            m.then_inc(s["mod_acc"], 1)
                        elif v == 1:
                            m.then_inc(s["mod_step1"], 1)

            for l in range(DEPTH):
                occ = l * per_layer
                whole = l * (RUN_PAIRS + OUT_PAIRS)
                split(0, 0, occ, whole)
                fence(dve, FENCES * l + 1)
                dve.wait_ge(s["mod_taken"], MOD_CHUNKS // 2 + l * RUN_PAIRS + SEED)
                dve.wait_ge(s["vecs_ready"], DEPTH)
                dve.tensor_tensor(mod[:], mod_raw[:, l], vecs[:, l, R_BMOD:R_BMOD + MOD_T].unsqueeze(2)
                                  .to_broadcast([P, MOD_T, 2]), ALU.add).then_inc(s["mod_added"], 1)
                dve.wait_ge(s["mod_added"], l + 1)
                dve.scalar_tensor_tensor(mod_a[:], mod[:, KT:2 * KT, :], 1.0, vecs[:, l, R_NORM:R_NORM + KT].unsqueeze(2)
                                         .to_broadcast([P, KT, 2]), ALU.add, ALU.mult).then_inc(s["mod_ready"], 1)
                dve.wait_ge(s["stat_summed"], l + 1)
                dve.tensor_scalar(r_a[:], psO[:, 0:TOK], 1.0 / D, EPS, ALU.mult, ALU.add).then_inc(s["stat_var"], 1)
                refine(rstd[:], r_a[:], r_b[:], sq_sum[:], "stat_exp", l + 1, "stat_rs", 3 * l)\
                    .then_inc(s["stat_rs"], 1)
                dve.wait_ge(s["stat_rs"], 3 * l + 3)
                with dve.Fori(0, KT // 2) as i:
                    n = i + l * KT // 2
                    for slot in range(2):
                        dve.wait_ge(s[f"x_high{slot}"], n + SEED)
                        dve.tensor_tensor(xt[slot][:], xf[:, bass.ds(i * 2 + slot, 1), :].rearrange("p a b -> p (a b)"),
                                          rstd[:], ALU.mult).then_inc(s[f"scaled{slot}"], 1)
                    for slot in range(2):
                        dve.wait_ge(s[f"x_high{slot}"], n + 1 + SEED)
                        dve.tensor_tensor(x_low[:, bass.ds(i * 2 + slot, 1), :].rearrange("p a b -> p (a b)"), stage[slot][:],
                                          x_high[:, bass.ds(i * 2 + slot, 1), :].rearrange("p a b -> p (a b)").bitcast(F32),
                                          ALU.subtract).then_inc(s["x_split"], 1)
                split(1, 0, occ, whole)
                if l + 1 < DEPTH:
                    mod_tiles(l * RUN_PAIRS)
                before = 0
                for run, (first, pairs, _) in enumerate(RUNS):
                    with dve.Fori(int(run == 0), pairs) as i:
                        for slot in range(2):
                            split(slot, i, occ + before, whole + before)
                        if l + 1 < DEPTH:
                            mod_tiles(i + (before + l * RUN_PAIRS))
                    before += pairs
                dve.wait_ge(s["lr_in"], 16 * (l + 1))
                dve.wait_ge(s["tile_done0"], occ + RUN_PAIRS + SEED)
                dve.tensor_copy(high[0][:, :, 0:LR_W], raw[0][:, :, 0:LR_W]).then_inc(s["lr_split"], 1)
                dve.wait_ge(s["lr_split"], 2 * l + 1)
                dve.tensor_tensor(low[0][:, :, 0:LR_W], raw[0][:, :, 0:LR_W], high[0][:, :, 0:LR_W].bitcast(F32),
                                  ALU.subtract).then_inc(s["lr_split"], 1)

                fence(dve, FENCES * l + 2)
                dve.wait_ge(s["x_saved"], 16 * (l + 1))
                dve.wait_ge(s["lr_done"], l + 1)
                split(0, 0, occ + RUN_PAIRS, whole + RUN_PAIRS)
                dve.wait_ge(s["tables_in"], 64 * l + 32)
                with dve.Fori(0, KVH) as g:
                    kv = g + l * KVH
                    hd0 = g * GROUP + l * HEADS
                    dve.wait_ge(s["k_stat"], kv + 1 + SEED)
                    dve.tensor_scalar(r_a[:], psO[:, 0:TOK], 1.0 / HD, EPS, ALU.mult, ALU.add).then_inc(s["k_var"], 1)
                    refine(rstd[:], r_a[:], r_b[:], ksq[:], "k_exp", kv + 1, "k_n", kv * 3).then_inc(s["k_n"], 1)
                    dve.wait_ge(s["k_n"], kv * 3 + 3)
                    dve.wait_ge(s["kv_turned"], kv + SEED)
                    dve.scalar_tensor_tensor(kn[:], kraw[:], vecs[:, l, R_K:R_K + 1], rstd[:], ALU.mult, ALU.mult)\
                        .then_inc(s["k_normed"], 1)
                    dve.wait_ge(s["k_rot"], kv + 1)
                    dve.tensor_tensor(t2[:], psO[:, 0:DEC], sin[:], ALU.mult).then_inc(s["k_r"], 1)
                    dve.wait_ge(s["k_normed"], kv + 1 + SEED)
                    dve.tensor_tensor(t1[:], kn[:, 0:DEC], cos[:], ALU.mult).then_inc(s["k_r"], 1)
                    dve.tensor_copy(keys[:, KEYS:], kn[:, DEC:TOK]).then_inc(s["k_r"], 1)
                    dve.wait_ge(s["k_r"], kv * 3 + 3)
                    dve.tensor_tensor(keys[:, 0:DEC], t1[:], t2[:], ALU.add).then_inc(s["k_roped"], 1)
                    with dve.Fori(0, GROUP) as h:
                        hd = h + hd0
                        n = g * GROUP + h + (occ + RUN_PAIRS)
                        dve.wait_ge(s["q_in"], hd * 16 + 16)
                        dve.tensor_scalar(qw[:], qraw[:], vecs[:, l, R_Q:R_Q + 1], None, ALU.mult).then_inc(s["q_scaled"], 1)
                        dve.wait_ge(s["q_scaled"], hd + 1 + SEED)
                        dve.tensor_tensor(t1[:], qw[:, 0:DEC], cos[:], ALU.mult).then_inc(s["q_r"], 1)
                        split_quarter(1, 0, n, hd)
                        dve.wait_ge(s["q_rot"], hd + 1 + SEED)
                        dve.tensor_tensor(t2[:], psO[:, 0:DEC], sin[:], ALU.mult).then_inc(s["q_r"], 1)
                        dve.tensor_scalar(qv[:], psO[:, TOK:TOK + TT], 1.0 / HD, EPS, ALU.mult, ALU.add)\
                            .then_inc(s["q_r"], 1)
                        dve.wait_ge(s["q_r"], hd * 3 + 3)
                        dve.tensor_tensor(qr[:], t1[:], t2[:], ALU.add).then_inc(s["q_roped"], 1)
                        split_quarter(1, 1, n, hd)
                        refine(inv[:], qv[:], qa[:], mx_[:], "q_exp", hd + 1, "q_n", hd * 3).then_inc(s["q_n"], 1)
                        dve.wait_ge(s["q_n"], hd * 3 + 3)
                        dve.tensor_scalar(qs[:], inv[:], HD ** -0.5, None, ALU.mult).then_inc(s["q_rs"], 1)
                        dve.wait_ge(s["q_rs"], hd + 1)

                        def row_max(i):
                            width = KEYS if i < TT - 1 else SEQ
                            dve.wait_ge(s["scored"], hd * TT + i + 1)
                            dve.tensor_reduce(mx_[:, i:i + 1], psP[1][:, 0:width], AX.X, ALU.max)\
                                .then_inc(s["max_step"], 1)
                            dve.wait_ge(s["max_step"], hd * TT + i + 1)
                            dve.tensor_scalar(nm[:, i:i + 1], mx_[:, i:i + 1], qs[:, i:i + 1], -1.0, ALU.mult, ALU.mult)\
                                .then_inc(s["nm_ready"], 1)

                        def scale_probs(i):
                            width = KEYS if i < TT - 1 else SEQ
                            dve.wait_ge(s["probs_made"], hd * TT + i + 1 + SEED)
                            dve.reciprocal(inv[:, i:i + 1], sums[:, i:i + 1]).then_inc(s["inv_ready"], 1)
                            dve.wait_ge(s["inv_ready"], hd * TT + i + 1)
                            dve.tensor_scalar(probs[i % 2][:, 0:width], probs[i % 2][:, 0:width], inv[:, i:i + 1], None,
                                              ALU.mult).then_inc(s["probs_scaled"], 1)

                        for i in range(TT):
                            row_max(i)
                            if i < 2:
                                split_quarter(1, i + 2, n, hd)
                            else:
                                split_quarter(0, i - 2, n + 1, hd)
                            scale_probs(i)
                        split_quarter(0, 3, n + 1, hd)
                        dve.wait_ge(s["pv_done"], hd + 1 + SEED)
                        dve.wait_ge(s["ag_in"], hd * 16 + 16)
                        dve.tensor_tensor(xf[:, bass.ds(g * GROUP + h, 1), :].rearrange("p a b -> p (a b)"),
                                          psO[:, 0:TOK], ag[:], ALU.mult).then_inc(s["gated"], 1)

                fence(dve, FENCES * l + 3)
                dve.memset(aup[:], 0.0).then_inc(s["aup_clear"], 1)
                split(1, 0, occ + IN_PAIRS, whole + RUN_PAIRS)
                dve.wait_ge(s["tables_in"], 64 * l + 64)
                with dve.Fori(0, PAIRS) as pr:
                    gp = pr + l * PAIRS
                    dve.wait_ge(s["g_z"], gp * 2 + 2)
                    dve.tensor_scalar(gm[:], gz[:], 0.0, None, ALU.min).then_inc(s["g_min"], 1)
                    dve.wait_ge(s["g_min"], gp + 1)
                    dve.scalar_tensor_tensor(gz[:].rearrange("p a b -> p (a b)"), gm[:].rearrange("p a b -> p (a b)"), 2.0,
                                             gz[:].rearrange("p a b -> p (a b)"), ALU.mult, ALU.subtract)\
                        .then_inc(s["g_neg"], 1)
                    dve.wait_ge(s["g_ln"], gp * 2 + 2)
                    dve.tensor_tensor(gm[:], gm[:], gz[:], ALU.subtract).then_inc(s["g_lf"], 1)
                    dve.wait_ge(s["g_lf"], gp + 1)
                    dve.tensor_tensor_scan(cum[:, 0, :], chunk_keep[:], gm[:, 0, :], 0.0, ALU.mult, ALU.add)\
                        .then_inc(s["g_scan"], 1)
                    dve.tensor_tensor_scan(cum[:, 1, ::-1], chunk_keep[:], gm[:, 1, ::-1], 0.0, ALU.mult, ALU.add)\
                        .then_inc(s["g_scan"], 1)
                    dve.wait_ge(s["g_scan"], gp * 2 + 2)
                    for z in range(2):
                        mid, last = (CH // 2 - 1, CH - 1) if z == 0 else (CH // 2, 0)
                        c = cum[:, z, :].rearrange("p (c t) -> p c t", t=CH)
                        dve.tensor_tensor(gm[:, z, :].rearrange("p (c t) -> p c t", t=CH), c,
                                          c[:, :, mid:mid + 1].to_broadcast([P, NCH, CH]), ALU.subtract)\
                            .then_inc(s["g_mid"], 1)
                        dve.tensor_copy(small[:, z, 0, :], c[:, :, mid]).then_inc(s["g_mid"], 1)
                        dve.tensor_copy(small[:, z, 1, :], c[:, :, last]).then_inc(s["g_mid"], 1)
                    dve.wait_ge(s["g_mid"], gp * 8 + 6)
                    dve.tensor_scalar(gm[:], gm[:], CLAMP, -CLAMP, ALU.min, ALU.max).then_inc(s["g_clamp"], 1)
                    for z in range(2):
                        dve.tensor_tensor(small[:, z, 2, :], small[:, z, 1, :], small[:, z, 0, :], ALU.subtract)\
                            .then_inc(s["g_mid"], 1)
                    dve.wait_ge(s["g_factors"], gp * 2 + 2)
                    dve.scalar_tensor_tensor(qt[:], gq[:].unsqueeze(1).to_broadcast([P, 2, TOK]), DK ** -0.5, qt[:],
                                             ALU.mult, ALU.mult).then_inc(s["g_qk"], 1)
                    dve.tensor_tensor(kt_[:], gk[:].unsqueeze(1).to_broadcast([P, 2, TOK]), kt_[:], ALU.mult)\
                        .then_inc(s["g_qk"], 1)
                    dve.wait_ge(s["g_smallx"], gp + 1)
                    dve.wait_ge(s["g_qk"], gp * 2 + 2)
                    for z in range(2):
                        dve.tensor_tensor(gm[:, z, :].rearrange("p (c t) -> p c t", t=CH),
                                          kt_[:, z, :].rearrange("p (c t) -> p c t", t=CH),
                                          small[:, z, 2, :].unsqueeze(2).to_broadcast([P, NCH, CH]), ALU.mult)\
                            .then_inc(s["g_hat"], 1)
                        dve.tensor_tensor(gz[:, z, :].rearrange("p (c t) -> p c t", t=CH),
                                          qt[:, z, :].rearrange("p (c t) -> p c t", t=CH),
                                          small[:, z, 0, :].unsqueeze(2).to_broadcast([P, NCH, CH]), ALU.mult)\
                            .then_inc(s["g_hat"], 1)
                    for i in range(TT):
                        dve.wait_ge(s["g_att"], gp * TT + i + 1)
                        dve.tensor_tensor(att_m[:].rearrange("p h z t -> p h (z t)"),
                                          psP[i % 2][:].rearrange("p (h t) -> p h t", h=2)[:, :, 0:2 * P],
                                          pair_mask[:].rearrange("p h z t -> p h (z t)"), ALU.mult).then_inc(s["g_masked"], 1)
                        dve.wait_ge(s["g_masked"], gp * TT + i + 1)
                        dve.tensor_tensor(att_s[:, i], att_m[:, :, 0], att_m[:, :, 1], ALU.add).then_inc(s["g_summed"], 1)
                        dve.wait_ge(s["g_summed"], gp * TT + i + 1)
                    for n, chunks in enumerate(STEPS):
                        dve.wait_ge(s["g_u"], gp * len(STEPS) + n + 1)
                        dve.wait_ge(s["g_state"], (gp * len(STEPS) + n) * 4 + SEED)
                        for z, ch in enumerate(chunks):
                            at = state_at(z, ch)
                            for hh in range(2):
                                part = slice(hh * DK, (hh + 1) * DK)
                                added = (psT, psO)[n % 2][part, ch % 2 * 512 + hh * DV:][:, 0:DV]
                                if at == DEC_CH + 1:
                                    m = dve.tensor_copy(states[part, z, at + 1, :], added)
                                else:
                                    m = dve.scalar_tensor_tensor(states[part, z, at + 1, :], states[part, z, at, :],
                                                                 small[part, z, 1, ch:ch + 1], added, ALU.mult, ALU.add)
                                m.then_inc(s["g_state"], 1)
                    for hh in range(2):
                        n = gp * 2 + hh
                        dve.wait_ge(s["g_ostat"], n + 1)
                        dve.tensor_scalar(r_a[:], psO[:, 0:TOK], 1.0 / DV, EPS, ALU.mult, ALU.add).then_inc(s["g_ovar"], 1)
                        refine(rstd[:], r_a[:], r_b[:], sq_sum[:], "g_oexp", n + 1, "g_on", n * 3).then_inc(s["g_on"], 1)
                        dve.wait_ge(s["g_on"], n * 3 + 3)
                        dve.scalar_tensor_tensor(stage[hh][:], psP[hh][:, 0:TOK], vecs[:, l, R_GNORM:R_GNORM + 1], rstd[:],
                                                 ALU.mult, ALU.mult).then_inc(s["g_normed"], 1)
                        dve.wait_ge(s["g_normed"], n + 1)
                        dve.tensor_tensor(xf[:, bass.ds(pr * 2 + (KT - GLA_H + hh), 1), :].rearrange("p a b -> p (a b)"),
                                          stage[hh][:], gg[:, hh, :], ALU.mult).then_inc(s["g_out"], 1)

                fence(dve, FENCES * l + 4)
                with dve.Fori(0, KT) as k:
                    dve.wait_ge(s["mix_high"], k + l * KT + 1)
                    dve.tensor_tensor(x_low[:, bass.ds(k, 1), :], xf[:, bass.ds(k, 1), :],
                                      x_high[:, bass.ds(k, 1), :].bitcast(F32), ALU.subtract).then_inc(s["mix_split"], 1)
                with dve.Fori(1, OUT_PAIRS) as i:
                    for slot in range(2):
                        split(slot, i, occ + IN_PAIRS, whole + RUN_PAIRS)

            fence(dve, FENCES * DEPTH + 1)
            dve.wait_ge(s["stat_summed"], DEPTH + 1)
            dve.tensor_scalar(r_a[:], psO[:, 0:TOK], 1.0 / D, EPS, ALU.mult, ALU.add).then_inc(s["stat_var"], 1)
            refine(rstd[:], r_a[:], r_b[:], sq_sum[:], "stat_exp", DEPTH + 1, "stat_rs", 3 * DEPTH).then_inc(s["stat_rs"], 1)
            dve.wait_ge(s["stat_rs"], 3 * DEPTH + 3)
            for k in range(KT):
                dve.scalar_tensor_tensor(xf[:, k, :], xf[:, k, :], head[:, 2 * KT + k:2 * KT + k + 1], rstd[:],
                                         ALU.mult, ALU.mult).then_inc(s["y_scaled"], 1)

        @block.gpsimd
        def _(pool):
            for name in SEEDED:
                pool.sem_inc(s[name], SEED)
            for l in range(DEPTH):
                fence(pool, FENCES * l + 1)
                fence(pool, FENCES * l + 2)
                fence(pool, FENCES * l + 3)
                pool.memset(cu[:], 0.0).then_inc(s["conv_clear"], 1)
                pool.wait_ge(s["x_saved"], 16 * (l + 1))
                pool.wait_ge(s["cg_silu"], l + 1)
                with pool.Fori(0, CONV_T) as j:
                    n = j + l * CONV_T
                    pool.wait_ge(s["conv_clear"], l + 1)
                    pool.wait_ge(s["conv_in"], n * 48 + 48)
                    for at, part in ((1, slice(0, DEC)), (2 + DEC, slice(DEC, TOK))):
                        pool.tensor_tensor(cu[:, at:at + part.stop - part.start], cin[:, 2, part], cin[:, 0, part], ALU.mult)\
                            .then_inc(s["conv_u"], 1)
                    pool.tensor_tensor(cin[:, 1, :], cin[:, 1, :],
                                       cgate[:, bass.ds(j, 1), :].rearrange("p a b -> p (a b)"), ALU.mult).then_inc(s["conv_u"], 1)
                    pool.wait_ge(s["conv_u"], n * 3 + 3)
                    for tap in range(3):
                        pool.tensor_tensor(ct[tap][:], cu[:, tap:tap + TOK + 1],
                                           vecs[:, l, bass.ds(j + (R_CONV + tap * CONV_T), 1)].to_broadcast([P, TOK + 1]),
                                           ALU.mult).then_inc(s["conv_t"], 1)
                    pool.wait_ge(s["conv_t"], n * 3 + 3)
                    pool.tensor_tensor(ct[0][:], ct[0][:], ct[1][:], ALU.add).then_inc(s["conv_sum"], 1)
                    pool.wait_ge(s["conv_sum"], n * 2 + 1)
                    pool.tensor_tensor(ct[0][:], ct[0][:], ct[2][:], ALU.add).then_inc(s["conv_sum"], 1)
                    pool.wait_ge(s["conv_sum"], n * 2 + 2)
                    for at, part in ((0, slice(0, DEC)), (1 + DEC, slice(DEC, TOK))):
                        pool.tensor_tensor(xf[:, bass.ds(j + HEADS, 1), part].rearrange("p a b -> p (a b)"),
                                           ct[0][:, at:at + part.stop - part.start], cin[:, 1, part], ALU.mult)\
                            .then_inc(s["conv_out"], 1)
                    pool.wait_ge(s["conv_out"], n * 2 + 2 + SEED)

                fence(pool, FENCES * l + 4)
                pool.memset(sq_sum[:], 0.0).then_inc(s["x_acc"], 1)
                occ = l * per_layer
                with pool.Fori(0, OUT_PAIRS) as i:
                    for slot in range(2):
                        n = i * 2 + (l * KT + slot)
                        pool.wait_ge(s[f"taken{slot}"], i + occ + IN_PAIRS + 1 + SEED)
                        pool.wait_ge(s[f"old_in{slot}"], (i + l * OUT_PAIRS) * 16 + 16)
                        pool.tensor_tensor(stage[slot][:], stage[slot][:], old[slot], ALU.add).then_inc(s["x_sum"], 1)
                        pool.wait_ge(s["x_sum"], n + 1)
                        pool.tensor_tensor(xt[slot][:], stage[slot][:], stage[slot][:], ALU.mult).then_inc(s["x_sq"], 1)
                        pool.tensor_copy(xf[:, bass.ds(i * 2 + slot, 1), :].rearrange("p a b -> p (a b)"), stage[slot][:])\
                            .then_inc(s[f"x_new{slot}"], 1)
                        pool.wait_ge(s["x_sq"], n + 1)
                        pool.wait_ge(s["x_acc"], n + l + 1)
                        pool.tensor_tensor(sq_sum[:], sq_sum[:], xt[slot][:], ALU.add).then_inc(s["x_acc"], 1)
            fence(pool, FENCES * DEPTH + 1)


_INS = ["x_prompt", "x_sample", "cache_k", "cache_v", "state_gla", "c", "c_ctx", "w_mod", "b_mod", "norm_w", "w_in",
        "q_norm_w", "k_norm_w", "conv_w", "gla_a_up", "gla_a_bias", "gla_norm_w", "w_out", "final_norm_w"]
_OUTS = {"y_prompt": (1, SEQ, D), "y_sample": (1, DEC, D), "new_k": (1, DEPTH, SEQ, KVH, HD),
         "new_v": (1, DEPTH, SEQ, KVH, HD), "new_state": (1, DEPTH, 2, GLA_H, DK, DV)}


def tables():
    f = np.float32
    d = np.arange(HD)
    half = HD // 2
    n_freq = HD // 4
    inv = (f(10000.0) ** (-np.arange(n_freq, dtype=f) / f(n_freq))).astype(f)
    pos = np.arange(DEC)
    where = np.where((d < half)[:, None], (pos // GRID_W)[None, :], (pos % GRID_W)[None, :]).astype(f)
    angle = (where * inv[d % n_freq][:, None]).astype(f)
    rotate = np.zeros((P, P), f)
    for m in range(HD):
        if m % half < n_freq:
            rotate[m + n_freq, m] = -1.0
        else:
            rotate[m - n_freq, m] = 1.0
    a = np.arange(P)
    same = (a[:, None] // CH) == (a[None, :] // CH)
    fwd = same & (a[:, None] <= a[None, :])
    bwd = same & (a[:, None] >= a[None, :])
    mask = np.stack([np.stack([fwd, bwd], 1)] * 2, 1).astype(f)
    keep = np.broadcast_to((np.arange(TOK) % CH != 0).astype(f), (P, TOK))
    return {"ident": np.eye(P, dtype=f), "rotate": rotate, "cos": np.cos(angle).astype(f), "sin": np.sin(angle).astype(f),
            "pair_mask": np.ascontiguousarray(mask), "chunk_keep": np.ascontiguousarray(keep)}


def kernel(**inputs):
    import concourse.bacc as _bacc
    from concourse.bass_utils import run_bass_kernel_spmd as _run

    nc = _bacc.Bacc("TRN2", target_bir_lowering=False, num_devices=1, dynamic_dma_scratch_size=1024)
    arrays, io = {}, {}
    given = {name: np.ascontiguousarray(inputs[name]) for name in _INS}
    given.update(tables())
    for name, a in given.items():
        arrays[f"in_{name}_dram"] = a
        io[name] = nc.dram_tensor(f"in_{name}_dram", a.shape, mybir.dt.from_np(a.dtype), kind="ExternalInput").ap()
    for name, shape in _OUTS.items():
        io[name] = nc.dram_tensor(f"out_{name}_dram", shape, F32, kind="ExternalOutput").ap()
    backbone(nc, io)
    r = _run(nc, [arrays], core_ids=[0])
    return tuple(r.results[0][f"out_{name}_dram"] for name in _OUTS)
```

```python
from contextlib import ExitStack

import numpy as np

import concourse.bass as bass
from concourse import mybir

F32 = mybir.dt.float32
F32R = mybir.dt.float32r
ALU = mybir.AluOpType
ACT = mybir.ActivationFunctionType
AX = mybir.AxisListType

P = 128
SEQ, DEC, PAST = 128, 512, 128
TOK = DEC + SEQ
TT = TOK // P
DEPTH = 2
D = 2048
KT = D // P
HD = 128
HEADS, KVH = 8, 2
GROUP = HEADS // KVH
KEYS = DEC + PAST
CH = 64
NCH = TOK // CH
DEC_CH = DEC // CH
GLA_H, DK, DV, RANK = 4, 64, 128, 16
PAIRS = GLA_H // 2
TAU = 16.0
GRID_W = 64
EPS = 1e-6
ATT_W, KV_W, CONV_W, GKW, GVW = HEADS * HD, KVH * HD, D // 4, GLA_H * DK, GLA_H * DV
CONV_T = CONV_W // P

SIZES = [ATT_W, KV_W, KV_W, ATT_W, CONV_W, CONV_W, CONV_W, CONV_W, GKW, GKW, GVW, GVW]
T_AQ, T_AK, T_AV, T_AG, T_CH, T_CB, T_CC, T_CG, T_GQ, T_GK, T_GV, T_GG, T_LR = [
    int(x) // P for x in np.cumsum([0] + SIZES)]
RUNS = [(T_AQ, (T_AG - T_AQ) // 2, False), (T_GQ, (T_GG - T_GQ) // 2, False), (T_AG, (T_CH - T_AG) // 2, True),
        (T_GG, (T_LR - T_GG) // 2, True)]
RUN_PAIRS = sum(n for _, n, _ in RUNS)
IN_PAIRS = RUN_PAIRS + HEADS
FENCES = 4
OUT_PAIRS = KT // 2
HALF_K = KT // 2
assert HEADS == HALF_K
MOD_T = 3 * KT
MOD_N = 512
MOD_CHUNKS = 2 * D // MOD_N
MOD_BEFORE = MOD_CHUNKS // 4
GATE_STEP, NEXT_STEP = KT // RUN_PAIRS, 2 * KT // RUN_PAIRS
MOD_STEP = GATE_STEP + NEXT_STEP


def mod_step(l):
    return MOD_STEP if l + 1 < DEPTH else GATE_STEP


FILL = KT // PAIRS
LR_W = 2 * RANK

R_BMOD, R_NORM, R_Q, R_K = 0, MOD_T, MOD_T + KT, MOD_T + KT + 1
R_CONV = R_K + 1
R_ABIAS = R_CONV + 3 * CONV_T
R_GNORM = R_ABIAS + 2 * PAIRS
ROWS = R_GNORM + 1

HALF = TOK // 2
AT = 512 - HALF
CLAMP = 40.0 * TAU
STATES = DEC_CH + 1 + SEQ // CH + 1


def state_at(z, chunk):
    if chunk < DEC_CH:
        return chunk if z == 0 else DEC_CH - 1 - chunk
    n = chunk - DEC_CH
    return DEC_CH + 1 + (n if z == 0 else SEQ // CH - 1 - n)


STEPS = [(n, DEC_CH - 1 - n) for n in range(DEC_CH - 1)] + [(DEC_CH + n, NCH - 1 - n) for n in range(SEQ // CH)]

NAMES = """gla_lr_in x_part0 x_part1 rows_in x_in consts_in rows_turned vecs_ready head_ready embed_turned x_taken x_squared
x_saved cg_in cg_silu high_quarter0 high_quarter1 wmod_in0 wmod_in1 wmod_in2 wmod_in3 wmod_used0 wmod_used1
wmod_used2 wmod_used3 mod_row mod_turned mod_taken raw_in0 raw_in1 high0 high1 split0 split1 tile_done0
tile_done1 taken0 taken1 stored0 stored1 phase_over x_split mix_high mix_split stat_summed stat_var stat_ln
stat_exp stat_rs mod_added mod_ready scaled0 scaled1 shifted0 shifted1 x_high0 x_high1 mraw_in0 mraw_in1
mod_step0 mod_step1 mod_half mod_acc mod_summed lr_in lr_split lr_done lr_taken lr_stored old_in0 old_in1
x_sq x_acc k_in v_in ck_in cv_in q_in ag_in k_sq k_stat k_var k_ln k_exp k_n k_normed k_rot k_r k_roped
kv_turned kv_ready kv_stored q_sq q_scaled q_rot q_r q_roped q_ln q_exp q_n q_rs scored max_step nm_ready
probs_made inv_ready probs_scaled prob_turned pt_copied pv_done gated conv_in conv_clear conv_u conv_t
conv_sum conv_out gla_in aup_clear g_logit g_z g_min g_neg g_ln g_lf g_scan g_mid g_clamp g_factors g_smallx
g_qk g_hat g_turned g_tok g_att g_masked g_summed g_u g_state g_o g_osq g_ostat g_ovar g_oln g_oexp g_on
g_normed g_out g_saved y_scaled y_turned y_taken y_out ones_set tables_in""".split()


SEED = 1
SEEDED = """x_split x_acc x_part0 x_part1 conv_out wmod_used0 wmod_used1 wmod_used2 wmod_used3 split0 split1 mod_half mod_acc
k_normed kv_turned pv_done q_sq q_scaled gated g_saved mod_taken taken0 taken1 pt_copied probs_made g_out
g_tok g_ovar tile_done0 tile_done1 stored0 stored1 k_stat kv_stored q_rot prob_turned x_high0 x_high1
mod_summed g_state mod_step0 mod_step1""".split()


def backbone(nc, io):
    with ExitStack() as ctx:
        def sb(name, shape, dtype=F32, stack=ctx):
            return stack.enter_context(nc.sbuf_tensor(name, shape, dtype))

        s = {name: ctx.enter_context(nc.semaphore(name)) for name in NAMES}

        proj_dram = nc.dram_tensor("proj_scratch", [T_LR + 1, P, TOK], F32)
        x_dram = nc.dram_tensor("x_scratch", [P, KT, TOK], F32)

        ident = sb("ident", [P, P])
        rotate = sb("rotate", [P, P])
        ones = sb("ones", [P, P])
        rows = [sb(f"rows{l}", [P, P]) for l in range(DEPTH)]
        vecs = sb("vecs", [P, DEPTH, ROWS])
        head_rows = sb("head_rows", [3 * KT, P])
        head = sb("head", [P, 3 * KT])
        cond = sb("cond", [P, KT, 2])
        mod_raw = sb("mod_raw", [P, DEPTH, MOD_T, 2])
        mod = sb("mod", [P, MOD_T, 2])
        mod_a = sb("mod_a", [P, KT, 2])
        xf = sb("xf", [P, KT, TOK])
        sq_sum = sb("sq_sum", [P, TOK])
        raw = [sb(f"raw{i}", [P, KT, P]) for i in range(2)]
        high = [sb(f"high{i}", [P, KT, P], F32R) for i in range(2)]
        low = [sb(f"low{i}", [P, KT, P], F32R) for i in range(2)]
        stage = [sb(f"stage{i}", [P, TOK]) for i in range(2)]
        rstd = sb("rstd", [P, TOK])
        r_a = sb("r_a", [P, TOK])
        r_b = sb("r_b", [P, TOK])

        with ExitStack() as proj_space:
            def ps_(name, shape, dtype=F32, stack=proj_space):
                return sb(name, shape, dtype, stack)
            x_high = ps_("x_high", [P, KT, TOK], F32R)
            operand_high, operand_low = x_high[:, 0:HALF_K], x_high[:, HALF_K:]
            with ExitStack() as mixers:
                def mx(name, shape, dtype=F32, stack=mixers):
                    return sb(name, shape, dtype, stack)
                old = [mx(f"old{i}", [P, TOK]) for i in range(2)]
                cgate, cin = xf[:, 0:CONV_T, :], xf[:, CONV_T:CONV_T + 3, :]
                cu = mx("cu", [P, TOK + 3])
                ct = [mx(f"ct{i}", [P, TOK + 1]) for i in range(2)]
                pair_mask, chunk_keep = mx("pair_mask", [P, 2 * P]), xf[:, CONV_T + 3, :]
                gqk, gv, gg = mx("gqk", [P, 2, TOK]), mx("gv", [P, 2, TOK]), mx("gg", [P, 2, TOK])
                gq, gk = gqk[:, 0, :], gqk[:, 1, :]
                lr_att = mx("lr_att", [P, TOK])
                lr = lr_att[0:LR_W, :]
                aup = mx("aup", [LR_W, 2, P])
                gz, gm, cum = mx("gz", [P, 2, TOK]), mx("gm", [P, 2, TOK]), mx("cum", [P, 2, TOK])
                qt, kt_ = mx("qt", [P, 2, TOK]), mx("kt_", [P, 2, TOK])
                small = mx("small", [P, 2, 3, NCH])
                v_tok = mx("v_tok", [P, TT, 2, P])
                k_tok = gv[:].rearrange("p z (i t) -> p z i t", t=P)
                att_m = lr_att[:, 0:4 * P].rearrange("p (h z t) -> p h z t", h=2, z=2)
                att_s = gqk[:].rearrange("p a t -> p (a t)").rearrange("p (i h t) -> p i h t", h=2, t=P)
                states = mx("states", [P, 2, STATES, DV])
            x_low = ps_("x_low", [P, KT, TOK], F32R)
            with ExitStack() as next_mod:
                mraw = [ps_(f"mraw{i}", [P, KT // 2, MOD_STEP * P], stack=next_mod) for i in range(2)]
                macc = ps_("macc", [P, 2, MOD_STEP * P], stack=next_mod)
            cos, sin = ps_("cos", [P, DEC]), ps_("sin", [P, DEC])
            probs_t = xf[:, HEADS:HEADS + 4, :].rearrange("p a b -> p (a b)").rearrange("p (a b) -> p a b", b=DEC)
            kraw, kn, ksq, vraw = (xf[:, HEADS + 4 + i, :] for i in range(4))
            ck = ps_("ck", [P, P])
            keys = ps_("keys", [P, KEYS + SEQ])
            vals = ps_("vals", [P, TT + 1, P])
            newk = ps_("newk", [P, P])
            qraw, qw, qsq = ps_("qraw", [P, TOK]), ps_("qw", [P, TOK]), ps_("qsq", [P, TOK])
            ag = ps_("ag", [P, TOK])
            t1, t2 = ps_("t1", [P, DEC]), ps_("t2", [P, DEC])
            qr = ps_("qr", [P, DEC])
            qv, qa, qb, qs = (ps_(n, [P, TT]) for n in ("qv", "qa", "qb", "qs"))
            mx_, nm, sums, inv = (ps_(n, [P, TT]) for n in ("mx_", "nm", "sums", "inv"))
            probs = [ps_(f"probs{i}", [P, KEYS]) for i in range(2)]
            probs_p = ps_("probs_p", [P, P])
        xt = [r_a, r_b]
        with ExitStack() as ends:
            xtok = sb("xtok", [P, TT, D], F32, ends)
            with ExitStack() as last:
                ytok = sb("ytok", [P, TT, D], F32, last)
            wmod = [sb(f"wmod{i}", [P, KT // 4, MOD_N], F32, ends) for i in range(4)]
            mod_rows = [sb(f"mod_rows{i}", [2, MOD_N], F32, ends) for i in range(2)]
        psP = [ctx.enter_context(nc.psum_tensor(f"psP{i}", [P, 1024], F32)) for i in range(2)]
        psT = ctx.enter_context(nc.psum_tensor("psT", [P, 1024], F32))
        psO = ctx.enter_context(nc.psum_tensor("psO", [P, 1024], F32))

        FIRST, SECOND = IN_PAIRS, IN_PAIRS + OUT_PAIRS
        per_layer = IN_PAIRS + 2 * OUT_PAIRS
        block = ctx.enter_context(nc.Block())

        def fill_place(f):
            return psT if f in (1, 3, 7) else psO

        def arrive(eng):
            eng.drain().then_inc(s["phase_over"], 1)

        def fence(eng, n):
            arrive(eng)
            eng.wait_ge(s["phase_over"], 4 * n)

        @block.sync
        def _(sp):
            for name, dst in (("ident", ident[:]), ("rotate", rotate[:])):
                sp.dma_start(dst, io[name]).then_inc(s["consts_in"], 16)
            sp.dma_start(head_rows[0:KT, :], io["c"].rearrange("b (k p) -> (b k) p", p=P)).then_inc(s["consts_in"], 16)
            sp.dma_start(head_rows[KT:2 * KT, :], io["c_ctx"].rearrange("(k p) -> k p", p=P)).then_inc(s["consts_in"], 16)
            sp.dma_start(head_rows[2 * KT:, :], io["final_norm_w"].rearrange("(k p) -> k p", p=P)).then_inc(s["consts_in"], 16)
            def weight_pair(w, first, i, occ):
                for slot in range(2):
                    sp.wait_ge(s[f"split{slot}"], occ + i + SEED)
                    sp.dma_start(raw[slot][:], w[:, :, bass.ds((i * 2 + slot) * P + first * P, P)])\
                        .then_inc(s[f"raw_in{slot}"], 16)

            wm = io["w_mod"][0].rearrange("(k p) n -> p k n", p=P)
            with sp.Fori(0, MOD_CHUNKS) as i:
                for q in range(4):
                    sp.wait_ge(s[f"wmod_used{q}"], i + SEED)
                    sp.dma_start(wmod[q][:], wm[:, q * KT // 4:(q + 1) * KT // 4, bass.ds(i * MOD_N, MOD_N)])\
                        .then_inc(s[f"wmod_in{q}"], 16)

            weight_pair(io["w_in"][0].rearrange("(k p) n -> p k n", p=P), 0, 0, 0)

            def mod_weights(l, u):
                own = io["w_mod"][l].rearrange("(k p) n -> p k n", p=P)
                for hf, used in enumerate(("mod_half", "mod_acc")):
                    part = slice(hf * KT // 2, (hf + 1) * KT // 2)
                    sp.wait_ge(s[used], u + l * RUN_PAIRS + SEED)
                    sp.dma_start(mraw[hf][:, :, 0:GATE_STEP * P], own[:, part, bass.ds(u * (GATE_STEP * P) + 2 * D, GATE_STEP * P)])\
                        .then_inc(s[f"mraw_in{hf}"], 16)
                    if l + 1 < DEPTH:
                        nxt = io["w_mod"][l + 1].rearrange("(k p) n -> p k n", p=P)
                        sp.dma_start(mraw[hf][:, :, GATE_STEP * P:], nxt[:, part, bass.ds(u * (NEXT_STEP * P), NEXT_STEP * P)])\
                            .then_inc(s[f"mraw_in{hf}"], 16)

            for l in range(DEPTH):
                occ = l * per_layer
                w_in = io["w_in"][l].rearrange("(k p) n -> p k n", p=P)
                if l > 0:
                    weight_pair(w_in, 0, 0, occ)
                sp.wait_ge(s["phase_over"], 4 * (FENCES * l + 1))
                sp.dma_start(x_dram[:], xf[:]).then_inc(s["x_saved"], 16)
                mod_weights(l, 0)
                before = 0
                for run, (first, pairs, _) in enumerate(RUNS):
                    with sp.Fori(int(run == 0), pairs) as i:
                        weight_pair(w_in, first, i, occ + before)
                        mod_weights(l, i + before)
                    before += pairs
                sp.wait_ge(s["split0"], occ + RUN_PAIRS + SEED)
                sp.dma_start(raw[0][:, :, 0:LR_W], w_in[:, :, T_LR * P:T_LR * P + LR_W]).then_inc(s["lr_in"], 16)

                sp.wait_ge(s["lr_split"], 2 * l + 2)
                weight_pair(w_in, T_CH, 0, occ + RUN_PAIRS)

                def group_in(g):
                    kv = g + l * KVH
                    sp.wait_ge(s["k_normed"], kv + SEED)
                    sp.dma_start(kraw[:], proj_dram[g + T_AK]).then_inc(s["k_in"], 16)
                    sp.wait_ge(s["kv_turned"], kv + SEED)
                    sp.dma_start(vraw[:], proj_dram[g + T_AV]).then_inc(s["v_in"], 16)
                    sp.dma_start(ck[:], io["cache_k"][0, l, :, g, :]).then_inc(s["ck_in"], 16)

                sp.wait_ge(s["phase_over"], 4 * (FENCES * l + 2))
                sp.wait_ge(s["x_saved"], 16 * (l + 1))
                group_in(0)
                sp.dma_start(cos[:], io["cos"]).then_inc(s["tables_in"], 16)
                sp.dma_start(sin[:], io["sin"]).then_inc(s["tables_in"], 16)
                for h in range(HEADS):
                    hd = h + l * HEADS
                    sp.wait_ge(s["q_sq"], hd + SEED)
                    sp.wait_ge(s["q_scaled"], hd + SEED)
                    sp.dma_start(qraw[:], proj_dram[h + T_AQ]).then_inc(s["q_in"], 16)
                    sp.wait_ge(s["gated"], hd + SEED)
                    sp.dma_start(ag[:], proj_dram[h + T_AG]).then_inc(s["ag_in"], 16)
                    if h + 1 < HEADS:
                        weight_pair(w_in, T_CH, h + 1, occ + RUN_PAIRS)
                    if h % GROUP == 0 and h + GROUP < HEADS:
                        group_in(h // GROUP + 1)
                w_out = io["w_out"][l].rearrange("(k p) n -> p k n", p=P)

                def half_weights(half, j, i, base):
                    sp.wait_ge(s[f"split{j % 2}"], occ + base + i + SEED)
                    sp.dma_start(raw[j % 2][:, 0:HALF_K, :], w_out[:, half * HALF_K:(half + 1) * HALF_K,
                                                                   bass.ds(i * (2 * P) + j % 2 * P, P)])\
                        .then_inc(s[f"raw_in{j % 2}"], 16)

                def old_x(j, i):
                    sp.dma_start(old[j % 2][:], x_dram[:, bass.ds(i * 2 + j % 2, 1), :].rearrange("p a t -> p (a t)"))\
                        .then_inc(s[f"old_in{j % 2}"], 16)

                def conv_in(j):
                    sp.wait_ge(s["conv_out"], 2 * (j + l * CONV_T) + SEED)
                    for m, first in enumerate((T_CH, T_CB, T_CC)):
                        sp.dma_start(cin[:, m, :], proj_dram[j + first]).then_inc(s["conv_in"], 16)

                def fill_in(j):
                    if j >= 2:
                        half_weights(0, j, j // 2, FIRST)
                    sp.wait_ge(s[f"x_part{j % 2}"], 16 * (l * OUT_PAIRS + j // 2) + SEED)
                    old_x(j, j // 2)

                for j in range(2):
                    half_weights(0, j, 0, FIRST)
                sp.wait_ge(s["phase_over"], 4 * (FENCES * l + 3))
                sp.wait_ge(s["aup_clear"], l + 1)
                for pr in range(PAIRS):
                    sp.wait_ge(s["g_out"], 2 * (pr + l * PAIRS) + SEED)
                    sp.dma_start(lr, proj_dram[T_LR, 0:LR_W, :]).then_inc(s["gla_lr_in"], 16)
                    for z in range(2):
                        sp.dma_start(aup[z * RANK:(z + 1) * RANK, z, :], io["gla_a_up"][l, z][:, pr * P:(pr + 1) * P])\
                            .then_inc(s["gla_lr_in"], 16)
                    if pr == 0:
                        fill_in(0)
                        fill_in(1)
                    sp.dma_start(gv[:], proj_dram[pr * 2 + T_GV:pr * 2 + T_GV + 2].rearrange("a p t -> p a t"))\
                        .then_inc(s["gla_in"], 16)
                    sp.dma_start(gq, proj_dram[pr + T_GQ]).then_inc(s["gla_in"], 16)
                    sp.dma_start(gk, proj_dram[pr + T_GK]).then_inc(s["gla_in"], 16)
                    for z in range(2):
                        sp.dma_start(states[:, z, 0, :], io["state_gla"][0, l, z].rearrange("h d v -> (h d) v")
                                     [pr * P:(pr + 1) * P, :]).then_inc(s["gla_in"], 16)
                    if pr == 0:
                        sp.wait_ge(s["mix_split"], l * KT + HALF_K)
                        sp.dma_start(chunk_keep, io["chunk_keep"]).then_inc(s["tables_in"], 16)
                        sp.dma_start(pair_mask[:], io["pair_mask"]).then_inc(s["tables_in"], 16)
                    fill_in(FILL * pr + 2)
                    sp.dma_start(gg[:], proj_dram[pr * 2 + T_GG:pr * 2 + T_GG + 2].rearrange("a p t -> p a t"))\
                        .then_inc(s["gla_in"], 16)
                    fill_in(FILL * pr + 3)
                    for slot in range(2):
                        sp.wait_ge(s[f"stored{slot}"], 16 * IN_PAIRS * (l + 1) + SEED)
                    sp.dma_start(cgate[:, 2 * pr:2 * pr + 2], proj_dram[T_CG + 2 * pr:T_CG + 2 * pr + 2]
                                 .rearrange("a p t -> p a t")).then_inc(s["cg_in"], 16)
                    conv_in(2 * pr)
                    for f in range(4, FILL):
                        fill_in(FILL * pr + f)
                        if f == FILL - 2:
                            conv_in(2 * pr + 1)
                    if pr + 1 < PAIRS:
                        fill_in(FILL * (pr + 1))
                        fill_in(FILL * (pr + 1) + 1)

                for j in range(2):
                    half_weights(1, j, 0, SECOND)
                for j in range(2):
                    sp.wait_ge(s[f"x_part{j}"], 16 * (l + 1) * OUT_PAIRS + SEED)
                for j in range(2):
                    old_x(j, 0)
                with sp.Fori(1, OUT_PAIRS) as i:
                    for j in range(2):
                        half_weights(1, j, i, SECOND)
                        sp.wait_ge(s[f"taken{j}"], i + occ + SECOND + SEED)
                        old_x(j, i)
            for q in range(4):
                part = slice(q * D // 4, (q + 1) * D // 4)
                sp.wait_ge(s["y_taken"], (q + 1) * KT // 4)
                for i in range(TT):
                    dst = io["y_sample"][0, i * P:(i + 1) * P, part] if i < TT - 1 else io["y_prompt"][0][:, part]
                    sp.dma_start(dst, ytok[:, i, part]).then_inc(s["y_out"], 16)
            sp.wait_ge(s["y_out"], 16 * TT * 4)

        @block.tensor
        def _(pe):
            def spread(out, lhsT, rhs, start=True, stop=True):
                pe.matmul(out[:, 0:512], lhsT, rhs[:, 0:512], start=start, stop=stop)
                return pe.matmul(out[:, 512:TOK], lhsT, rhs[:, 512:TOK], start=start, stop=stop)

            pe.wait_ge(s["ones_set"], 1)
            pe.wait_ge(s["consts_in"], 16 * 5)
            pe.transpose(psO[:, 0:3 * KT], head_rows[:], ident[0:3 * KT, 0:3 * KT]).then_inc(s["rows_turned"], 1)

            def mod_pair(i):
                for half in range(2):
                    if half == 0:
                        pe.wait_ge(s["mod_taken"], i + SEED)
                    for q in range(4):
                        pe.wait_ge(s[f"wmod_in{q}"], i * 32 + (half * 16 + 16))
                        for k in range(KT // 4):
                            n = q * KT // 4 + k
                            mm = pe.matmul(psT[0:2, half * 512:half * 512 + MOD_N], cond[:, n, :], wmod[q][:, k, :],
                                           start=(n == 0), stop=(n == KT - 1))
                        mm.then_inc(s[f"wmod_used{q}"], 1)
                for half in range(2):
                    pe.wait_ge(s["mod_row"], i * 2 + (half + 1))
                    for j in range(MOD_N // P):
                        at = (half * (MOD_N // P) + j) * 2
                        mm = pe.matmul(psO[:, at:at + 2], mod_rows[half][:, j * P:(j + 1) * P], ident[0:2, 0:2],
                                       start=True, stop=True)
                    mm.then_inc(s["mod_turned"], 1)

            pe.wait_ge(s["head_ready"], 2)
            with pe.Fori(0, MOD_BEFORE) as i:
                mod_pair(i)
            pe.wait_ge(s["rows_in"], 16 * 7 * DEPTH)
            for l in range(DEPTH):
                pe.transpose(psP[l][:, 0:ROWS], rows[l][0:ROWS, :], ident[0:ROWS, 0:ROWS]).then_inc(s["rows_turned"], 1)
            pe.wait_ge(s["x_in"], 16 * TT)
            pe.wait_ge(s["vecs_ready"], DEPTH)
            for k in range(KT):
                if k >= 2:
                    pe.wait_ge(s["x_taken"], k - 1)
                for i in range(TT):
                    mm = pe.transpose(psP[k % 2][:, i * P:(i + 1) * P], xtok[:, i, k * P:(k + 1) * P], ident[:])
                mm.then_inc(s["embed_turned"], 1)
            for i in range(MOD_BEFORE, MOD_CHUNKS // 2):
                if i == MOD_CHUNKS // 2 - 1:
                    pe.wait_ge(s["x_squared"], 2 * KT - 1)
                    spread(psP[0], ones[:], sq_sum).then_inc(s["stat_summed"], 1)
                mod_pair(i)

            def project(slot, operand=None, done=0, first=0, last=KT):
                out = psP[slot]
                n = 3 * first
                for k in range(first, last):
                    if operand and k % 2 == 0:
                        pe.wait_ge(s[operand], done + k + 2)
                    for w, x in ((high, x_high), (high, x_low), (low, x_high)):
                        for half in range(2):
                            mm = pe.matmul(out[:, AT + half * HALF:AT + (half + 1) * HALF], w[slot][:, k, :],
                                           x[:, k, half * HALF:(half + 1) * HALF],
                                           start=(n == 0), stop=(n == 3 * KT - 1))
                        n += 1
                return mm

            def pair(i, occ, operand=None, done=0):
                for slot in range(2):
                    pe.wait_ge(s[f"split{slot}"], i + occ + 1 + SEED)
                    pe.wait_ge(s[f"taken{slot}"], i + occ + SEED)
                    project(slot, operand if slot == 0 else None, done).then_inc(s[f"tile_done{slot}"], 1)

            def project_quarter(slot, quarter, n):
                if quarter == 0:
                    pe.wait_ge(s[f"split{slot}"], n + 1 + SEED)
                    pe.wait_ge(s[f"taken{1 - slot}"], n + slot + SEED)
                for k in range(quarter * KT // 4, (quarter + 1) * KT // 4):
                    for w, x in ((high, x_high), (high, x_low), (low, x_high)):
                        for half in range(2):
                            mm = pe.matmul(psP[0][:, AT + half * HALF:AT + (half + 1) * HALF], w[slot][:, k, :],
                                           x[:, k, half * HALF:(half + 1) * HALF],
                                           start=(k == 0 and w is high and x is x_high),
                                           stop=(k == KT - 1 and w is low))
                if quarter == 3:
                    mm.then_inc(s[f"tile_done{slot}"], 1)

            def half_tile(j, out, n, done, waits=None):
                slot, at = j % 2, j // 2 % 2 * HALF_K
                pe.wait_ge(s[f"split{slot}"], n + 1 + SEED)
                pe.wait_ge(s[done[0]], done[1])
                for k in range(HALF_K):
                    if waits is not None and k % 2 == 0:
                        pe.wait_ge(s["mix_split"], waits + k + 2)
                    for w, x in ((high, operand_high), (high, operand_low), (low, operand_high)):
                        for half in range(2):
                            mm = pe.matmul(out[:, AT + half * HALF:AT + (half + 1) * HALF], w[slot][:, at + k, :],
                                           x[:, k, half * HALF:(half + 1) * HALF],
                                           start=(k == 0 and w is high and x is operand_high),
                                           stop=(k == HALF_K - 1 and w is low))
                mm.then_inc(s[f"tile_done{slot}"], 1)

            def mod_sums(l, u):
                pe.wait_ge(s["mod_acc"], u + l * RUN_PAIRS + 1 + SEED)
                pe.wait_ge(s["mod_taken"], u + l * RUN_PAIRS + MOD_CHUNKS // 2 + SEED)
                for n in range(mod_step(l)):
                    for v in range(2):
                        mm = pe.matmul(psT[:, 2 * n + v:2 * n + v + 1], macc[:, v, n * P:(n + 1) * P],
                                       ones[:, 0:1], start=True, stop=True)
                mm.then_inc(s["mod_summed"], 1)

            for l in range(DEPTH):
                occ = l * per_layer
                fence(pe, FENCES * l + 1)
                if l > 0:
                    spread(psO, ones[:], sq_sum).then_inc(s["stat_summed"], 1)
                pair(0, occ, "x_split", KT * l + SEED)
                mod_sums(l, 0)
                before = 0
                for run, (first, pairs, _) in enumerate(RUNS):
                    with pe.Fori(int(run == 0), pairs) as i:
                        pair(i, occ + before)
                        mod_sums(l, i + before)
                    before += pairs
                arrive(pe)
                pe.wait_ge(s["lr_split"], 2 * l + 2)
                pe.wait_ge(s["taken0"], occ + RUN_PAIRS + SEED)
                project(0, last=KT // 2)
                pe.wait_ge(s["phase_over"], 4 * (FENCES * l + 2))
                for g in range(KVH):
                    kv = g + l * KVH
                    hd0 = g * GROUP + l * HEADS
                    pe.wait_ge(s["k_sq"], kv + 1)
                    pe.wait_ge(s["gated"], hd0 + SEED)
                    spread(psO, ones[:], ksq).then_inc(s["k_stat"], 1)
                    if g == 0:
                        project(0, first=KT // 2).then_inc(s["lr_done"], 1)
                    pe.wait_ge(s["k_normed"], kv + 1 + SEED)
                    pe.matmul(psO[:, 0:DEC], rotate[:], kn[:, 0:DEC], start=True, stop=True).then_inc(s["k_rot"], 1)
                    pe.wait_ge(s["v_in"], kv * 16 + 16)
                    pe.wait_ge(s["ck_in"], kv * 16 + 16)
                    pe.wait_ge(s["pt_copied"], hd0 * TT + SEED)
                    pe.transpose(psT[:, 0:P], kn[:, DEC:TOK], ident[:])
                    pe.transpose(psT[:, P:2 * P], ck[:], ident[:])
                    for i in range(TT):
                        mm = pe.transpose(psT[:, (i + 2) * P:(i + 3) * P], vraw[:, i * P:(i + 1) * P], ident[:])
                    mm.then_inc(s["kv_turned"], 1)
                    pe.wait_ge(s["lr_taken"], l + 1)
                    with pe.Fori(0, GROUP) as h:
                        hd = h + hd0
                        n = g * GROUP + h + (occ + RUN_PAIRS)

                        def score(i):
                            pe.wait_ge(s["probs_made"], hd * TT + i + SEED)
                            if i < TT - 1:
                                q = qr[:, i * P:(i + 1) * P]
                                pe.matmul(psP[1][:, 0:512], q, keys[:, 0:512], start=True, stop=True)
                                mm = pe.matmul(psP[1][:, 512:KEYS], q, keys[:, 512:KEYS], start=True, stop=True)
                            else:
                                mm = pe.matmul(psP[1][:, 0:SEQ], qw[:, DEC:TOK], keys[:, KEYS:KEYS + SEQ],
                                               start=True, stop=True)
                            mm.then_inc(s["scored"], 1)

                        def turn(i):
                            pe.wait_ge(s["probs_scaled"], hd * TT + i + 1)
                            pe.wait_ge(s["pt_copied"], hd * TT + i + SEED)
                            for j in range(KEYS // P if i < TT - 1 else 1):
                                mm = pe.transpose(psT[:, j * P:(j + 1) * P], probs[i % 2][:, j * P:(j + 1) * P], ident[:])
                            mm.then_inc(s["prob_turned"], 1)

                        project_quarter(0, 0, n)
                        pe.wait_ge(s["q_scaled"], hd + 1 + SEED)
                        pe.wait_ge(s["gated"], hd + SEED)
                        pe.matmul(psO[:, 0:DEC], rotate[:], qw[:, 0:DEC], start=True, stop=True)
                        pe.wait_ge(s["q_sq"], hd + 1 + SEED)
                        for i in range(TT):
                            mm = pe.matmul(psO[:, TOK + i:TOK + i + 1], qsq[:, i * P:(i + 1) * P], ones[:, 0:1],
                                           start=True, stop=True)
                        mm.then_inc(s["q_rot"], 1)
                        project_quarter(0, 1, n)
                        pe.wait_ge(s["q_roped"], hd + 1)
                        pe.wait_ge(s["kv_ready"], kv * 3 + 3)
                        pe.wait_ge(s["k_roped"], kv + 1)
                        pe.wait_ge(s["cv_in"], kv * 16 + 16)
                        score(0)
                        for i in range(1, TT):
                            project_quarter((i + 1) // 4, (i + 1) % 4, n)
                            score(i)
                            turn(i - 1)
                        project_quarter(1, 2, n)
                        turn(TT - 1)
                        project_quarter(1, 3, n)
                        pe.wait_ge(s["pt_copied"], hd * TT + TT + SEED)
                        for j in range(TT):
                            pe.matmul(psO[:, 0:DEC], vals[:, j if j < TT - 1 else TT, :], probs_t[:, j, :],
                                      start=(j == 0), stop=(j == TT - 1))
                        pe.matmul(psO[:, DEC:TOK], vals[:, TT - 1, :], probs_p[:], start=True, stop=True)\
                            .then_inc(s["pv_done"], 1)

                fence(pe, FENCES * l + 3)
                with pe.Fori(0, PAIRS) as pr:
                    gp = pr + l * PAIRS

                    def fill(*tiles):
                        for f in tiles:
                            n = pr * (FILL // 2) + (f // 2 + occ + FIRST)
                            if f == 3:
                                pe.wait_ge(s["g_tok"], gp * 4 + 2 + SEED)
                            if f == 7:
                                pe.wait_ge(s["g_ovar"], gp * 2 + 2 + SEED)
                            done = {5: ("taken0", n + 1 + SEED), 6: ("taken1", n + SEED)}
                            half_tile(f, fill_place(f), n, done.get(f, (f"taken{f % 2}", n + SEED)),
                                      l * KT if f == 0 else None)

                    fill(0, 1)
                    pe.wait_ge(s["gla_lr_in"], gp * 16 * 3 + 16 * 3)
                    pe.wait_ge(s["g_out"], gp * 2 + SEED)
                    for z in range(2):
                        spread(psP[z], aup[:, z, :], lr).then_inc(s["g_logit"], 1)
                    pe.wait_ge(s["taken1"], pr * (FILL // 2) + (occ + FIRST + 1 + SEED))
                    pe.wait_ge(s["gla_in"], gp * 16 * 6 + 16 * 6)
                    for hh in range(2):
                        pe.wait_ge(s["g_tok"], gp * 4 + hh + SEED)
                        for i in range(TT):
                            mm = pe.transpose(psT[:, i * P:(i + 1) * P], gv[:, hh, i * P:(i + 1) * P], ident[:])
                        mm.then_inc(s["g_turned"], 1)
                    fill(2, 3, 4)
                    pe.wait_ge(s["g_qk"], gp * 2 + 2)
                    for i in range(TT):
                        if i >= 2:
                            pe.wait_ge(s["g_masked"], gp * TT + i - 1)
                        else:
                            pe.wait_ge(s["g_z"], gp * 2 + 2)
                        for z in range(2):
                            for hh in range(2):
                                part = slice(hh * DK, (hh + 1) * DK)
                                mm = pe.matmul(psP[i % 2][:, hh * 512 + z * P:][:, 0:P],
                                               kt_[part, z, i * P:(i + 1) * P], qt[part, z, i * P:(i + 1) * P],
                                               start=True, stop=True)
                        mm.then_inc(s["g_att"], 1)
                    pe.wait_ge(s["g_hat"], gp * 4 + 4)
                    pe.wait_ge(s["taken1"], pr * (FILL // 2) + (occ + FIRST + 2 + SEED))
                    for z in range(2):
                        pe.wait_ge(s["g_tok"], gp * 4 + 2 + z + SEED)
                        for i in range(TT):
                            mm = pe.transpose(psT[:, i * P:(i + 1) * P], gm[:, z, i * P:(i + 1) * P], ident[:])
                        mm.then_inc(s["g_turned"], 1)
                    pe.wait_ge(s["g_tok"], gp * 4 + 4 + SEED)
                    pe.wait_ge(s["g_masked"], gp * TT + TT)
                    for n, (fwd, bwd) in enumerate(STEPS):
                        if n >= 2:
                            pe.wait_ge(s["g_state"], (gp * len(STEPS) + n - 1) * 4 + SEED)
                        for z, ch in enumerate((fwd, bwd)):
                            part = slice(ch % 2 * CH, (ch % 2 + 1) * CH)
                            mm = pe.matmul((psT, psP[1])[n % 2][:, ch % 2 * 512:][:, 0:256], k_tok[part, z, ch // 2, :],
                                           v_tok[part, ch // 2, :, :].rearrange("p a b -> p (a b)"),
                                           start=True, stop=True)
                        mm.then_inc(s["g_u"], 1)
                    pe.wait_ge(s["g_state"], (gp + 1) * len(STEPS) * 4 + SEED)
                    pe.wait_ge(s["g_summed"], gp * TT + TT)
                    for hh in range(2):
                        part = slice(hh * DK, (hh + 1) * DK)
                        for i in range(TT):
                            parts = [(z, ch) for ch in (2 * i, 2 * i + 1) for z in range(2)
                                     if state_at(z, ch) != DEC_CH + 1]
                            pe.matmul(psP[hh][:, i * P:(i + 1) * P], v_tok[:, i, hh, :], att_s[:, i, hh, :],
                                      start=True, stop=False)
                            for n, (z, ch) in enumerate(parts):
                                mm = pe.matmul(psP[hh][:, ch * CH:(ch + 1) * CH], states[part, z, state_at(z, ch), :],
                                               gz[part, z, ch * CH:(ch + 1) * CH],
                                               start=False, stop=(n == len(parts) - 1))
                        mm.then_inc(s["g_o"], 1)
                    fill(5)
                    for hh in range(2):
                        pe.wait_ge(s["g_osq"], gp * 2 + hh + 1)
                        pe.wait_ge(s["g_ovar"], gp * 2 + hh + SEED)
                        spread(psT, ones[:], stage[hh]).then_inc(s["g_ostat"], 1)
                    fill(6, 7)

                fence(pe, FENCES * l + 4)
                for f in range(4):
                    n = occ + SECOND + f // 2
                    half_tile(f, psP[f % 2], n, (f"taken{f % 2}", n + SEED), l * KT + HALF_K if f == 0 else None)
                with pe.Fori(1, KT // 4) as i:
                    for f in range(4):
                        n = i * 2 + (occ + SECOND + f // 2)
                        half_tile(f, psP[f % 2], n, (f"taken{f % 2}", n + SEED))

            fence(pe, FENCES * DEPTH + 1)
            spread(psO, ones[:], sq_sum).then_inc(s["stat_summed"], 1)
            for k in range(KT):
                pe.wait_ge(s["y_scaled"], k + 1)
                if k >= 2:
                    pe.wait_ge(s["y_taken"], k - 1)
                for i in range(TT):
                    mm = pe.transpose(psP[k % 2][:, i * P:(i + 1) * P], xf[:, k, i * P:(i + 1) * P], ident[:])
                mm.then_inc(s["y_turned"], 1)

        @block.scalar
        def _(act):
            act.wait_ge(s["rows_turned"], 1)
            act.activation(head[:], psO[:, 0:3 * KT], ACT.Copy).then_inc(s["head_ready"], 1)
            act.wait_ge(s["head_ready"], 1)
            act.activation(cond[:].rearrange("p k v -> p v k"), head[:, 0:2 * KT].rearrange("p (v k) -> p v k", v=2),
                           ACT.Silu).then_inc(s["head_ready"], 1)
            def ln_exp(src, tmp, out, ready, n, ln_sem, exp_sem):
                act.wait_ge(s[ready], n + (SEED if ready in SEEDED else 0))
                act.activation(tmp, src, ACT.Ln).then_inc(s[ln_sem], 1)
                act.wait_ge(s[ln_sem], n)
                act.activation(out, tmp, ACT.Exp, scale=-0.5).then_inc(s[exp_sem], 1)

            def mod_take(i, after=((), ())):
                for half in range(2):
                    act.wait_ge(s["wmod_used3"], i * 2 + (half + 1 + SEED))
                    act.activation(mod_rows[half][:], psT[0:2, half * 512:half * 512 + MOD_N], ACT.Copy)\
                        .then_inc(s["mod_row"], 1)
                    for tile in after[half]:
                        tokens_in(tile)
                act.wait_ge(s["mod_turned"], i * 2 + 2)
                act.activation(mod_raw[:, 0, bass.ds(i * (2 * MOD_N // P), 2 * MOD_N // P), :].rearrange("p a b -> p (a b)"),
                               psO[:, 0:4 * MOD_N // P], ACT.Copy).then_inc(s["mod_taken"], 1)

            for l in range(DEPTH):
                for at, src in (
                        (R_BMOD, io["b_mod"][l].rearrange("(k p) -> k p", p=P)),
                        (R_NORM, io["norm_w"][l].rearrange("(k p) -> k p", p=P)),
                        (R_Q, io["q_norm_w"][l:l + 1]), (R_K, io["k_norm_w"][l:l + 1]),
                        (R_CONV, io["conv_w"][l].rearrange("t (j p) -> (t j) p", p=P)),
                        (R_ABIAS, io["gla_a_bias"][l].rearrange("z (j p) -> (z j) p", p=P)),
                        (R_GNORM, io["gla_norm_w"][l:l + 1])):
                    act.dma_start(rows[l][at:at + src.shape[0], :], src).then_inc(s["rows_in"], 16)
            def tokens_in(i):
                src = io["x_sample"][0, i * P:(i + 1) * P, :] if i < TT - 1 else io["x_prompt"][0]
                act.dma_start(xtok[:, i, :], src).then_inc(s["x_in"], 16)

            tokens_in(0)
            for i in range(MOD_BEFORE):
                mod_take(i, after=[[2 * i + 1], [2 * i + 2]])
            for l in range(DEPTH):
                act.wait_ge(s["rows_turned"], l + 2)
                act.activation(vecs[:, l, :], psP[l][:, 0:ROWS], ACT.Copy).then_inc(s["vecs_ready"], 1)

            for k in range(KT):
                act.wait_ge(s["embed_turned"], k + 1)
                act.activation(xf[:, k, :], psP[k % 2][:, 0:TOK], ACT.Copy).then_inc(s["x_taken"], 1)
            for i in range(MOD_BEFORE, MOD_CHUNKS // 2):
                if i == MOD_CHUNKS // 2 - 1:
                    ln_exp(r_a[:], rstd[:], r_b[:], "stat_var", 1, "stat_ln", "stat_exp")
                mod_take(i)

            for l in range(DEPTH):
                occ = l * per_layer
                fence(act, FENCES * l + 1)
                if l > 0:
                    ln_exp(r_a[:], rstd[:], r_b[:], "stat_var", l + 1, "stat_ln", "stat_exp")
                act.wait_ge(s["mod_ready"], 2 * l + 1)
                with act.Fori(0, KT // 2) as i:
                    for slot in range(2):
                        act.wait_ge(s[f"scaled{slot}"], i + l * KT // 2 + 1)
                        if slot == 1:
                            act.wait_ge(s["x_split"], i * 2 + l * KT + SEED)
                        for v, part in ((0, slice(0, DEC)), (1, slice(DEC, TOK))):
                            a = act.activation(stage[slot][:, part], xt[slot][:, part], ACT.Identity,
                                               bias=mod[:, bass.ds(i * 2 + slot, 1), v:v + 1].rearrange("p a b -> p (a b)"),
                                               scale=mod_a[:, bass.ds(i * 2 + slot, 1), v:v + 1].rearrange("p a b -> p (a b)"))
                            a.then_inc(s[f"shifted{slot}"], 1)
                before = 0
                act.wait_ge(s["x_split"], KT * (l + 1) + SEED)
                for run, (first, pairs, gate) in enumerate(RUNS):
                    with act.Fori(0, pairs) as i:
                        for slot in range(2):
                            act.wait_ge(s[f"stored{slot}"], i * 16 + (before + l * IN_PAIRS) * 16 + SEED)
                            act.wait_ge(s[f"tile_done{slot}"], i + occ + before + 1 + SEED)
                            act.activation(stage[slot][:], psP[slot][:, AT:AT + TOK], ACT.Silu if gate else ACT.Copy)\
                                .then_inc(s[f"taken{slot}"], 1)
                            act.wait_ge(s[f"taken{slot}"], i + occ + before + 1 + SEED)
                            act.dma_start(proj_dram[bass.ds(i * 2 + (slot + first), 1)].rearrange("a p t -> p (a t)"),
                                          stage[slot][:]).then_inc(s[f"stored{slot}"], 16)
                        act.wait_ge(s["mod_summed"], i + before + l * RUN_PAIRS + 1 + SEED)
                        m = act.activation(mod_raw[:, l, bass.ds((i + before) * GATE_STEP + 2 * KT, GATE_STEP), :]
                                           .rearrange("p a b -> p (a b)"), psT[:, 0:2 * GATE_STEP], ACT.Copy)
                        if l + 1 < DEPTH:
                            m = act.activation(mod_raw[:, l + 1, bass.ds((i + before) * NEXT_STEP, NEXT_STEP), :]
                                               .rearrange("p a b -> p (a b)"), psT[:, 2 * GATE_STEP:2 * MOD_STEP], ACT.Copy)
                        m.then_inc(s["mod_taken"], 1)
                    before += pairs
                for slot in range(2):
                    act.wait_ge(s[f"stored{slot}"], 16 * (IN_PAIRS * l + RUN_PAIRS) + SEED)

                fence(act, FENCES * l + 2)
                for g in range(KVH):
                    kv = g + l * KVH
                    hd0 = g * GROUP + l * HEADS
                    act.wait_ge(s["k_in"], kv * 16 + 16)
                    act.wait_ge(s["k_stat"], kv + SEED)
                    act.activation(ksq[:], kraw[:], ACT.Square).then_inc(s["k_sq"], 1)
                    ln_exp(r_a[:], rstd[:], r_b[:], "k_var", kv + 1, "k_ln", "k_exp")
                    if g == 0:
                        act.wait_ge(s["lr_done"], l + 1)
                        act.activation(stage[0][0:LR_W, :], psP[0][0:LR_W, AT:AT + TOK], ACT.Copy).then_inc(s["lr_taken"], 1)
                        act.wait_ge(s["lr_taken"], l + 1)
                        act.dma_start(proj_dram[T_LR, 0:LR_W, :], stage[0][0:LR_W, :]).then_inc(s["lr_stored"], 16)
                    act.wait_ge(s["kv_turned"], kv + 1 + SEED)
                    act.wait_ge(s["kv_stored"], kv * 32 + SEED)
                    act.activation(newk[:], psT[:, 0:P], ACT.Copy).then_inc(s["kv_ready"], 1)
                    act.activation(keys[:, DEC:KEYS], psT[:, P:2 * P], ACT.Copy).then_inc(s["kv_ready"], 1)
                    act.activation(vals[:, 0:TT, :], psT[:, 2 * P:2 * P + TOK].rearrange("p (a b) -> p a b", b=P), ACT.Copy)\
                        .then_inc(s["kv_ready"], 1)
                    act.wait_ge(s["kv_ready"], kv * 3 + 3)
                    act.dma_start(vals[:, TT, :], io["cache_v"][0, l].rearrange("s g d -> s (g d)")[:, bass.ds(g * HD, HD)])\
                        .then_inc(s["cv_in"], 16)
                    act.dma_start(io["new_k"][0, l].rearrange("s g d -> s (g d)")[:, bass.ds(g * HD, HD)], newk[:])\
                        .then_inc(s["kv_stored"], 16)
                    act.dma_start(io["new_v"][0, l].rearrange("s g d -> s (g d)")[:, bass.ds(g * HD, HD)],
                                  vals[:, TT - 1, :]).then_inc(s["kv_stored"], 16)
                    act.wait_ge(s["lr_stored"], 16 * (l + 1))
                    with act.Fori(0, GROUP) as h:
                        hd = h + hd0
                        act.wait_ge(s["q_in"], hd * 16 + 16)
                        act.wait_ge(s["q_rot"], hd + SEED)
                        act.activation(qsq[:], qraw[:], ACT.Square).then_inc(s["q_sq"], 1)
                        ln_exp(qv[:], qb[:], qa[:], "q_roped", hd + 1, "q_ln", "q_exp")
                        act.wait_ge(s["q_rs"], hd + 1)

                        def prob(i):
                            width = KEYS if i < TT - 1 else SEQ
                            act.wait_ge(s["nm_ready"], hd * TT + i + 1)
                            act.wait_ge(s["prob_turned"], hd * TT + max(i - 1, 0) + SEED)
                            act.activation(probs[i % 2][:, 0:width], psP[1][:, 0:width], ACT.Exp,
                                           bias=nm[:, i:i + 1], scale=qs[:, i:i + 1], accum_out=sums[:, i:i + 1])\
                                .then_inc(s["probs_made"], 1)

                        def take(i):
                            act.wait_ge(s["prob_turned"], hd * TT + i + 1 + SEED)
                            if i < TT - 1:
                                act.activation(probs_t[:, :, i * P:(i + 1) * P],
                                               psT[:, 0:KEYS].rearrange("p (a b) -> p a b", b=P), ACT.Copy)\
                                    .then_inc(s["pt_copied"], 1)
                            else:
                                act.activation(probs_p[:], psT[:, 0:P], ACT.Copy).then_inc(s["pt_copied"], 1)

                        def take_tile(slot):
                            n = g * GROUP + h
                            act.wait_ge(s[f"stored{slot}"], n * 16 + (RUN_PAIRS + l * IN_PAIRS) * 16 + SEED)
                            act.wait_ge(s[f"tile_done{slot}"], n + occ + RUN_PAIRS + 1 + SEED)
                            act.activation(stage[slot][:], psP[0][:, AT:AT + TOK], ACT.Copy).then_inc(s[f"taken{slot}"], 1)
                            act.wait_ge(s[f"taken{slot}"], n + occ + RUN_PAIRS + 1 + SEED)
                            act.dma_start(proj_dram[bass.ds(n * 2 + (slot + T_CH), 1)].rearrange("a p t -> p (a t)"),
                                          stage[slot][:]).then_inc(s[f"stored{slot}"], 16)

                        prob(0)
                        prob(1)
                        act.wait_ge(s["pv_done"], hd + SEED)
                        take(0)
                        take_tile(0)
                        for i in range(2, TT):
                            prob(i)
                            take(i - 1)
                        take(TT - 1)
                        take_tile(1)
                act.wait_ge(s["kv_stored"], 32 * KVH * (l + 1) + SEED)

                fence(act, FENCES * l + 3)
                with act.Fori(0, HALF_K) as k:
                    act.activation(operand_high[:, bass.ds(k, 1), :], xf[:, bass.ds(k, 1), :], ACT.Copy)\
                        .then_inc(s["mix_high"], 1)
                for slot in range(2):
                    act.wait_ge(s[f"stored{slot}"], 16 * IN_PAIRS * (l + 1) + SEED)
                with act.Fori(0, PAIRS) as pr:
                    gp = pr + l * PAIRS

                    def keep_sum(f):
                        act.wait_ge(s[f"taken{f % 2}"], pr * (FILL // 2) + (f // 2 + occ + FIRST + 1 + SEED))
                        act.dma_start(x_dram[:, bass.ds(pr * FILL + f, 1), :].rearrange("p a t -> p (a t)"), old[f % 2][:])\
                            .then_inc(s[f"x_part{f % 2}"], 16)

                    keep_sum(0)
                    act.wait_ge(s["g_out"], gp * 2 + SEED)
                    for z in range(2):
                        act.wait_ge(s["g_logit"], gp * 2 + z + 1)
                        act.activation(gz[:, z, :], psP[z][:, 0:TOK], ACT.Identity,
                                       bias=vecs[:, l, bass.ds(pr + (R_ABIAS + z * PAIRS), 1)]).then_inc(s["g_z"], 1)
                    for hh in range(2):
                        act.wait_ge(s["g_turned"], gp * 4 + hh + 1)
                        act.activation(v_tok[:, :, hh, :], psT[:, 0:TOK].rearrange("p (a b) -> p a b", b=P), ACT.Copy)\
                            .then_inc(s["g_tok"], 1)
                    keep_sum(1)
                    act.wait_ge(s["g_neg"], gp + 1)
                    act.activation(cum[:], gz[:], ACT.Exp).then_inc(s["g_ln"], 1)
                    act.wait_ge(s["g_ln"], gp * 2 + 1)
                    act.activation(gz[:], cum[:], ACT.Ln, bias=1.0).then_inc(s["g_ln"], 1)
                    act.wait_ge(s["g_clamp"], gp + 1)
                    act.activation(qt[:], gm[:], ACT.Exp, scale=1 / TAU).then_inc(s["g_factors"], 1)
                    act.activation(kt_[:], gm[:], ACT.Exp, scale=-1 / TAU).then_inc(s["g_factors"], 1)
                    act.wait_ge(s["g_mid"], gp * 8 + 8)
                    act.activation(small[:], small[:], ACT.Exp, scale=1 / TAU).then_inc(s["g_smallx"], 1)
                    keep_sum(2)
                    act.wait_ge(s["cg_in"], gp * 16 + 16)
                    act.activation(cgate[:, bass.ds(pr * 2, 2), :], cgate[:, bass.ds(pr * 2, 2), :], ACT.Silu)\
                        .then_inc(s["cg_silu"], 2)
                    keep_sum(3)
                    for z in range(2):
                        act.wait_ge(s["g_turned"], gp * 4 + 3 + z)
                        act.activation(k_tok[:, z, :, :], psT[:, 0:TOK].rearrange("p (a b) -> p a b", b=P), ACT.Copy)\
                            .then_inc(s["g_tok"], 1)
                    keep_sum(4)
                    for hh in range(2):
                        act.wait_ge(s["g_o"], gp * 2 + hh + 1)
                        act.activation(stage[hh][:], psP[hh][:, 0:TOK], ACT.Square).then_inc(s["g_osq"], 1)
                    keep_sum(5)
                    for hh in range(2):
                        ln_exp(r_a[:], rstd[:], r_b[:], "g_ovar", gp * 2 + hh + 1, "g_oln", "g_oexp")
                    keep_sum(6)
                    keep_sum(7)
                    act.wait_ge(s["g_out"], gp * 2 + 2 + SEED)
                    for z in range(2):
                        act.dma_start(io["new_state"][0, l, z].rearrange("h d v -> (h d) v")[bass.ds(pr * P, P), :],
                                      states[:, z, STATES - 1, :]).then_inc(s["g_saved"], 16)

                fence(act, FENCES * l + 4)
                with act.Fori(0, HALF_K) as k:
                    act.activation(operand_high[:, bass.ds(k, 1), :], xf[:, bass.ds(k + HALF_K, 1), :], ACT.Copy)\
                        .then_inc(s["mix_high"], 1)
                with act.Fori(0, OUT_PAIRS) as i:
                    for slot in range(2):
                        act.wait_ge(s[f"taken{slot}"], i + occ + SECOND + 1 + SEED)
                        act.wait_ge(s["x_acc"], i * 2 + (slot + l * (KT + 1)) + SEED)
                        act.activation(xt[slot][:], xf[:, bass.ds(i * 2 + slot, 1), :].rearrange("p a b -> p (a b)"),
                                       ACT.Square).then_inc(s["x_sq"], 1)
                act.wait_ge(s["g_saved"], 32 * PAIRS * (l + 1) + SEED)

            fence(act, FENCES * DEPTH + 1)
            ln_exp(r_a[:], rstd[:], r_b[:], "stat_var", DEPTH + 1, "stat_ln", "stat_exp")
            for k in range(KT):
                act.wait_ge(s["y_turned"], k + 1)
                act.activation(ytok[:, :, k * P:(k + 1) * P], psP[k % 2][:, 0:TOK].rearrange("p (a b) -> p a b", b=P),
                               ACT.Copy).then_inc(s["y_taken"], 1)

        @block.vector
        def _(dve):
            dve.memset(ones[:], 1.0).then_inc(s["ones_set"], 1)
            for k in range(KT):
                dve.wait_ge(s["x_taken"], k + 1)
                if k == 0:
                    dve.tensor_tensor(sq_sum[:], xf[:, k, :], xf[:, k, :], ALU.mult).then_inc(s["x_squared"], 1)
                    continue
                dve.wait_ge(s["x_squared"], 2 * k - 1)
                dve.tensor_tensor(r_a[:], xf[:, k, :], xf[:, k, :], ALU.mult).then_inc(s["x_squared"], 1)
                dve.wait_ge(s["x_squared"], 2 * k)
                dve.tensor_tensor(sq_sum[:], sq_sum[:], r_a[:], ALU.add).then_inc(s["x_squared"], 1)

            def refine(out, v, r0, tmp, exp_sem, n, step_sem, base, scale=None):
                dve.wait_ge(s[exp_sem], n)
                dve.scalar_tensor_tensor(tmp, r0, -0.5, r0, ALU.mult, ALU.mult).then_inc(s[step_sem], 1)
                dve.wait_ge(s[step_sem], base + 1)
                dve.tensor_tensor(tmp, tmp, v, ALU.mult).then_inc(s[step_sem], 1)
                dve.wait_ge(s[step_sem], base + 2)
                return dve.scalar_tensor_tensor(out, tmp, 1.5, r0, ALU.add, ALU.mult)

            def norm_factor(stat, n):
                dve.wait_ge(s["stat_summed"], n + 1)
                dve.tensor_scalar(r_a[:], stat[:, 0:TOK], 1.0 / D, EPS, ALU.mult, ALU.add).then_inc(s["stat_var"], 1)
                refine(rstd[:], r_a[:], r_b[:], sq_sum[:], "stat_exp", n + 1, "stat_rs", 3 * n)\
                    .then_inc(s["stat_rs"], 1)
                dve.wait_ge(s["stat_rs"], 3 * n + 3)

            norm_factor(psP[0], 0)

            def split(slot, i, occ, whole):
                dve.wait_ge(s[f"raw_in{slot}"], (i + occ) * 16 + 16)
                dve.wait_ge(s[f"tile_done{slot}"], i + occ + SEED)
                dve.tensor_copy(high[slot][:], raw[slot][:]).then_inc(s[f"high{slot}"], 1)
                dve.wait_ge(s[f"high{slot}"], i + whole + 1)
                dve.tensor_tensor(low[slot][:], raw[slot][:], high[slot][:].bitcast(F32), ALU.subtract)\
                    .then_inc(s[f"split{slot}"], 1)

            def split_quarter(slot, quarter, n, quarters):
                if quarter == 0:
                    dve.wait_ge(s[f"raw_in{slot}"], n * 16 + 16)
                    dve.wait_ge(s[f"tile_done{slot}"], n + SEED)
                part = slice(quarter * KT // 4, (quarter + 1) * KT // 4)
                dve.tensor_copy(high[slot][:, part], raw[slot][:, part]).then_inc(s[f"high_quarter{slot}"], 1)
                dve.wait_ge(s[f"high_quarter{slot}"], quarters * 4 + quarter + 1)
                m = dve.tensor_tensor(low[slot][:, part], raw[slot][:, part], high[slot][:, part].bitcast(F32), ALU.subtract)
                if quarter == 3:
                    m.then_inc(s[f"split{slot}"], 1)

            def split_half(j, n, whole):
                slot, part = j % 2, slice(j // 2 % 2 * HALF_K, (j // 2 % 2 + 1) * HALF_K)
                dve.wait_ge(s[f"raw_in{slot}"], n * 16 + 16)
                dve.wait_ge(s[f"tile_done{slot}"], n - 1 + SEED)
                dve.tensor_copy(high[slot][:, part], raw[slot][:, 0:HALF_K]).then_inc(s[f"high{slot}"], 1)
                dve.wait_ge(s[f"high{slot}"], whole + 1)
                dve.tensor_tensor(low[slot][:, part], raw[slot][:, 0:HALF_K], high[slot][:, part].bitcast(F32),
                                  ALU.subtract).then_inc(s[f"split{slot}"], 1)

            def mix_low(at):
                with dve.Fori(0, HALF_K) as k:
                    dve.wait_ge(s["mix_high"], k + (at + 1))
                    dve.tensor_tensor(operand_low[:, bass.ds(k, 1), :], xf[:, bass.ds(k + at % KT, 1), :],
                                      operand_high[:, bass.ds(k, 1), :].bitcast(F32), ALU.subtract)\
                        .then_inc(s["mix_split"], 1)

            def add_product(dst, product, j, tile, n, loaded):
                slot = j % 2
                dve.wait_ge(s[f"tile_done{slot}"], n + 1 + SEED)
                dve.wait_ge(s[f"old_in{slot}"], loaded * 16 + 16)
                for v, part in ((0, slice(0, DEC)), (1, slice(DEC, TOK))):
                    m = dve.scalar_tensor_tensor(dst(part), product[:, AT:AT + TOK][:, part],
                                                 mod[:, bass.ds(tile + 2 * KT, 1), v:v + 1].rearrange("p a b -> p (a b)"),
                                                 old[slot][:, part], ALU.mult, ALU.add)
                m.then_inc(s[f"taken{slot}"], 1)

            def mod_tiles(l, i):
                u, width = i + l * RUN_PAIRS, mod_step(l) * P
                dve.wait_ge(s["mod_summed"], u + SEED)
                for n in range(KT):
                    hf, k = n // (KT // 2), n % (KT // 2)
                    if k == 0:
                        loads = 2 if l + 1 < DEPTH else 1
                        dve.wait_ge(s[f"mraw_in{hf}"], i * (16 * loads) + (l * RUN_PAIRS * 32 + 16 * loads))
                    for v in range(2):
                        c = cond[:, n, v:v + 1]
                        if n == 0:
                            m = dve.tensor_scalar(macc[:, v, 0:width], mraw[hf][:, k, 0:width], c, None, ALU.mult)
                        else:
                            if v == 0:
                                dve.wait_ge(s["mod_step0"], u * (KT - 1) + n + SEED)
                            elif n == KT // 2:
                                dve.wait_ge(s["mod_half"], u + 1 + SEED)
                            else:
                                dve.wait_ge(s["mod_step1"], u * (KT - 2) + (n if n < KT // 2 else n - 1) + SEED)
                            m = dve.scalar_tensor_tensor(macc[:, v, 0:width], mraw[hf][:, k, 0:width], c,
                                                         macc[:, v, 0:width], ALU.mult, ALU.add)
                        if v == 0 and n < KT - 1:
                            m.then_inc(s["mod_step0"], 1)
                        elif v == 1 and n == KT // 2 - 1:
                            m.then_inc(s["mod_half"], 1)
                        elif v == 1 and n == KT - 1:
                            m.then_inc(s["mod_acc"], 1)
                        elif v == 1:
                            m.then_inc(s["mod_step1"], 1)

            for l in range(DEPTH):
                occ = l * per_layer
                whole = l * (RUN_PAIRS + 2 * OUT_PAIRS)
                split(0, 0, occ, whole)
                fence(dve, FENCES * l + 1)
                dve.wait_ge(s["mod_taken"], MOD_CHUNKS // 2 + l * RUN_PAIRS + SEED)
                dve.wait_ge(s["vecs_ready"], DEPTH)
                dve.tensor_tensor(mod[:, 0:2 * KT], mod_raw[:, l, 0:2 * KT], vecs[:, l, R_BMOD:R_BMOD + 2 * KT].unsqueeze(2)
                                  .to_broadcast([P, 2 * KT, 2]), ALU.add).then_inc(s["mod_added"], 1)
                dve.wait_ge(s["mod_added"], l + 1)
                dve.scalar_tensor_tensor(mod_a[:], mod[:, KT:2 * KT, :], 1.0, vecs[:, l, R_NORM:R_NORM + KT].unsqueeze(2)
                                         .to_broadcast([P, KT, 2]), ALU.add, ALU.mult).then_inc(s["mod_ready"], 1)
                if l > 0:
                    norm_factor(psO, l)
                def scale_even(i):
                    dve.tensor_tensor(xt[0][:], xf[:, bass.ds(i * 2, 1), :].rearrange("p a b -> p (a b)"),
                                      rstd[:], ALU.mult).then_inc(s["scaled0"], 1)

                def split_x(slot, i):
                    at = bass.ds(i * 2 + slot, 1)
                    dve.wait_ge(s[f"shifted{slot}"], i * 2 + l * KT + 2)
                    dve.tensor_copy(x_high[:, at, :].rearrange("p a b -> p (a b)"), stage[slot][:])\
                        .then_inc(s[f"x_high{slot}"], 1)
                    dve.wait_ge(s[f"x_high{slot}"], i + l * KT // 2 + 1 + SEED)
                    dve.tensor_tensor(x_low[:, at, :].rearrange("p a b -> p (a b)"), stage[slot][:],
                                      x_high[:, at, :].rearrange("p a b -> p (a b)").bitcast(F32),
                                      ALU.subtract).then_inc(s["x_split"], 1)

                scale_even(0)
                with dve.Fori(0, KT // 2 - 1) as i:
                    split_x(0, i)
                    scale_even(i + 1)
                    split_x(1, i)
                for slot in range(2):
                    split_x(slot, KT // 2 - 1)
                split(1, 0, occ, whole)
                mod_tiles(l, 0)
                before = 0
                for run, (first, pairs, _) in enumerate(RUNS):
                    with dve.Fori(int(run == 0), pairs) as i:
                        for slot in range(2):
                            split(slot, i, occ + before, whole + before)
                        mod_tiles(l, i + before)
                    before += pairs
                dve.wait_ge(s["lr_in"], 16 * (l + 1))
                dve.wait_ge(s["tile_done0"], occ + RUN_PAIRS + SEED)
                dve.tensor_copy(high[0][:, :, 0:LR_W], raw[0][:, :, 0:LR_W]).then_inc(s["lr_split"], 1)
                dve.wait_ge(s["lr_split"], 2 * l + 1)
                dve.tensor_tensor(low[0][:, :, 0:LR_W], raw[0][:, :, 0:LR_W], high[0][:, :, 0:LR_W].bitcast(F32),
                                  ALU.subtract).then_inc(s["lr_split"], 1)

                fence(dve, FENCES * l + 2)
                dve.wait_ge(s["x_saved"], 16 * (l + 1))
                for g in range(KVH):
                    kv = g + l * KVH
                    hd0 = g * GROUP + l * HEADS
                    dve.wait_ge(s["k_stat"], kv + 1 + SEED)
                    dve.tensor_scalar(r_a[:], psO[:, 0:TOK], 1.0 / HD, EPS, ALU.mult, ALU.add).then_inc(s["k_var"], 1)
                    refine(rstd[:], r_a[:], r_b[:], ksq[:], "k_exp", kv + 1, "k_n", kv * 3).then_inc(s["k_n"], 1)
                    dve.wait_ge(s["k_n"], kv * 3 + 3)
                    dve.wait_ge(s["kv_turned"], kv + SEED)
                    dve.scalar_tensor_tensor(kn[:], kraw[:], vecs[:, l, R_K:R_K + 1], rstd[:], ALU.mult, ALU.mult)\
                        .then_inc(s["k_normed"], 1)
                    if g == 0:
                        dve.wait_ge(s["lr_done"], l + 1)
                        split(0, 0, occ + RUN_PAIRS, whole + RUN_PAIRS)
                        dve.wait_ge(s["tables_in"], 64 * l + 32)
                    dve.wait_ge(s["k_rot"], kv + 1)
                    dve.tensor_tensor(t2[:], psO[:, 0:DEC], sin[:], ALU.mult).then_inc(s["k_r"], 1)
                    dve.wait_ge(s["k_normed"], kv + 1 + SEED)
                    dve.tensor_tensor(t1[:], kn[:, 0:DEC], cos[:], ALU.mult).then_inc(s["k_r"], 1)
                    dve.tensor_copy(keys[:, KEYS:], kn[:, DEC:TOK]).then_inc(s["k_r"], 1)
                    dve.wait_ge(s["k_r"], kv * 3 + 3)
                    dve.tensor_tensor(keys[:, 0:DEC], t1[:], t2[:], ALU.add).then_inc(s["k_roped"], 1)
                    with dve.Fori(0, GROUP) as h:
                        hd = h + hd0
                        n = g * GROUP + h + (occ + RUN_PAIRS)
                        dve.wait_ge(s["q_in"], hd * 16 + 16)
                        dve.tensor_scalar(qw[:], qraw[:], vecs[:, l, R_Q:R_Q + 1], None, ALU.mult).then_inc(s["q_scaled"], 1)
                        dve.wait_ge(s["q_scaled"], hd + 1 + SEED)
                        dve.tensor_tensor(t1[:], qw[:, 0:DEC], cos[:], ALU.mult).then_inc(s["q_r"], 1)
                        split_quarter(1, 0, n, hd)
                        dve.wait_ge(s["q_rot"], hd + 1 + SEED)
                        dve.tensor_tensor(t2[:], psO[:, 0:DEC], sin[:], ALU.mult).then_inc(s["q_r"], 1)
                        dve.tensor_scalar(qv[:], psO[:, TOK:TOK + TT], 1.0 / HD, EPS, ALU.mult, ALU.add)\
                            .then_inc(s["q_r"], 1)
                        dve.wait_ge(s["q_r"], hd * 3 + 3)
                        dve.tensor_tensor(qr[:], t1[:], t2[:], ALU.add).then_inc(s["q_roped"], 1)
                        split_quarter(1, 1, n, hd)
                        refine(inv[:], qv[:], qa[:], mx_[:], "q_exp", hd + 1, "q_n", hd * 3).then_inc(s["q_n"], 1)
                        dve.wait_ge(s["q_n"], hd * 3 + 3)
                        dve.tensor_scalar(qs[:], inv[:], HD ** -0.5, None, ALU.mult).then_inc(s["q_rs"], 1)
                        dve.wait_ge(s["q_rs"], hd + 1)

                        def row_max(i):
                            width = KEYS if i < TT - 1 else SEQ
                            dve.wait_ge(s["scored"], hd * TT + i + 1)
                            dve.tensor_reduce(mx_[:, i:i + 1], psP[1][:, 0:width], AX.X, ALU.max)\
                                .then_inc(s["max_step"], 1)
                            dve.wait_ge(s["max_step"], hd * TT + i + 1)
                            dve.tensor_scalar(nm[:, i:i + 1], mx_[:, i:i + 1], qs[:, i:i + 1], -1.0, ALU.mult, ALU.mult)\
                                .then_inc(s["nm_ready"], 1)

                        def scale_probs(i):
                            width = KEYS if i < TT - 1 else SEQ
                            dve.wait_ge(s["probs_made"], hd * TT + i + 1 + SEED)
                            dve.reciprocal(inv[:, i:i + 1], sums[:, i:i + 1]).then_inc(s["inv_ready"], 1)
                            dve.wait_ge(s["inv_ready"], hd * TT + i + 1)
                            dve.tensor_scalar(probs[i % 2][:, 0:width], probs[i % 2][:, 0:width], inv[:, i:i + 1], None,
                                              ALU.mult).then_inc(s["probs_scaled"], 1)

                        for i in range(TT):
                            row_max(i)
                            if i < 2:
                                split_quarter(1, i + 2, n, hd)
                            else:
                                split_quarter(0, i - 2, n + 1, hd)
                            scale_probs(i)
                        split_quarter(0, 3, n + 1, hd)
                        dve.wait_ge(s["pv_done"], hd + 1 + SEED)
                        dve.wait_ge(s["ag_in"], hd * 16 + 16)
                        dve.tensor_tensor(xf[:, bass.ds(g * GROUP + h, 1), :].rearrange("p a b -> p (a b)"),
                                          psO[:, 0:TOK], ag[:], ALU.mult).then_inc(s["gated"], 1)

                fence(dve, FENCES * l + 3)
                dve.memset(aup[:], 0.0).then_inc(s["aup_clear"], 1)
                dve.wait_ge(s["mod_taken"], MOD_CHUNKS // 2 + (l + 1) * RUN_PAIRS + SEED)
                dve.tensor_tensor(mod[:, 2 * KT:], mod_raw[:, l, 2 * KT:], vecs[:, l, R_BMOD + 2 * KT:R_BMOD + MOD_T]
                                  .unsqueeze(2).to_broadcast([P, KT, 2]), ALU.add).then_inc(s["mod_ready"], 1)
                mix_low(l * KT)
                dve.wait_ge(s["mod_ready"], 2 * l + 2)
                with dve.Fori(0, PAIRS) as pr:
                    gp = pr + l * PAIRS

                    def split_fill(*tiles):
                        for f in tiles:
                            i = pr * (FILL // 2) + f // 2
                            split_half(f, i + (occ + FIRST), i + (whole + RUN_PAIRS))

                    def add_fill(f):
                        i = pr * (FILL // 2) + f // 2
                        add_product(lambda part: old[f % 2][:, part], fill_place(f), f, pr * FILL + f, i + (occ + FIRST),
                                    i + l * KT)

                    split_fill(1)
                    add_fill(0)
                    split_fill(2)
                    add_fill(1)
                    dve.wait_ge(s["g_z"], gp * 2 + 2)
                    dve.tensor_scalar(gm[:], gz[:], 0.0, None, ALU.min).then_inc(s["g_min"], 1)
                    dve.wait_ge(s["g_min"], gp + 1)
                    dve.scalar_tensor_tensor(gz[:].rearrange("p a b -> p (a b)"), gm[:].rearrange("p a b -> p (a b)"), 2.0,
                                             gz[:].rearrange("p a b -> p (a b)"), ALU.mult, ALU.subtract)\
                        .then_inc(s["g_neg"], 1)
                    split_fill(3)
                    dve.wait_ge(s["tables_in"], 64 * l + 64)
                    dve.wait_ge(s["g_ln"], gp * 2 + 2)
                    dve.tensor_tensor(gm[:], gm[:], gz[:], ALU.subtract).then_inc(s["g_lf"], 1)
                    dve.wait_ge(s["g_lf"], gp + 1)
                    dve.tensor_tensor_scan(cum[:, 0, :], chunk_keep[:], gm[:, 0, :], 0.0, ALU.mult, ALU.add)\
                        .then_inc(s["g_scan"], 1)
                    dve.tensor_tensor_scan(cum[:, 1, ::-1], chunk_keep[:], gm[:, 1, ::-1], 0.0, ALU.mult, ALU.add)\
                        .then_inc(s["g_scan"], 1)
                    add_fill(2)
                    dve.wait_ge(s["g_scan"], gp * 2 + 2)
                    for z in range(2):
                        mid, last = (CH // 2 - 1, CH - 1) if z == 0 else (CH // 2, 0)
                        c = cum[:, z, :].rearrange("p (c t) -> p c t", t=CH)
                        dve.tensor_tensor(gm[:, z, :].rearrange("p (c t) -> p c t", t=CH), c,
                                          c[:, :, mid:mid + 1].to_broadcast([P, NCH, CH]), ALU.subtract)\
                            .then_inc(s["g_mid"], 1)
                        dve.tensor_copy(small[:, z, 0, :], c[:, :, mid]).then_inc(s["g_mid"], 1)
                        dve.tensor_copy(small[:, z, 1, :], c[:, :, last]).then_inc(s["g_mid"], 1)
                    dve.wait_ge(s["g_mid"], gp * 8 + 6)
                    dve.tensor_scalar(gm[:], gm[:], CLAMP, -CLAMP, ALU.min, ALU.max).then_inc(s["g_clamp"], 1)
                    for z in range(2):
                        dve.tensor_tensor(small[:, z, 2, :], small[:, z, 1, :], small[:, z, 0, :], ALU.subtract)\
                            .then_inc(s["g_mid"], 1)
                    split_fill(4)
                    dve.wait_ge(s["gla_in"], gp * 16 * 6 + 16 * 6)
                    dve.wait_ge(s["g_factors"], gp * 2 + 2)
                    dve.scalar_tensor_tensor(qt[:], gq.unsqueeze(1).to_broadcast([P, 2, TOK]), DK ** -0.5, qt[:],
                                             ALU.mult, ALU.mult).then_inc(s["g_qk"], 1)
                    dve.tensor_tensor(kt_[:], gk.unsqueeze(1).to_broadcast([P, 2, TOK]), kt_[:], ALU.mult)\
                        .then_inc(s["g_qk"], 1)
                    add_fill(3)
                    dve.wait_ge(s["g_smallx"], gp + 1)
                    dve.wait_ge(s["g_qk"], gp * 2 + 2)
                    for z in range(2):
                        dve.tensor_tensor(gm[:, z, :].rearrange("p (c t) -> p c t", t=CH),
                                          kt_[:, z, :].rearrange("p (c t) -> p c t", t=CH),
                                          small[:, z, 2, :].unsqueeze(2).to_broadcast([P, NCH, CH]), ALU.mult)\
                            .then_inc(s["g_hat"], 1)
                        dve.tensor_tensor(gz[:, z, :].rearrange("p (c t) -> p c t", t=CH),
                                          qt[:, z, :].rearrange("p (c t) -> p c t", t=CH),
                                          small[:, z, 0, :].unsqueeze(2).to_broadcast([P, NCH, CH]), ALU.mult)\
                            .then_inc(s["g_hat"], 1)
                    for i in range(TT):
                        dve.wait_ge(s["g_att"], gp * TT + i + 1)
                        dve.tensor_tensor(att_m.rearrange("p h z t -> p h (z t)"),
                                          psP[i % 2][:].rearrange("p (h t) -> p h t", h=2)[:, :, 0:2 * P],
                                          pair_mask[:].unsqueeze(1).to_broadcast([P, 2, 2 * P]), ALU.mult).then_inc(s["g_masked"], 1)
                        dve.wait_ge(s["g_masked"], gp * TT + i + 1)
                        dve.tensor_tensor(att_s[:, i], att_m[:, :, 0], att_m[:, :, 1], ALU.add).then_inc(s["g_summed"], 1)
                        dve.wait_ge(s["g_summed"], gp * TT + i + 1)
                    add_fill(4)
                    split_fill(5, 6)
                    dve.wait_ge(s["g_saved"], gp * 32 + SEED)
                    for n, chunks in enumerate(STEPS):
                        dve.wait_ge(s["g_u"], gp * len(STEPS) + n + 1)
                        dve.wait_ge(s["g_state"], (gp * len(STEPS) + n) * 4 + SEED)
                        for z, ch in enumerate(chunks):
                            at = state_at(z, ch)
                            for hh in range(2):
                                part = slice(hh * DK, (hh + 1) * DK)
                                added = (psT, psP[1])[n % 2][part, ch % 2 * 512 + hh * DV:][:, 0:DV]
                                if at == DEC_CH + 1:
                                    m = dve.tensor_copy(states[part, z, at + 1, :], added)
                                else:
                                    m = dve.scalar_tensor_tensor(states[part, z, at + 1, :], states[part, z, at, :],
                                                                 small[part, z, 1, ch:ch + 1], added, ALU.mult, ALU.add)
                                m.then_inc(s["g_state"], 1)
                    split_fill(7)
                    add_fill(5)
                    def spread_taken(hh):
                        dve.wait_ge(s["g_ostat"], gp * 2 + hh + 1)
                        dve.tensor_scalar(r_a[:], psT[:, 0:TOK], 1.0 / DV, EPS, ALU.mult, ALU.add).then_inc(s["g_ovar"], 1)

                    spread_taken(0)
                    for hh in range(2):
                        n = gp * 2 + hh
                        refine(rstd[:], r_a[:], r_b[:], sq_sum[:], "g_oexp", n + 1, "g_on", n * 3).then_inc(s["g_on"], 1)
                        dve.wait_ge(s["g_on"], n * 3 + 3)
                        dve.scalar_tensor_tensor(stage[hh][:], psP[hh][:, 0:TOK], vecs[:, l, R_GNORM:R_GNORM + 1], rstd[:],
                                                 ALU.mult, ALU.mult).then_inc(s["g_normed"], 1)
                        dve.wait_ge(s["g_normed"], n + 1)
                        if hh == 0:
                            spread_taken(1)
                        dve.tensor_tensor(xf[:, bass.ds(pr * 2 + (KT - GLA_H + hh), 1), :].rearrange("p a b -> p (a b)"),
                                          stage[hh][:], gg[:, hh, :], ALU.mult).then_inc(s["g_out"], 1)
                        add_fill(6 + hh)
                        if hh == 0:
                            split_fill(8)

                fence(dve, FENCES * l + 4)
                mix_low(l * KT + HALF_K)

                def finish(i, last=False):
                    for f in range(4):
                        if not (last and f == 3):
                            after = i * 2 + (f + 1) // 2
                            split_half(f + 1, after + (occ + SECOND), after + (whole + RUN_PAIRS + OUT_PAIRS))
                        add_product(lambda part: xf[:, bass.ds(i * 4 + f, 1), part].rearrange("p a b -> p (a b)"),
                                    psP[f % 2], f, i * 4 + f, i * 2 + (f // 2 + occ + SECOND),
                                    i * 2 + (f // 2 + l * KT + OUT_PAIRS))

                with dve.Fori(0, KT // 4 - 1) as i:
                    finish(i)
                finish(KT // 4 - 1, last=True)

            fence(dve, FENCES * DEPTH + 1)
            norm_factor(psO, DEPTH)
            for k in range(KT):
                dve.scalar_tensor_tensor(xf[:, k, :], xf[:, k, :], head[:, 2 * KT + k:2 * KT + k + 1], rstd[:],
                                         ALU.mult, ALU.mult).then_inc(s["y_scaled"], 1)

        @block.gpsimd
        def _(pool):
            for name in SEEDED:
                pool.sem_inc(s[name], SEED)
            for l in range(DEPTH):
                fence(pool, FENCES * l + 1)
                pool.wait_ge(s["stat_rs"], 3 * l + 3)
                for i in range(KT // 2):
                    pool.wait_ge(s["x_high1"], i + l * KT // 2 + SEED)
                    pool.tensor_tensor(xt[1][:], xf[:, i * 2 + 1, :], rstd[:], ALU.mult).then_inc(s["scaled1"], 1)
                fence(pool, FENCES * l + 2)
                fence(pool, FENCES * l + 3)
                pool.memset(cu[:], 0.0).then_inc(s["conv_clear"], 1)
                pool.wait_ge(s["x_saved"], 16 * (l + 1))
                with pool.Fori(0, CONV_T) as j:
                    n = j + l * CONV_T
                    pool.wait_ge(s["conv_clear"], l + 1)
                    pool.wait_ge(s["conv_in"], n * 48 + 48)
                    for at, part in ((1, slice(0, DEC)), (2 + DEC, slice(DEC, TOK))):
                        pool.tensor_tensor(cu[:, at:at + part.stop - part.start], cin[:, 2, part], cin[:, 0, part], ALU.mult)\
                            .then_inc(s["conv_u"], 1)
                    pool.wait_ge(s["cg_silu"], n + 1)
                    pool.tensor_tensor(cin[:, 1, :], cin[:, 1, :],
                                       cgate[:, bass.ds(j, 1), :].rearrange("p a b -> p (a b)"), ALU.mult).then_inc(s["conv_u"], 1)
                    pool.wait_ge(s["conv_u"], n * 3 + 3)
                    def tap(t, dst):
                        return pool.tensor_tensor(dst, cu[:, t:t + TOK + 1],
                                                  vecs[:, l, bass.ds(j + (R_CONV + t * CONV_T), 1)]
                                                  .to_broadcast([P, TOK + 1]), ALU.mult)

                    tap(0, ct[0][:]).then_inc(s["conv_t"], 1)
                    tap(1, ct[1][:]).then_inc(s["conv_t"], 1)
                    pool.wait_ge(s["conv_t"], n * 2 + 2)
                    pool.tensor_tensor(ct[0][:], ct[0][:], ct[1][:], ALU.add).then_inc(s["conv_sum"], 1)
                    pool.wait_ge(s["conv_sum"], n * 3 + 1)
                    tap(2, ct[1][:]).then_inc(s["conv_sum"], 1)
                    pool.wait_ge(s["conv_sum"], n * 3 + 2)
                    pool.tensor_tensor(ct[0][:], ct[0][:], ct[1][:], ALU.add).then_inc(s["conv_sum"], 1)
                    pool.wait_ge(s["conv_sum"], n * 3 + 3)
                    for at, part in ((0, slice(0, DEC)), (1 + DEC, slice(DEC, TOK))):
                        pool.tensor_tensor(xf[:, bass.ds(j + HEADS, 1), part].rearrange("p a b -> p (a b)"),
                                           ct[0][:, at:at + part.stop - part.start], cin[:, 1, part], ALU.mult)\
                            .then_inc(s["conv_out"], 1)
                    pool.wait_ge(s["conv_out"], n * 2 + 2 + SEED)

                fence(pool, FENCES * l + 4)
                pool.memset(sq_sum[:], 0.0).then_inc(s["x_acc"], 1)
                with pool.Fori(0, OUT_PAIRS) as i:
                    for slot in range(2):
                        n = i * 2 + (l * KT + slot)
                        pool.wait_ge(s["x_sq"], n + 1)
                        pool.wait_ge(s["x_acc"], n + l + 1 + SEED)
                        pool.tensor_tensor(sq_sum[:], sq_sum[:], xt[slot][:], ALU.add).then_inc(s["x_acc"], 1)
            fence(pool, FENCES * DEPTH + 1)


_INS = ["x_prompt", "x_sample", "cache_k", "cache_v", "state_gla", "c", "c_ctx", "w_mod", "b_mod", "norm_w", "w_in",
        "q_norm_w", "k_norm_w", "conv_w", "gla_a_up", "gla_a_bias", "gla_norm_w", "w_out", "final_norm_w"]
_OUTS = {"y_prompt": (1, SEQ, D), "y_sample": (1, DEC, D), "new_k": (1, DEPTH, SEQ, KVH, HD),
         "new_v": (1, DEPTH, SEQ, KVH, HD), "new_state": (1, DEPTH, 2, GLA_H, DK, DV)}


def tables():
    f = np.float32
    d = np.arange(HD)
    half = HD // 2
    n_freq = HD // 4
    inv = (f(10000.0) ** (-np.arange(n_freq, dtype=f) / f(n_freq))).astype(f)
    pos = np.arange(DEC)
    where = np.where((d < half)[:, None], (pos // GRID_W)[None, :], (pos % GRID_W)[None, :]).astype(f)
    angle = (where * inv[d % n_freq][:, None]).astype(f)
    rotate = np.zeros((P, P), f)
    for m in range(HD):
        if m % half < n_freq:
            rotate[m + n_freq, m] = -1.0
        else:
            rotate[m - n_freq, m] = 1.0
    a = np.arange(P)
    same = (a[:, None] // CH) == (a[None, :] // CH)
    fwd = same & (a[:, None] <= a[None, :])
    bwd = same & (a[:, None] >= a[None, :])
    mask = np.concatenate([fwd, bwd], 1).astype(f)
    keep = np.broadcast_to((np.arange(TOK) % CH != 0).astype(f), (P, TOK))
    return {"ident": np.eye(P, dtype=f), "rotate": rotate, "cos": np.cos(angle).astype(f), "sin": np.sin(angle).astype(f),
            "pair_mask": np.ascontiguousarray(mask), "chunk_keep": np.ascontiguousarray(keep)}


def kernel(**inputs):
    import concourse.bacc as _bacc
    from concourse.bass_utils import run_bass_kernel_spmd as _run

    nc = _bacc.Bacc("TRN2", target_bir_lowering=False, num_devices=1, dynamic_dma_scratch_size=1024)
    arrays, io = {}, {}
    given = {name: np.ascontiguousarray(inputs[name]) for name in _INS}
    given.update(tables())
    for name, a in given.items():
        arrays[f"in_{name}_dram"] = a
        io[name] = nc.dram_tensor(f"in_{name}_dram", a.shape, mybir.dt.from_np(a.dtype), kind="ExternalInput").ap()
    for name, shape in _OUTS.items():
        io[name] = nc.dram_tensor(f"out_{name}_dram", shape, F32, kind="ExternalOutput").ap()
    backbone(nc, io)
    r = _run(nc, [arrays], core_ids=[0])
    return tuple(r.results[0][f"out_{name}_dram"] for name in _OUTS)
```
